# Optimizing a Trainium2 kernel written in Bass

```python
import jax, jax.numpy as jnp
from jax import lax
import numpy as np

D_MODEL = 2048
BATCH = 1
SEQ = 256
DEPTH = 1
DEC_BATCH = 8
DEC_SEQ = 4
PAST_LEN = 256
PAGE_SIZE = 128

A_WIDTH = D_MODEL
A_GROUPS = 8
A_GROUP_DIM = A_WIDTH // A_GROUPS
CHUNK = 128
N_HEADS = 16
KV_HEADS = 4
HEAD_DIM = 128
Q_PER_KV = N_HEADS // KV_HEADS
ROPE_DIM = HEAD_DIM // 4
ROPE_THETA = 500000.0
CMP_BLOCK = 32
SLC_BLOCK = 64
CMP_PER_SLC = SLC_BLOCK // CMP_BLOCK
N_SELECT = 8
WINDOW = 512
Q_BLOCK = 128
SCALE = HEAD_DIM ** -0.5
N_GROUPS = 4
EXPERTS_PER_GROUP = 8
N_EXPERTS = N_GROUPS * EXPERTS_PER_GROUP
TOP_K_IN_GROUP = 2
EXPERT_DIM = 256
EPS = 1e-6
NEG = -1e30
FORCE_BONUS = 1e4
Q_COLS = N_HEADS * HEAD_DIM
KV_COLS = KV_HEADS * HEAD_DIM
IN_COLS = 2 * A_WIDTH + Q_COLS + 6 * KV_COLS + 3 * N_HEADS + 2 * D_MODEL

kernel_name = 'hybrid_gmlp_nsa_hmoe_step'

def rmsnorm(x, g):
    x32 = x.astype(jnp.float32)
    y = x32 * lax.rsqrt(jnp.mean(x32 * x32, axis=-1, keepdims=True) + EPS)
    return (y * g.astype(jnp.float32)).astype(x.dtype)

def layernorm(x, g, b):
    x32 = x.astype(jnp.float32)
    xc = x32 - jnp.mean(x32, axis=-1, keepdims=True)
    var = jnp.mean(xc * xc, axis=-1, keepdims=True)
    return (xc * lax.rsqrt(var + EPS) * g.astype(jnp.float32) + b.astype(jnp.float32)).astype(x.dtype)

def rope(x, pos):
    half = ROPE_DIM // 2
    inv = jnp.power(jnp.float32(ROPE_THETA), -jnp.arange(0, ROPE_DIM, 2, dtype=jnp.float32) / ROPE_DIM)
    ang = pos.astype(jnp.float32)[:, None] * inv[None, :]
    cos = jnp.cos(ang)[:, None, :]
    sin = jnp.sin(ang)[:, None, :]
    xr = x[..., :ROPE_DIM].astype(jnp.float32)
    x1, x2 = xr[..., :half], xr[..., half:]
    rot = jnp.concatenate([x1 * cos - x2 * sin, x2 * cos + x1 * sin], axis=-1).astype(x.dtype)
    return jnp.concatenate([rot, x[..., ROPE_DIM:]], axis=-1)

def split_cols(z):
    sizes = (A_WIDTH, A_WIDTH, Q_COLS) + (KV_COLS,) * 6 + (3 * N_HEADS, D_MODEL, D_MODEL)
    cuts = [int(c) for c in np.cumsum(sizes)[:-1]]
    return jnp.split(z, cuts, axis=-1)

def project(h, w_in, pos):
    bt, t, _ = h.shape
    z = jnp.einsum('btd,dc->btc', h, w_in)
    a_u, a_v, q, k_c, v_c, k_s, v_s, k_w, v_w, g_br, g_a, g_b = split_cols(z)
    def heads(a, n):
        return a.reshape(bt, t, n, HEAD_DIM)
    q = rope(heads(q, N_HEADS), pos).reshape(bt, t, KV_HEADS, Q_PER_KV, HEAD_DIM)
    kv = (rope(heads(k_c, KV_HEADS), pos), heads(v_c, KV_HEADS),
          rope(heads(k_s, KV_HEADS), pos), heads(v_s, KV_HEADS),
          rope(heads(k_w, KV_HEADS), pos), heads(v_w, KV_HEADS))
    return a_u, a_v, q, kv, g_br, g_a, g_b

def chunk_gmlp(a_u, a_v, ln_g, ln_b, w_s, b_s):
    bt, t, _ = a_u.shape
    ln = min(t, CHUNK)
    u = jax.nn.gelu(a_u)
    v = layernorm(jax.nn.gelu(a_v), ln_g, ln_b)
    vc = v.reshape(bt, t // ln, ln, A_GROUPS, A_GROUP_DIM)
    causal = jnp.tril(jnp.ones((ln, ln), dtype=bool))
    w = jnp.where(causal, w_s[:, :ln, :ln], 0.0).astype(v.dtype)
    bias = b_s[:, :ln].T[None, None, :, :, None].astype(v.dtype)
    s = jnp.einsum('gij,bcjgd->bcigd', w, vc) + bias
    return u * s.reshape(bt, t, A_WIDTH), v

def compress(rows, pe, w1, w2):
    bt, tc = rows.shape[:2]
    r = rows.reshape(bt, tc // CMP_BLOCK, CMP_BLOCK, KV_HEADS, HEAD_DIM) + pe[None, None, :, None, :]
    hid = jax.nn.gelu(jnp.einsum('bnjhd,jde->bnhe', r, w1))
    return jnp.einsum('bnhe,ef->bnhf', hid, w2)

def cmp_attend(q, q_pos, kc, vc):
    nc = kc.shape[1]
    s = jnp.einsum('bqhgd,bnhd->bhgqn', q, kc).astype(jnp.float32) * SCALE
    valid = ((jnp.arange(nc) + 1) * CMP_BLOCK - 1)[None, :] <= q_pos[:, None]
    p = jax.nn.softmax(jnp.where(valid, s, NEG), axis=-1) * valid
    o = jnp.einsum('bhgqn,bnhd->bqhgd', p.astype(vc.dtype), vc)
    return o, p.sum(axis=2)

def select_blocks(imp, q_pos, n_blocks):
    bt, kv, tq, nc = imp.shape
    imp = jnp.pad(imp, ((0, 0), (0, 0), (0, 0), (0, n_blocks * CMP_PER_SLC - nc)))
    imp = imp.reshape(bt, kv, tq, n_blocks, CMP_PER_SLC).sum(-1)
    j = jnp.arange(n_blocks)[None, :]
    forced = (j == 0) | (j == (q_pos // SLC_BLOCK)[:, None])
    future = j * SLC_BLOCK > q_pos[:, None]
    score = jnp.where(future, -1.0, imp + FORCE_BONUS * forced)
    _, idx = lax.top_k(score, min(N_SELECT, n_blocks))
    return idx

def gathered_attend(q, q_pos, kg, vg, kpos):
    s = jnp.einsum('bqhgd,bhqld->bhgql', q, kg).astype(jnp.float32) * SCALE
    valid = (kpos <= q_pos[None, None, :, None])[:, :, None]
    p = jax.nn.softmax(jnp.where(valid, s, NEG), axis=-1)
    return jnp.einsum('bhgql,bhqld->bqhgd', p.astype(vg.dtype), vg)

def window_attend(q, q_pos, k, v, k_pos):
    s = jnp.einsum('bqhgd,blhd->bhgql', q, k).astype(jnp.float32) * SCALE
    d = q_pos[:, None] - k_pos[None, :]
    valid = (d >= 0) & (d < WINDOW) & (k_pos[None, :] >= 0)
    p = jax.nn.softmax(jnp.where(valid, s, NEG), axis=-1)
    return jnp.einsum('bhgql,blhd->bqhgd', p.astype(v.dtype), v)

def nsa_prompt(q, kv, cmp_k, cmp_v):
    k_c, v_c, k_s, v_s, k_w, v_w = kv
    b, s = q.shape[:2]
    kc = compress(k_c, *cmp_k)
    vc = compress(v_c, *cmp_v)
    nsb = s // SLC_BLOCK
    kr = k_s.reshape(b, nsb, SLC_BLOCK, KV_HEADS, HEAD_DIM)
    vr = v_s.reshape(b, nsb, SLC_BLOCK, KV_HEADS, HEAD_DIM)
    zpad = jnp.zeros((b, WINDOW, KV_HEADS, HEAD_DIM), k_w.dtype)
    kwp = jnp.concatenate([zpad, k_w], axis=1)
    vwp = jnp.concatenate([zpad, v_w], axis=1)
    bi = jnp.arange(b)[:, None, None, None]
    hi = jnp.arange(KV_HEADS)[None, :, None, None]
    offs = jnp.arange(SLC_BLOCK)
    nqb = s // Q_BLOCK
    qb = jnp.moveaxis(q.reshape(b, nqb, Q_BLOCK, KV_HEADS, Q_PER_KV, HEAD_DIM), 1, 0)

    def block(args):
        q_blk, n = args
        start = n * Q_BLOCK
        q_pos = start + jnp.arange(Q_BLOCK)
        o_c, imp = cmp_attend(q_blk, q_pos, kc, vc)
        idx = select_blocks(imp, q_pos, nsb)
        kg = kr[bi, idx, :, hi, :].reshape(b, KV_HEADS, Q_BLOCK, -1, HEAD_DIM)
        vg = vr[bi, idx, :, hi, :].reshape(b, KV_HEADS, Q_BLOCK, -1, HEAD_DIM)
        kpos = (idx[..., None] * SLC_BLOCK + offs).reshape(b, KV_HEADS, Q_BLOCK, -1)
        o_s = gathered_attend(q_blk, q_pos, kg, vg, kpos)
        kwin = lax.dynamic_slice_in_dim(kwp, start, WINDOW + Q_BLOCK, axis=1)
        vwin = lax.dynamic_slice_in_dim(vwp, start, WINDOW + Q_BLOCK, axis=1)
        k_pos = start - WINDOW + jnp.arange(WINDOW + Q_BLOCK)
        o_w = window_attend(q_blk, q_pos, kwin, vwin, k_pos)
        return o_c, o_s, o_w

    oc, osl, ow = lax.map(block, (qb, jnp.arange(nqb)))
    def unblock(o):
        return jnp.moveaxis(o, 0, 1).reshape(b, s, KV_HEADS, Q_PER_KV, HEAD_DIM)
    return unblock(oc), unblock(osl), unblock(ow)

def nsa_sample(q, q_pos, kv, pool_k_cmp, pool_v_cmp, pool_k_slc, pool_v_slc, layer, page_table,
               kbuf, vbuf, cmp_k, cmp_v):
    k_c, v_c, k_s, v_s, k_w, v_w = kv
    db, t = q.shape[:2]
    past = page_table.shape[1] * PAGE_SIZE
    kp_rows = pool_k_cmp[layer, page_table].reshape(db, past, KV_HEADS, HEAD_DIM)
    vp_rows = pool_v_cmp[layer, page_table].reshape(db, past, KV_HEADS, HEAD_DIM)
    n_new_c = (t // CMP_BLOCK) * CMP_BLOCK
    kc = jnp.concatenate([compress(kp_rows, *cmp_k), compress(k_c[:, :n_new_c], *cmp_k)], axis=1)
    vc = jnp.concatenate([compress(vp_rows, *cmp_v), compress(v_c[:, :n_new_c], *cmp_v)], axis=1)
    o_c, imp = cmp_attend(q, q_pos, kc, vc)
    nb_past = past // SLC_BLOCK
    nb_new = -(-t // SLC_BLOCK)
    idx = select_blocks(imp, q_pos, nb_past + nb_new)
    sub = PAGE_SIZE // SLC_BLOCK
    bi = jnp.arange(db)[:, None, None, None]
    hi = jnp.arange(KV_HEADS)[None, :, None, None]
    offs = jnp.arange(SLC_BLOCK)
    is_past = (idx < nb_past)[..., None, None]
    pi = jnp.minimum(idx, nb_past - 1)
    phys = page_table[bi, pi // sub][..., None]
    rows = ((pi % sub) * SLC_BLOCK)[..., None] + offs
    ni = jnp.clip(idx - nb_past, 0, nb_new - 1)
    pad = ((0, 0), (0, nb_new * SLC_BLOCK - t), (0, 0), (0, 0))
    knb = jnp.pad(k_s, pad).reshape(db, nb_new, SLC_BLOCK, KV_HEADS, HEAD_DIM)
    vnb = jnp.pad(v_s, pad).reshape(db, nb_new, SLC_BLOCK, KV_HEADS, HEAD_DIM)

    def gather(pool, newb):
        from_pool = pool[layer, phys, rows, hi[..., None], :]
        from_new = newb[bi, ni, :, hi, :]
        return jnp.where(is_past, from_pool, from_new).reshape(db, KV_HEADS, t, -1, HEAD_DIM)

    kg = gather(pool_k_slc, knb)
    vg = gather(pool_v_slc, vnb)
    kpos = (idx[..., None] * SLC_BLOCK + offs).reshape(db, KV_HEADS, t, -1)
    o_s = gathered_attend(q, q_pos, kg, vg, kpos)
    wb = kbuf.shape[1]
    kwin = jnp.concatenate([kbuf, k_w], axis=1)
    vwin = jnp.concatenate([vbuf, v_w], axis=1)
    k_pos = past - wb + jnp.arange(wb + t)
    o_w = window_attend(q, q_pos, kwin, vwin, k_pos)
    return o_c, o_s, o_w, kwin[:, -wb:], vwin[:, -wb:]

def merge(a_out, o_c, o_s, o_w, g_br, g_a, g_b, w_pa, w_pb, w_o):
    bt, t = a_out.shape[:2]
    gb = jax.nn.sigmoid(g_br.astype(jnp.float32)).reshape(bt, t, KV_HEADS, Q_PER_KV, 3).astype(o_c.dtype)
    o = o_c * gb[..., 0:1] + o_s * gb[..., 1:2] + o_w * gb[..., 2:3]
    y_b = jnp.einsum('btc,cd->btd', o.reshape(bt, t, Q_COLS), w_pb)
    y_a = jnp.einsum('btc,cd->btd', a_out, w_pa)
    m = jax.nn.sigmoid(g_a) * y_a + jax.nn.sigmoid(g_b) * y_b
    return jnp.einsum('btd,de->bte', m, w_o)

def hier_moe(h, w_rg, b_rg, w_re, b_re, w_gate, w_up, w_down):
    x = h.reshape(-1, D_MODEL)
    n = x.shape[0]
    pg = jax.nn.softmax(jnp.einsum('nd,dg->ng', x, w_rg).astype(jnp.float32) + b_rg.astype(jnp.float32), axis=-1)
    pg_top, g_idx = lax.top_k(pg, 1)
    le = (jnp.einsum('nd,de->ne', x, w_re).astype(jnp.float32) + b_re.astype(jnp.float32))
    le = le.reshape(n, N_GROUPS, EXPERTS_PER_GROUP)[jnp.arange(n), g_idx[:, 0]]
    pe = jax.nn.softmax(le, axis=-1)
    pe_top, e_idx = lax.top_k(pe, TOP_K_IN_GROUP)
    w = pg_top * pe_top / jnp.sum(pe_top, axis=-1, keepdims=True)
    expert = g_idx * EXPERTS_PER_GROUP + e_idx
    gate = jnp.sum(jax.nn.one_hot(expert, N_EXPERTS, dtype=jnp.float32) * w[..., None], axis=1)
    hid = jax.nn.silu(jnp.einsum('nd,edf->nef', x, w_gate)) * jnp.einsum('nd,edf->nef', x, w_up)
    y = jnp.einsum('nef,efd->nd', hid * gate[..., None].astype(hid.dtype), w_down)
    return y.reshape(h.shape)

def setup_inputs(seed: int = 0) -> dict:
    key = jax.random.key(seed)
    ks = jax.random.split(key, 40)
    f32 = jnp.float32
    n_pages = PAST_LEN // PAGE_SIZE
    n_used = DEC_BATCH * n_pages
    n_phys = n_used + n_used // 4
    win_buf = min(WINDOW, PAST_LEN)
    def nrm(k, shape, scale):
        return jax.random.normal(k, shape, f32) * scale
    pool = (DEPTH, n_phys, PAGE_SIZE, KV_HEADS, HEAD_DIM)
    wbuf = (DEPTH, DEC_BATCH, win_buf, KV_HEADS, HEAD_DIM)
    page_table = jax.random.permutation(ks[8], n_phys)[:n_used].reshape(DEC_BATCH, n_pages).astype(jnp.int32)
    return {
        'x_prompt': nrm(ks[0], (BATCH, SEQ, D_MODEL), 1.0),
        'x_sample': nrm(ks[1], (DEC_BATCH, DEC_SEQ, D_MODEL), 1.0),
        'cache_k_cmp': nrm(ks[2], pool, 1.0),
        'cache_v_cmp': nrm(ks[3], pool, 1.0),
        'cache_k_slc': nrm(ks[4], pool, 1.0),
        'cache_v_slc': nrm(ks[5], pool, 1.0),
        'state_k_win': nrm(ks[6], wbuf, 1.0),
        'state_v_win': nrm(ks[7], wbuf, 1.0),
        'page_table': page_table,
        'g_mix': 1.0 + nrm(ks[9], (DEPTH, D_MODEL), 0.1),
        'w_in': nrm(ks[10], (DEPTH, D_MODEL, IN_COLS), D_MODEL ** -0.5),
        'a_ln_g': 1.0 + nrm(ks[11], (DEPTH, A_WIDTH), 0.1),
        'a_ln_b': nrm(ks[12], (DEPTH, A_WIDTH), 0.1),
        'a_w_s': nrm(ks[13], (DEPTH, A_GROUPS, CHUNK, CHUNK), CHUNK ** -0.5),
        'a_b_s': 1.0 + nrm(ks[14], (DEPTH, A_GROUPS, CHUNK), 0.1),
        'cmp_pe_k': nrm(ks[15], (DEPTH, CMP_BLOCK, HEAD_DIM), 0.1),
        'cmp_w1_k': nrm(ks[16], (DEPTH, CMP_BLOCK, HEAD_DIM, HEAD_DIM), (CMP_BLOCK * HEAD_DIM) ** -0.5),
        'cmp_w2_k': nrm(ks[17], (DEPTH, HEAD_DIM, HEAD_DIM), HEAD_DIM ** -0.5),
        'cmp_pe_v': nrm(ks[18], (DEPTH, CMP_BLOCK, HEAD_DIM), 0.1),
        'cmp_w1_v': nrm(ks[19], (DEPTH, CMP_BLOCK, HEAD_DIM, HEAD_DIM), (CMP_BLOCK * HEAD_DIM) ** -0.5),
        'cmp_w2_v': nrm(ks[20], (DEPTH, HEAD_DIM, HEAD_DIM), HEAD_DIM ** -0.5),
        'w_pa': nrm(ks[21], (DEPTH, A_WIDTH, D_MODEL), A_WIDTH ** -0.5),
        'w_pb': nrm(ks[22], (DEPTH, Q_COLS, D_MODEL), Q_COLS ** -0.5),
        'w_o': nrm(ks[23], (DEPTH, D_MODEL, D_MODEL), D_MODEL ** -0.5),
        'g_ffn': 1.0 + nrm(ks[24], (DEPTH, D_MODEL), 0.1),
        'w_rg': nrm(ks[25], (DEPTH, D_MODEL, N_GROUPS), D_MODEL ** -0.5),
        'b_rg': nrm(ks[26], (DEPTH, N_GROUPS), 0.01),
        'w_re': nrm(ks[27], (DEPTH, D_MODEL, N_EXPERTS), D_MODEL ** -0.5),
        'b_re': nrm(ks[28], (DEPTH, N_EXPERTS), 0.01),
        'w_gate': nrm(ks[29], (DEPTH, N_EXPERTS, D_MODEL, EXPERT_DIM), D_MODEL ** -0.5),
        'w_up': nrm(ks[30], (DEPTH, N_EXPERTS, D_MODEL, EXPERT_DIM), D_MODEL ** -0.5),
        'w_down': nrm(ks[31], (DEPTH, N_EXPERTS, EXPERT_DIM, D_MODEL), EXPERT_DIM ** -0.5),
        'g_final': 1.0 + nrm(ks[32], (D_MODEL,), 0.1),
    }

def reference(x_prompt, x_sample, cache_k_cmp, cache_v_cmp, cache_k_slc, cache_v_slc,
              state_k_win, state_v_win, page_table, g_mix, w_in, a_ln_g, a_ln_b, a_w_s, a_b_s,
              cmp_pe_k, cmp_w1_k, cmp_w2_k, cmp_pe_v, cmp_w1_v, cmp_w2_v,
              w_pa, w_pb, w_o, g_ffn, w_rg, b_rg, w_re, b_re, w_gate, w_up, w_down, g_final):
    s = x_prompt.shape[1]
    t = x_sample.shape[1]
    past = page_table.shape[1] * PAGE_SIZE
    pos_p = jnp.arange(s)
    pos_s = past + jnp.arange(t)
    wl = min(WINDOW, s)
    xp, xs = x_prompt, x_sample
    kcp, vcp, ksp, vsp, kwp, vwp = [], [], [], [], [], []
    kcs, vcs, kss, vss, kws, vws, ach = [], [], [], [], [], [], []
    for l in range(DEPTH):
        cmp_k = (cmp_pe_k[l], cmp_w1_k[l], cmp_w2_k[l])
        cmp_v = (cmp_pe_v[l], cmp_w1_v[l], cmp_w2_v[l])
        moe_w = (w_rg[l], b_rg[l], w_re[l], b_re[l], w_gate[l], w_up[l], w_down[l])
        out_w = (w_pa[l], w_pb[l], w_o[l])
        gm_w = (a_ln_g[l], a_ln_b[l], a_w_s[l], a_b_s[l])
        h = rmsnorm(xp, g_mix[l])
        a_u, a_v, q, kv, g_br, g_a, g_b = project(h, w_in[l], pos_p)
        a_out, _ = chunk_gmlp(a_u, a_v, *gm_w)
        o_c, o_s, o_w = nsa_prompt(q, kv, cmp_k, cmp_v)
        xp = xp + merge(a_out, o_c, o_s, o_w, g_br, g_a, g_b, *out_w)
        xp = xp + hier_moe(rmsnorm(xp, g_ffn[l]), *moe_w)
        kcp.append(kv[0]); vcp.append(kv[1]); ksp.append(kv[2]); vsp.append(kv[3])
        kwp.append(kv[4][:, -wl:]); vwp.append(kv[5][:, -wl:])
        h = rmsnorm(xs, g_mix[l])
        a_u, a_v, q, kv, g_br, g_a, g_b = project(h, w_in[l], pos_s)
        a_out, v_new = chunk_gmlp(a_u, a_v, *gm_w)
        o_c, o_s, o_w, kbuf, vbuf = nsa_sample(q, pos_s, kv, cache_k_cmp, cache_v_cmp, cache_k_slc,
                                               cache_v_slc, l, page_table, state_k_win[l],
                                               state_v_win[l], cmp_k, cmp_v)
        xs = xs + merge(a_out, o_c, o_s, o_w, g_br, g_a, g_b, *out_w)
        xs = xs + hier_moe(rmsnorm(xs, g_ffn[l]), *moe_w)
        kcs.append(kv[0]); vcs.append(kv[1]); kss.append(kv[2]); vss.append(kv[3])
        kws.append(kbuf); vws.append(vbuf); ach.append(v_new)
    y_prompt = rmsnorm(xp, g_final)
    y_sample = rmsnorm(xs, g_final)
    return (y_prompt, y_sample,
            jnp.stack(kcp), jnp.stack(vcp), jnp.stack(ksp), jnp.stack(vsp), jnp.stack(kwp), jnp.stack(vwp),
            jnp.stack(kcs), jnp.stack(vcs), jnp.stack(kss), jnp.stack(vss), jnp.stack(kws), jnp.stack(vws),
            jnp.stack(ach))


_drawn_inputs = setup_inputs


def setup_inputs(seed=0):
    import zlib

    import numpy as np

    out = dict(_drawn_inputs(seed))
    spreads = {}
    factors = {'cmp_pe_k': 6.17, 'b_re': 3.033, 'b_rg': 6.492}
    for name, (base, spread) in spreads.items():
        noise = np.random.default_rng([zlib.crc32(name.encode()), seed]).standard_normal(out[name].shape)
        drawn = base * np.exp(spread * noise) if base else spread * noise
        out[name] = __import__('jax').numpy.asarray(drawn.astype(out[name].dtype))
    for name, factor in factors.items():
        out[name] = (out[name] * factor).astype(out[name].dtype)
    return out
```

```python
from contextlib import ExitStack

import numpy as np

import concourse.bass as bass
from concourse import mybir

F32 = mybir.dt.float32
I32 = mybir.dt.int32
U32 = mybir.dt.uint32
ALU = mybir.AluOpType
ACT = mybir.ActivationFunctionType
AX_X = mybir.AxisListType.X
ds = bass.ds

P = 128
D = 2048
KT = D // P
SEQ, DB, DT = 256, 8, 4
NS = DB * DT
TOK = SEQ + NS
ROWS = (P, P, NS)
NH, KVH, GQ, HD = 16, 4, 4, 128
RD, HALF = 32, 16
PAST = 256
PAGES = DB * PAST // P
CB = 32
NSEQ = DB + 1
NCB = PAST // CB
SCALE = float(HD) ** -0.5
EPS = 1e-6
NEG = -1e30
AG = 8
NG, EPG = 4, 8
NE = NG * EPG
ED = 256
CAP = 64
MAXCH = -(-TOK // CAP)
NOVF = 2 * TOK // CAP
NITEM = NE + NOVF
NOWHERE = 1 << 20
C_U, C_V, C_Q, C_KV = 0, D, 2 * D, 3 * D
C_BR = C_KV + 6 * KVH * HD
C_GA = C_BR + 3 * NH
C_GB = C_GA + D
KVC = KVH * HD

CONSTS = {}
CW = 0
for _n, _w in (("ident", P), ("before", P), ("ones", P), ("pmask", 2 * P), ("cmask", 2 * NCB), ("anyvalid", 3),
               ("smask", DB * NS), ("cosT", TOK), ("sinT", TOK), ("swap", RD), ("cos", 3 * HALF), ("sin", 3 * HALF),
               ("iota32", NE), ("base32", NE), ("iota8", 8), ("ovf_no", NOVF * NE), ("token", 3), ("pair", 6)):
    CONSTS[_n] = (CW, _w)
    CW += _w


def constants():
    f = np.float32
    c = np.zeros((P, CW), f)

    def put(name, a):
        o, w = CONSTS[name]
        a = np.asarray(a, f).reshape(a.shape[0], -1)
        c[:a.shape[0], o:o + w] = a

    r = np.arange(P)
    put("ident", np.eye(P))
    put("before", (r[:, None] < r[None, :]))
    put("ones", np.ones((P, P)))
    put("pmask", np.concatenate([np.zeros((P, P)), np.where(r[None, :] <= r[:, None], 0, NEG)], 1))
    ends = (np.arange(NCB) + 1) * CB - 1
    put("cmask", np.stack([np.where(ends[None] <= (r + q * P)[:, None], 0, NEG) for q in range(2)], 1))
    av = np.ones((P, 3))
    av[:CB - 1, 0] = 0
    put("anyvalid", av)
    row_t = np.arange(NH * DT) % DT
    k = np.arange(NS)
    put("smask", np.where((k // DT)[None, None] == np.arange(DB)[None, :, None],
                          np.where((k % DT)[None, None] <= row_t[:, None, None], 0, NEG), NEG))
    inv = np.power(f(500000.0), -np.arange(0, RD, 2, dtype=f) / f(RD))
    pos = np.concatenate([np.arange(SEQ), PAST + np.arange(NS) % DT]).astype(f)
    ang = (pos[:, None] * inv[None]).astype(f)
    cos, sin = np.cos(ang), np.sin(ang)
    put("cosT", np.concatenate([cos, cos], 1).T)
    put("sinT", np.concatenate([-sin, sin], 1).T)
    put("swap", np.roll(np.eye(RD), HALF, 1))
    tiles = np.zeros((2, P, 3, HALF))
    for t in range(3):
        tiles[0, :ROWS[t], t] = cos[t * P:t * P + ROWS[t]]
        tiles[1, :ROWS[t], t] = sin[t * P:t * P + ROWS[t]]
    put("cos", tiles[0])
    put("sin", tiles[1])
    put("iota32", np.tile(np.arange(NE), (P, 1)))
    put("base32", np.tile(np.arange(NE) * CAP, (P, 1)))
    put("iota8", np.tile(np.arange(8), (P, 1)))
    put("ovf_no", np.tile(np.repeat(np.arange(NOVF), NE), (P, 1)))
    tok = r[:, None] + P * np.arange(3)[None]
    put("token", tok)
    put("pair", tok[:, :, None] + TOK * np.arange(2)[None, None])
    return c


def bcast(ap, shape):
    return ap.broadcast_to(shape)


class Chain:

    def __init__(self, eng, sem):
        self.eng, self.sem, self.n, self.lead = eng, sem, 0, None

    def value(self):
        return self.n if self.lead is None else self.lead + self.n

    def link(self, ins):
        ins.then_inc(self.sem, 1)
        self.n += 1
        self.eng.wait_ge(self.sem, self.value())


def apart(eng, sem, value, passed):
    if not (isinstance(value, int) and value <= 0):
        eng.wait_ge(sem, value)
        eng.sem_inc(passed, 1)


def loop(eng, chain, count, body):
    start = chain.n if chain else 0
    body(0)
    if chain:
        per = chain.n - start
        chain.n = start
    with eng.Fori(1, count) as i:
        if chain and per:
            chain.lead = i * per
        body(i)
    if chain:
        assert chain.n == start + per
        chain.lead = None
        chain.n = start + per * count


def after(eng, sem, value):
    if not (isinstance(value, int) and value <= 0):
        eng.wait_ge(sem, value)


def build(nc, a, outs, cap_debug=None):
    (y_prompt, y_sample, o_kcp, o_vcp, o_ksp, o_vsp, o_kwp, o_vwp,
     o_kcs, o_vcs, o_kss, o_vss, o_kws, o_vws, o_vchunk) = outs
    with ExitStack() as ctx:
        def sb(name, shape, dt=F32):
            return ctx.enter_context(nc.sbuf_tensor(name, shape, dt))

        def sem(name):
            return ctx.enter_context(nc.semaphore(name))

        gate_d = nc.dram_tensor("gate_d", (NS, 3 * NH), F32, kind="Internal").ap()
        h2_d = nc.dram_tensor("h2_d", (TOK, D), F32, kind="Internal").ap()
        slot_d = nc.dram_tensor("slot_d", (NITEM * CAP, 2), I32, kind="Internal").ap()
        ypair_d = nc.dram_tensor("ypair_d", (2 * TOK, D), F32, kind="Internal").ap()

        h_mem = sb("h_mem", [P, KT * TOK])
        hT = h_mem[:].rearrange("p (k t) -> p k t", k=KT)
        Q0, U0 = 0, KT * TOK
        K0 = U0 + 3 * D + KT * TOK
        W0 = K0 + 3 * 6 * KVC
        END = W0 + 4 * 8 * 256
        mem = sb("mem", [P, END])
        qT = mem[:, Q0:Q0 + KT * TOK].rearrange("p (k t) -> p k t", k=KT)
        v_tok = mem[:, U0:U0 + 3 * D].rearrange("p (t c) -> p t c", t=3)
        uT = mem[:, U0 + 3 * D:K0].rearrange("p (k t) -> p k t", k=KT)
        kv = mem[:, K0:W0].rearrange("p (t c) -> p t c", t=3)
        ring = mem[:, W0:END].rearrange("p (s k c) -> p s k c", s=4, k=8)
        rowsT = mem[:, U0:U0 + 18 * 512]
        w1 = mem[:, Q0:Q0 + CB * P].rearrange("p (j e) -> p j e", j=CB)
        kx = mem[:, U0:U0 + 2 * 2048].rearrange("p (b t c) -> p b t c", b=2, t=4)
        vx = mem[:, U0 + 4096:U0 + 8192].rearrange("p (b t c) -> p b t c", b=2, t=4)
        kxT = mem[:, U0 + 8192:U0 + 8192 + 2048].rearrange("p (h c) -> p h c", h=KVH)
        mT = mem[:, K0:K0 + KT * TOK].rearrange("p (k t) -> p k t", k=KT)
        ln_g = mem[:, K0:K0 + D]
        ln_b = mem[:, K0 + D:K0 + 2 * D]
        ws_raw = mem[:, K0 + 4096:K0 + 5120].rearrange("p (g j) -> p g j", g=AG)
        wsT = mem[:, K0 + 5120:K0 + 6144].rearrange("p (g j) -> p g j", g=AG)
        sbias = mem[:, K0 + 6144:K0 + 6144 + AG * TOK].rearrange("p (g t) -> p g t", g=AG)
        wss_raw = mem[0:NS, K0 + 8448:K0 + 8704].rearrange("p (g j) -> p g j", g=AG)
        wssT = mem[0:NS, K0 + 8704:K0 + 8960].rearrange("p (g j) -> p g j", g=AG)
        wgu = [mem[:, 12288 * b:12288 * b + 8192].rearrange("p (k c) -> p k c", k=KT) for b in range(2)]
        wdn = [mem[:, 12288 * b + 8192:12288 * b + 12288].rearrange("p (f c) -> p f c", f=2) for b in range(2)]
        y_sb = [mem[0:CAP, 24576 + D * b:24576 + D * (b + 1)] for b in range(2)]
        xg = [mem[0:CAP, 28672 + D * b:28672 + D * (b + 1)] for b in range(2)]
        xgT = [h_mem[:, KT * CAP * b:KT * CAP * (b + 1)].rearrange("p (k r) -> p k r", k=KT) for b in range(2)]
        hgate = h_mem[0:CAP, 2048:2048 + ED]
        hid = h_mem[0:CAP, 2304:2304 + ED]
        hidT = h_mem[:, 2560:2560 + 2 * CAP].rearrange("p (f r) -> p f r", f=2)
        assert 28672 + 2 * D <= END
        yp = [mem[:, D * b:D * (b + 1)] for b in range(6)]
        gfin = mem[:, 6 * D:7 * D]
        fin = [mem[:, (7 + b) * D:(8 + b) * D] for b in range(3)]

        xt = sb("xt", [P, 3, D])
        cst = sb("cst", [P, CW])
        gT = sb("gT", [P, 2, KT])
        small_in = sb("small_in", [CB, 4, P])
        peT = sb("peT", [P, 2, CB])
        w2 = sb("w2", [P, 2, P])
        kT = sb("kT", [P, 2, KVH, TOK])
        hidcT = sb("hidcT", [P, 2, NSEQ * KVH * NCB])
        kcT = sb("kcT", [P, NSEQ * KVH * NCB])
        ptab = sb("ptab", [1, PAGES], I32)
        ss = sb("ss", [P, 3])
        rstd = sb("rstd", [P, 3])
        epsb = sb("epsb", [P, 1])
        gbr = sb("gbr", [P, 3, NH, 3])
        gsm = sb("gsm", [NH * DT, DB, 3])
        att = xt[:].rearrange("p t d -> p (t d)")
        page_rows = att[:, 0:1024].rearrange("p (b c) -> p b c", b=2)
        rtmp = att[:, 1024:1024 + 48 * HALF].rearrange("p (k c) -> p k c", k=4)
        q_st = att[:, 0:1024].rearrange("p (g t) -> p g t", g=GQ)
        v_st = att[:, 1024:1536].rearrange("p (t r d) -> p t r d", t=2, r=2)
        vc_st = att[0:NCB, 1536:2048]
        pr = att[:, 2048:2048 + 2 * 584].rearrange("p (b c) -> p b c", b=2)
        pT = att[:, 3216:3216 + 1024].rearrange("p (b c) -> p b c", b=2)
        pcT = att[:, 4240:4240 + 384].rearrange("p (b c) -> p b c", b=2)
        qpad = att[:, 4640:4640 + 320]
        vcs_st = att[0:NCB, 4960:5472]
        vch_st = att[0:NCB, 5504:5504 + HD]
        hidc_st = att[:, 5472:5472 + KVH * NCB]
        scr2 = att[:, D:D + 1152]
        squares_at = [mem[:, K0:K0 + D], mem[:, 30720:30720 + D], mem[:, 20480:20480 + D]]
        hn_at = [[mem[:, o + D * t:o + D * (t + 1)] for t in range(3)] for o in (U0, W0)]
        stt = sb("stt", [P, 2, 12])
        bn = sb("bn", [P, 3, 4, 6])
        mv = sb("mv", [P, 3, 2])
        sig = kT[:].rearrange("p b h t -> p (b h t)")[:, 0:4 * TOK].rearrange("p (a c t) -> p a c t", a=2, c=2)
        wbr = att[:, 4096:4096 + KT * 48].rearrange("p (k c) -> p k c", k=KT)
        wr = sb("wr", [P, KT, NG + NE])
        rb = sb("rb", [P, NG + NE])
        lg = sb("lg", [P, 3, NG + NE])
        g8 = sb("g8", [P, 3, 8])
        mx8 = sb("mx8", [P, 3, 8])
        mi8 = sb("mi8", [P, 3, 8], U32)
        mif = sb("mif", [P, 3, 8])
        goh = sb("goh", [P, 3, 8])
        le4 = sb("le4", [P, 3, EPG, NG])
        le = sb("le", [P, 3, 8])
        rs = sb("rs", [P, 12, 3])
        oh = sb("oh", [P, 3, 2, NE])
        selm = sb("selm", [P, 3, NE])
        cnt = sb("cnt", [P, NE])
        novf = sb("novf", [P, 3, NE])
        posn = sb("posn", [P, 3, NE])
        posn2 = sb("posn2", [P, 3, NE])
        slotf = sb("slotf", [P, 3, 2])
        sloti = sb("sloti", [P, 3, 2], I32)
        ids = sb("ids", [P, 3, 2, 2], I32)
        ovf_cmp = h_mem[:, 2688:2688 + NOVF * NE].rearrange("p (o e) -> p o e", o=NOVF)
        ovf_ef = sb("ovf_ef", [P, NOVF + 1])
        ovf_e = sb("ovf_e", [P, NOVF + 1], I32)
        slots = sb("slots", [CAP, NITEM, 2], I32)
        slot_fill = sb("slot_fill", [CAP, NITEM * 2], I32)
        idx = sb("idx", [CAP, 2, 2], I32)

        def c_(name, rows=P):
            o, w = CONSTS[name]
            return cst[0:rows, o:o + w]

        ident = c_("ident")
        ps = ctx.enter_context(nc.psum_tensor("ps", [P, 8, 512], F32))

        S = {}
        for n in ("x_in consts_in small_in_in w_aux_in w1k_in w1v_in wbr_in br_in rows_out ln_in ws_in wss_in ptab_in "
                  "page_in0 page_in1 kv0_in kv1_in gate_out gate_in h2_out slot_fill_out slot_out slots_in yp_in "
                  "stores_a stores_g stores_s "
                  "w_in0 w_in1 w_in2 w_in3 w_used "
                  "act_chain dve_chain pe_passed dve_passed pool_passed sp_passed "
                  "squares rstd_sq normed tp_full tp_free "
                  "kv_ev_act kv_ev_dve br_full br_done gates_done roped kT_ready "
                  "page_T page_ev cmp_hid_full cmp_hid kc_full kc_ready vc_full vc_ready "
                  "q_ev_act q_ev_dve rot_full rot_done q_ready "
                  "st_ready s_full s_free sc_ready p_exp p_ready pt_full pt_act pt_dve pv_done o_ev "
                  "kx_ev_a kx_ev_d qp_ready t_full t_free tsc_ready tp_exp tp_ready tpt_full tpt_act tpt_dve tpv_done to_ev "
                  "pool_init v_ev v_ready u_ev sp_full sp_done "
                  "ws_masked m_ev_act m_ev_dve wo_ev zsq lg_full lg_done rank_full rank_done "
                  "ids_ready slots_rdy xg_in0 xg_in1 xt_done xgT_ready gu_done hg_done hid_done ht_done hidT_ready "
                  "dn_done y_act y_dve y_out0 y_out1 wgu_in0 wgu_in1 wdn_in0 wdn_in1 "
                  "idx_ready o_idx o_xg o_w o_xt o_xgT o_gu o_hg o_hid o_ht o_hidT o_dn o_ya o_free o_yout "
                  "x2_done fin_sq fin_ready init_done dve_init kxT_full").split():
            S[n] = sem(n)
        s = type("Sems", (), S)

        w_view = a["w_in"].rearrange("l (k p) c -> p (l k) c", p=P)
        block = ctx.enter_context(nc.Block())

        N_STORES_KV = 6 + 4 + 2 * DB
        N_STORES_A = N_STORES_KV + 1
        KV_IT, Q_IT, V_IT, U_IT, M_IT, O_IT = 6, 4, 4, 4, 8, 4
        IT_Q = KV_IT
        IT_V = IT_Q + Q_IT
        IT_U = IT_V + V_IT
        IT_M = IT_U + U_IT
        IT_O = IT_M + 2 * M_IT
        IT_END = IT_O + O_IT

        def chunk_done(it, b):
            return it * 4 + (2 * b + 2)

        w_sems = [s.w_in0, s.w_in1, s.w_in2, s.w_in3]
        xg_sems, y_sems = [s.xg_in0, s.xg_in1], [s.y_out0, s.y_out1]
        wgu_sems, wdn_sems = [s.wgu_in0, s.wgu_in1], [s.wdn_in0, s.wdn_in1]
        page_sems, kvx_sems = [s.page_in0, s.page_in1], [s.kv0_in, s.kv1_in]

        @block.sync
        def _(sp):
            def load_x():
                for t in range(2):
                    sp.dma_start(xt[:, t, :], a["x_prompt"][0, t * P:(t + 1) * P, :]).then_inc(s.x_in, 16)
                sp.dma_start(xt[0:NS, 2, :], a["x_sample"].rearrange("b t d -> (b t) d")).then_inc(s.x_in, 16)

            load_x()

            def load(it, u, src, col):
                if not isinstance(it, int) or it > 0:
                    apart(sp, s.w_used, it * 4 + (u - 3), s.sp_passed)
                h = u % 2
                sp.dma_start(ring[:, u], src[:, 8 * h:8 * h + 8, ds(col, 256)]).then_inc(w_sems[u], 16)

            def stream(first, count, src, col0):
                def body(it):
                    for u in range(4):
                        load(it, u, src, (it - first) * 512 + (col0 + 256 * (u // 2)))
                if first == 0:
                    body(0)
                with sp.Fori(max(first, 1), first + count) as it:
                    body(it)

            wv = {n: a[n].rearrange("l (k p) c -> p (l k) c", p=P) for n in ("w_pa", "w_pb", "w_o")}
            stream(0, KV_IT, w_view, C_KV)
            stream(IT_Q, Q_IT, w_view, C_Q)
            stream(IT_V, V_IT, w_view, C_V)
            stream(IT_U, U_IT, w_view, C_U)
            with sp.Fori(0, M_IT) as c:
                for half, (g_col, w_p) in enumerate(((C_GA, "w_pa"), (C_GB, "w_pb"))):
                    it = c * 2 + (IT_M + half)
                    for u in range(2):
                        load(it, u, w_view, c * 256 + g_col)
                    for u in range(2, 4):
                        load(it, u, wv[w_p], c * 256)
            sp.wait_ge(s.sp_done, KT)
            load_x()
            stream(IT_O, O_IT, wv["w_o"], 0)

            wg = a["w_gate"].rearrange("l e (k p) f -> p (l e) k f", p=P)
            wu = a["w_up"].rearrange("l e (k p) f -> p (l e) k f", p=P)
            wd = a["w_down"].rearrange("l e (f p) d -> p (l e) f d", p=P)

            def one(view, e):
                return view[:, ds(e, 1)].rearrange("p a k f -> p (a k) f")

            def experts(j):
                for b in range(2):
                    e = j * 2 + b
                    if isinstance(j, int):
                        if b == 0:
                            sp.wait_ge(s.m_ev_dve, 2 * M_IT)
                            sp.wait_ge(s.stores_a, 16 * N_STORES_A)
                        else:
                            sp.wait_ge(s.w_used, 4 * IT_END)
                    after(sp, s.gu_done, e - 1)
                    sp.dma_start(wgu[b][:, :, 0:ED], one(wg, e)).then_inc(wgu_sems[b], 16)
                    sp.dma_start(wgu[b][:, :, ED:2 * ED], one(wu, e)).then_inc(wgu_sems[b], 16)
                    after(sp, s.dn_done, e - 1)
                    sp.dma_start(wdn[b], one(wd, e)).then_inc(wdn_sems[b], 16)

            loop(sp, None, NE // 2, experts)

            sp.wait_ge(s.slots_rdy, 1)
            n_ovf = sp.value_load(ovf_e[0:1, NOVF:NOVF + 1], min_val=0, max_val=NOVF)
            with sp.If(n_ovf > 0):
                sp.wait_ge(s.dn_done, NE)
                with sp.Fori(0, n_ovf) as o:
                    sp.wait_ge(s.o_free, o + 1)
                    e = sp.value_load(ovf_e[0:1, ds(o, 1)], min_val=0, max_val=NE - 1)
                    sp.dma_start(wgu[0][:, :, 0:ED], one(wg, e)).then_inc(s.o_w, 16)
                    sp.dma_start(wgu[0][:, :, ED:2 * ED], one(wu, e)).then_inc(s.o_w, 16)
                    sp.dma_start(wdn[0], one(wd, e)).then_inc(s.o_w, 16)

            sp.wait_ge(s.pool_init, 3)
            for k in range(2):
                for t in range(3):
                    r = ROWS[t]
                    sp.dma_start(yp[2 * t + k][0:r], ypair_d[k * TOK + t * P:k * TOK + t * P + r, :]).then_inc(s.yp_in, 16)
            sp.dma_start(gfin, a["g_final"].partition_broadcast(P)).then_inc(s.yp_in, 16)
            for t in range(3):
                sp.wait_ge(s.fin_ready, t + 1)
                dst = y_prompt[0, t * P:(t + 1) * P, :] if t < 2 else y_sample.rearrange("b t d -> (b t) d")
                sp.dma_start(dst, fin[t][0:ROWS[t]]).then_inc(s.stores_s, 16)
            sp.wait_ge(s.stores_s, 48)
            sp.wait_ge(s.stores_a, 16 * N_STORES_A)
            sp.wait_ge(s.stores_g, 32)

        @block.gpsimd
        def _(pool):
            nc.gpsimd.memset(slot_fill[:], NOWHERE).then_inc(s.init_done, 1)
            pool.dma_start(ptab[:], a["page_table"].rearrange("b n -> (b n)").rearrange("(o n) -> o n", o=1)).then_inc(s.ptab_in, 16)
            pool.wait_ge(s.init_done, 1)
            pool.dma_start(slot_d.rearrange("(c i) k -> c (i k)", c=CAP), slot_fill[:]).then_inc(s.slot_fill_out, 16)
            for src, dst in ((a["state_k_win"], o_kws), (a["state_v_win"], o_vws)):
                pool.dma_start(dst[0, :, 0:PAST - DT], src[0, :, DT:PAST]).then_inc(s.stores_g, 16)
            pool.wait_ge(s.ptab_in, 16)

            pool.wait_ge(s.normed, 3)
            for n, cache in enumerate(("cache_k_cmp", "cache_v_cmp")):
                rows = a[cache].rearrange("l n t h d -> t (l n) (h d)")

                def pages(i, n=n, rows=rows):
                    for b in range(2):
                        k = n * PAGES + i * 2 + b
                        if n or not isinstance(i, int):
                            apart(pool, s.page_T, k - 1, s.pool_passed)
                        page = pool.value_load(ptab[0:1, ds(i * 2 + b, 1)], min_val=0, max_val=a[cache].shape[1] - 1)
                        pool.dma_start(page_rows[:, b], rows[:, ds(page, 1)].rearrange("p a c -> p (a c)")).then_inc(page_sems[b], 16)

                loop(pool, None, PAGES // 2, pages)

            ks = a["cache_k_slc"].rearrange("l n t h d -> t (l n) (h d)")
            vs = a["cache_v_slc"].rearrange("l n t h d -> t (l n) (h d)")
            kw = a["state_k_win"].rearrange("l b (u t) h d -> t (l b) u (h d)", t=P)
            vw = a["state_v_win"].rearrange("l b (u t) h d -> t (l b) u (h d)", t=P)
            pool.wait_ge(s.cmp_hid, 2)

            def sequences(i):
                for b in range(2):
                    apart(pool, s.kxT_full, i * 8 + 4 * (b - 1), s.pool_passed)
                    apart(pool, s.tpv_done, i * 2 + (b - 1), s.pool_passed)
                    for u in range(2):
                        page = pool.value_load(ptab[0:1, ds(i * 4 + (2 * b + u), 1)], min_val=0, max_val=a["cache_k_slc"].shape[1] - 1)
                        pool.dma_start(kx[:, b, u], ks[:, ds(page, 1)].rearrange("p a c -> p (a c)")).then_inc(kvx_sems[b], 16)
                        pool.dma_start(vx[:, b, u], vs[:, ds(page, 1)].rearrange("p a c -> p (a c)")).then_inc(kvx_sems[b], 16)
                    pool.dma_start(kx[:, b, 2:4], kw[:, ds(i * 2 + b, 1)].rearrange("p a u c -> p (a u) c")).then_inc(kvx_sems[b], 16)
                    pool.dma_start(vx[:, b, 2:4], vw[:, ds(i * 2 + b, 1)].rearrange("p a u c -> p (a u) c")).then_inc(kvx_sems[b], 16)

            loop(pool, None, DB // 2, sequences)

            pool.wait_ge(s.tpv_done, DB)
            pool.wait_ge(s.stores_a, 16 * N_STORES_KV)
            nc.gpsimd.memset(wss_raw, 0.0).then_inc(s.pool_init, 1)
            pool.dma_start(ws_raw, a["a_w_s"][0].rearrange("g i j -> i g j")).then_inc(s.ws_in, 16)
            pool.wait_ge(s.pool_init, 1)
            for b in range(DB):
                r = slice(DT * b, DT * b + DT)
                pool.dma_start(wss_raw[r, :, r], a["a_w_s"][0, :, 0:DT, 0:DT].rearrange("g i j -> i g j")).then_inc(s.ws_in, 16)
            for t in range(2):
                pool.dma_start(sbias[:, :, t * P:(t + 1) * P], a["a_b_s"][0].partition_broadcast(P)).then_inc(s.ln_in, 16)
            for b in range(DB):
                pool.dma_start(sbias[:, :, SEQ + DT * b:SEQ + DT * b + DT], a["a_b_s"][0, :, 0:DT].partition_broadcast(P)).then_inc(s.ln_in, 16)
            pool.dma_start(ln_g, a["a_ln_g"][0].partition_broadcast(P)).then_inc(s.ln_in, 16)
            pool.dma_start(ln_b, a["a_ln_b"][0].partition_broadcast(P)).then_inc(s.ln_in, 16)
            pool.wait_ge(s.ws_in, 16 * (1 + DB))
            nc.gpsimd.affine_select(out=ws_raw, in_=ws_raw, compare_op=ALU.is_ge, fill=0.0, base=0,
                                    pattern=[[0, AG], [-1, P]], channel_multiplier=1).then_inc(s.ws_masked, 1)
            nc.gpsimd.affine_select(out=wss_raw, in_=wss_raw, compare_op=ALU.is_ge, fill=0.0, base=0,
                                    pattern=[[0, AG], [-1, NS]], channel_multiplier=1).then_inc(s.ws_masked, 1)

            pool.wait_ge(s.h2_out, 48)
            pool.wait_ge(s.lg_full, 1)
            nc.gpsimd.memset(mem[0:CAP, 28672:28672 + 2 * D], 0.0).then_inc(s.pool_init, 1)
            pool.wait_ge(s.ids_ready, 1)
            pool.wait_ge(s.slot_fill_out, 16)
            for t in range(3):
                for k in range(2):
                    pool.indirect_dma_start(out=slot_d, out_offset=bass.IndirectOffsetOnAxis(ap=sloti[0:ROWS[t], t, k:k + 1], axis=0),
                                            in_=ids[0:ROWS[t], t, k, :], in_offset=None).then_inc(s.slot_out, 16)
            pool.wait_ge(s.slot_out, 96)
            pool.dma_start(slots[:], slot_d.rearrange("(i c) k -> c i k", c=CAP)).then_inc(s.slots_in, 16)
            pool.wait_ge(s.slots_in, 16)
            pool.wait_ge(s.pool_init, 2)

            def gather(b, sem_):
                pool.indirect_dma_start(out=xg[b], out_offset=None, in_=h2_d,
                                        in_offset=bass.IndirectOffsetOnAxis(ap=idx[:, b, 0:1], axis=0),
                                        bounds_check=TOK - 1, oob_is_err=False).then_inc(sem_, 16)

            def scatter(b, sem_):
                pool.indirect_dma_start(out=ypair_d, out_offset=bass.IndirectOffsetOnAxis(ap=idx[:, b, 1:2], axis=0),
                                        in_=y_sb[b], in_offset=None,
                                        bounds_check=2 * TOK - 1, oob_is_err=False).then_inc(sem_, 16)

            def fetch(j, b):
                nc.gpsimd.tensor_copy(idx[:, b, :], slots[:, ds(j * 2 + b, 1), :].rearrange("p a k -> p (a k)")).then_inc(s.idx_ready, 1)
                apart(pool, s.idx_ready, j * 2 + (b + 1), s.pool_passed)
                gather(b, xg_sems[b])

            fetch(0, 0)
            fetch(0, 1)

            def items(j):
                for b in range(2):
                    e = j * 2 + b
                    pool.wait_ge(s.y_act, e + 1)
                    apart(pool, s.y_dve, e + 1, s.pool_passed)
                    scatter(b, y_sems[b])
                    apart(pool, y_sems[b], (j + 1) * 16, s.pool_passed)
                    apart(pool, s.xt_done, e + 1, s.pool_passed)
                    fetch(j + 1, b)

            loop(pool, None, NE // 2, items)

            n_ovf = pool.value_load(ovf_e[0:1, NOVF:NOVF + 1], min_val=0, max_val=NOVF)
            pool.wait_ge(s.xt_done, NE + 1)
            pool.wait_ge(xg_sems[1], 16 * (NE // 2 + 1))
            with pool.If(n_ovf > 0):
                with pool.Fori(0, n_ovf) as o:
                    nc.gpsimd.tensor_copy(idx[:, 0, :], slots[:, ds(o + NE, 1), :].rearrange("p a k -> p (a k)")).then_inc(s.o_idx, 1)
                    apart(pool, s.o_idx, o + 1, s.pool_passed)
                    gather(0, s.o_xg)
                    apart(pool, s.o_ya, o + 1, s.pool_passed)
                    scatter(0, s.o_yout)
                    apart(pool, s.o_yout, (o + 1) * 16, s.pool_passed)
            pool.sem_inc(s.pool_init, 1)

        @block.scalar
        def _(act):
            ch = Chain(act, s.act_chain)
            A = nc.scalar.activation
            act.dma_start(cst[:], a["consts"]).then_inc(s.consts_in, 16)
            act.dma_start(small_in[0:KT, 0], a["g_mix"][0].rearrange("(k p) -> k p", p=P)).then_inc(s.small_in_in, 16)
            act.dma_start(small_in[0:KT, 1], a["g_ffn"][0].rearrange("(k p) -> k p", p=P)).then_inc(s.small_in_in, 16)
            act.dma_start(small_in[:, 2], a["cmp_pe_k"][0]).then_inc(s.small_in_in, 16)
            act.dma_start(small_in[:, 3], a["cmp_pe_v"][0]).then_inc(s.small_in_in, 16)
            act.dma_start(w2[:, 0], a["cmp_w2_k"][0]).then_inc(s.w_aux_in, 16)
            act.dma_start(w2[:, 1], a["cmp_w2_v"][0]).then_inc(s.w_aux_in, 16)
            act.dma_start(wr[:, :, 0:NG], a["w_rg"][0].rearrange("(k p) g -> p k g", p=P)).then_inc(s.w_aux_in, 16)
            act.dma_start(wr[:, :, NG:], a["w_re"][0].rearrange("(k p) g -> p k g", p=P)).then_inc(s.w_aux_in, 16)
            act.dma_start(rb[:, 0:NG], a["b_rg"][0].partition_broadcast(P)).then_inc(s.w_aux_in, 16)
            act.dma_start(rb[:, NG:], a["b_re"][0].partition_broadcast(P)).then_inc(s.w_aux_in, 16)
            act.dma_start(w1, a["cmp_w1_k"][0].rearrange("j d e -> d j e")).then_inc(s.w1k_in, 16)

            def sum_squares(which, t, wait_sem, value):
                if wait_sem is not None:
                    act.wait_ge(wait_sem, value)
                after(act, s.squares, 3 * which + t)
                A(squares_at[which][0:ROWS[t]], xt[0:ROWS[t], t, :], ACT.Square, accum_out=ss[0:ROWS[t], t:t + 1]).then_inc(s.squares, 1)

            act.wait_ge(s.x_in, 48)
            act.wait_ge(s.dve_init, 1)
            for t in range(3):
                sum_squares(0, t, None, 0)
            act.wait_ge(s.squares, 3)
            A(rstd[:], ss[:], ACT.Sqrt, bias=epsb[:, 0:1], scale=1.0 / D).then_inc(s.rstd_sq, 1)

            act.wait_ge(s.normed, 3)
            act.dma_start(wbr, w_view[:, :, C_BR:C_BR + 48]).then_inc(s.wbr_in, 16)

            def kv_even(i):
                act.wait_ge(s.w_used, chunk_done(i, 0))
                nc.scalar.copy(kv[:, 0:2, ds(i * 512, 256)], ps[:, 0:2, 0:256])
                nc.scalar.copy(kv[0:NS, 2, ds(i * 512, 256)], ps[0:NS, 2, 0:256]).then_inc(s.kv_ev_act, 1)

            loop(act, None, KV_IT, kv_even)
            act.wait_ge(s.br_full, 1)
            act.wait_ge(s.dve_init, 2)
            for t in range(3):
                r = ROWS[t]
                for c, src in enumerate((1, 2, 0)):
                    A(gbr[0:r, t, :, c], ps[0:r, 6, t * 48:(t + 1) * 48].rearrange("p (h c) -> p h c", c=3)[:, :, src], ACT.Sigmoid).then_inc(s.br_done, 1)
            act.wait_ge(s.roped, 1)
            for br, (op, os) in enumerate(((o_kcp, o_kcs), (o_vcp, o_vcs), (o_ksp, o_kss), (o_vsp, o_vss), (o_kwp, None), (o_vwp, None))):
                act.dma_start(op[0, 0].rearrange("(t p) h d -> p t (h d)", p=P), kv[:, 0:2, br * KVC:(br + 1) * KVC]).then_inc(s.stores_a, 16)
                if os is not None:
                    act.dma_start(os[0].rearrange("b t h d -> (b t) (h d)"), kv[0:NS, 2, br * KVC:(br + 1) * KVC]).then_inc(s.stores_a, 16)
                else:
                    dst = (o_kws, o_vws)[br - 4]
                    for b in range(DB):
                        act.dma_start(dst[0, b, PAST - DT:PAST].rearrange("t h d -> t (h d)"),
                                      kv[b * DT:(b + 1) * DT, 2, br * KVC:(br + 1) * KVC]).then_inc(s.stores_a, 16)
            act.wait_ge(s.gates_done, 1)
            act.dma_start(gate_d, gbr[0:NS, 2].rearrange("p h c -> p (h c)")).then_inc(s.gate_out, 16)
            act.wait_ge(s.gate_out, 16)
            for h in range(NH):
                act.dma_start(gsm[h * DT:(h + 1) * DT], gate_d.rearrange("(b t) (h c) -> t b h c", t=DT, c=3)[:, :, h, :]).then_inc(s.gate_in, 16)

            for n in range(2):
                act.wait_ge(s.cmp_hid_full, n + 1)
                if n == 0:
                    act.dma_start(w1, a["cmp_w1_v"][0].rearrange("j d e -> d j e")).then_inc(s.w1v_in, 16)
                src = ps[:, n, 0:288].rearrange("p (s g h k) -> p s g h k", s=NSEQ, g=2, h=KVH)
                dst = hidcT[:, n].rearrange("p (s h g k) -> p s g h k", s=NSEQ, g=2, h=KVH)
                A(dst[:, :, 0], src[:, :, 0], ACT.Gelu_apprx_tanh)
                A(dst[:, :, 1], src[:, :, 1], ACT.Gelu_apprx_tanh).then_inc(s.cmp_hid, 1)

            def q_even(i):
                act.wait_ge(s.w_used, chunk_done(i + IT_Q, 0))
                nc.scalar.copy(qT[:, ds(i * 4, 2), :], ps[:, 0:2, 0:TOK]).then_inc(s.q_ev_act, 1)

            loop(act, None, Q_IT, q_even)

            def heads(kh):
                for g in range(GQ):
                    for qt in range(2):
                        n = kh * 8 + (g * 2 + qt)
                        nk = P * (qt + 1)
                        b = qt
                        act.wait_ge(s.sc_ready, n + 1)
                        st = stt[:, b]
                        for c, part in enumerate((pr[:, b, 0:nk], pr[:, b, 256:256 + nk], pr[:, b, 512:520])):
                            ins = A(part, part, ACT.Exp, bias=st[:, 3 + c:4 + c], accum_out=st[:, 6 + c:7 + c])
                        ins.then_inc(s.p_exp, 1)
                        act.wait_ge(s.pt_full, n + 1)
                        after(act, s.pv_done, n - 1)
                        if qt == 0:
                            for w in range(2):
                                ins = nc.scalar.copy(pT[:, b, w * 256:w * 256 + P], ps[:, 4, w * 256:w * 256 + P])
                        else:
                            ins = nc.scalar.copy(pT[:, b], ps[:, 4])
                        ins.then_inc(s.pt_act, 1)

            loop(act, None, KVH, heads)

            def sample(i):
                for b in range(2):
                    n = i * 2 + b
                    for h in (0, 2):
                        act.wait_ge(s.kxT_full, n * 4 + (h + 1))
                        nc.scalar.copy(kxT[:, h], ps[:, 6]).then_inc(s.kx_ev_a, 1)
                    act.wait_ge(s.tsc_ready, n + 1)
                    st = stt[0:64, 0]
                    for c, part in enumerate((pr[0:64, 0, 0:288], pr[0:64, 0, 288:576], pr[0:64, 0, 576:584])):
                        ins = A(part, part, ACT.Exp, bias=st[:, 3 + c:4 + c], accum_out=st[:, 6 + c:7 + c])
                    ins.then_inc(s.tp_exp, 1)
                    act.wait_ge(s.tpt_full, n + 1)
                    nc.scalar.copy(pT[:, 0, 0:256], ps[:, 2, 0:256]).then_inc(s.tpt_act, 1)

            loop(act, None, DB // 2, sample)

            def v_act(i):
                for b in range(2):
                    act.wait_ge(s.w_used, chunk_done(i + IT_V, b))
                    A(v_tok[:, 0:2, ds(i * 512 + b * 256, 256)], ps[:, 3 * b:3 * b + 2, 0:256], ACT.Gelu_apprx_tanh)
                    A(v_tok[0:NS, 2, ds(i * 512 + b * 256, 256)], ps[0:NS, 3 * b + 2, 0:256], ACT.Gelu_apprx_tanh).then_inc(s.v_ev, 1)

            loop(act, None, V_IT, v_act)
            act.wait_ge(s.rstd_sq, 2)
            A(rstd[:], mv[:, :, 1], ACT.Sqrt, bias=epsb[:, 0:1]).then_inc(s.rstd_sq, 1)
            act.wait_ge(s.v_ready, 1)
            act.dma_start(o_vchunk[0].rearrange("b t c -> (b t) c"), v_tok[0:NS, 2, :]).then_inc(s.stores_a, 16)

            def u_act(i):
                for b in range(2):
                    act.wait_ge(s.w_used, chunk_done(i + IT_U, b))
                    A(uT[:, ds(i * 4 + 2 * b, 2), :], ps[:, 3 * b:3 * b + 2, 0:TOK], ACT.Gelu_apprx_tanh).then_inc(s.u_ev, 1)

            loop(act, None, U_IT, u_act)

            def m_act(c):
                for half in range(2):
                    n = c * 2 + half
                    act.wait_ge(s.w_used, chunk_done(n + IT_M, 0))
                    after(act, s.m_ev_dve, n - 1)
                    A(sig[:, half], ps[:, 0:2, 0:TOK], ACT.Sigmoid).then_inc(s.m_ev_act, 1)

            loop(act, None, M_IT, m_act)

            for t in range(3):
                sum_squares(1, t, s.wo_ev, 2 * O_IT)
            act.wait_ge(s.squares, 6)
            A(rstd[:], ss[:], ACT.Sqrt, bias=epsb[:, 0:1], scale=1.0 / D).then_inc(s.rstd_sq, 1)
            for t in range(3):
                act.wait_ge(s.normed, 3 + t + 1)
                act.dma_start(h2_d[t * P:t * P + ROWS[t], :], hn_at[1][t][0:ROWS[t]]).then_inc(s.h2_out, 16)
            act.wait_ge(s.zsq, 1)
            for t in range(3):
                A(g8[:, t, 0:NG], lg[:, t, 0:NG], ACT.Exp, bias=rs[:, 0, t:t + 1], accum_out=rs[:, 1, t:t + 1]).then_inc(s.lg_done, 1)
            act.wait_ge(s.zsq, 2)
            A(rs[:, 3], rs[:, 2], ACT.Exp).then_inc(s.lg_done, 1)

            def item(j):
                for b in range(2):
                    e = j * 2 + b
                    act.wait_ge(s.gu_done, e + 1)
                    after(act, s.hid_done, e)
                    A(hgate, ps[0:CAP, 2, 0:ED], ACT.Silu).then_inc(s.hg_done, 1)
                    act.wait_ge(s.ht_done, e + 1)
                    after(act, s.dn_done, e)
                    nc.scalar.copy(hidT, ps[:, 3, 0:2 * CAP].rearrange("p (f r) -> p f r", f=2)).then_inc(s.hidT_ready, 1)
                    act.wait_ge(s.dn_done, e + 1)
                    after(act, y_sems[b], j * 16)
                    nc.scalar.copy(y_sb[b][:, 0:1024].rearrange("p (n c) -> p n c", n=2), ps[0:CAP, 4:6]).then_inc(s.y_act, 1)

            loop(act, None, NE // 2, item)
            n_ovf = act.value_load(ovf_e[0:1, NOVF:NOVF + 1], min_val=0, max_val=NOVF)
            with act.If(n_ovf > 0):
                with act.Fori(0, n_ovf) as o:
                    act.wait_ge(s.o_gu, o + 1)
                    A(hgate, ps[0:CAP, 2, 0:ED], ACT.Silu).then_inc(s.o_hg, 1)
                    act.wait_ge(s.o_ht, o + 1)
                    nc.scalar.copy(hidT, ps[:, 3, 0:2 * CAP].rearrange("p (f r) -> p f r", f=2)).then_inc(s.o_hidT, 1)
                    act.wait_ge(s.o_dn, o + 1)
                    nc.scalar.copy(y_sb[0].rearrange("p (n c) -> p n c", n=4), ps[0:CAP, 4:8]).then_inc(s.o_ya, 1)
            for t in range(3):
                act.wait_ge(s.x2_done, t + 1)
                sum_squares(2, t, None, 0)
            act.wait_ge(s.squares, 9)
            A(rstd[:], ss[:], ACT.Sqrt, bias=epsb[:, 0:1], scale=1.0 / D).then_inc(s.rstd_sq, 1)

        @block.vector
        def _(dve):
            ch = Chain(dve, s.dve_chain)
            V = nc.vector
            link = ch.link
            V.memset(epsb[:], EPS)
            V.memset(ss[:], 1.0).then_inc(s.dve_init, 1)
            V.memset(gbr[:], 0.0).then_inc(s.dve_init, 1)
            V.memset(lg[:], 0.0)
            V.memset(mv[:], 1.0)
            V.memset(posn[:], 0.0)
            link(V.memset(g8[:], NEG))
            tp = [0]

            def evac(out, in_, gain=None):
                dve.wait_ge(s.tp_full, tp[0] + 1)
                bank = 6 + tp[0] % 2
                src = in_(ps[:, bank])
                if gain is None:
                    V.tensor_copy(out, src).then_inc(s.tp_free, 1)
                else:
                    V.tensor_tensor(out, src, gain, ALU.mult).then_inc(s.tp_free, 1)
                tp[0] += 1

            evac(gT[:, 0], lambda p: p[:, 0:KT])
            evac(gT[:, 1], lambda p: p[:, 0:KT])
            evac(peT[:, 0], lambda p: p[:, 0:CB])
            evac(peT[:, 1], lambda p: p[:, 0:CB])

            def norm(which, sq_value):
                hn = hn_at[which]
                dve.wait_ge(s.rstd_sq, sq_value)
                link(V.reciprocal(rstd[:], rstd[:]))
                for t in range(3):
                    r = ROWS[t]
                    V.tensor_scalar(hn[t][0:r], xt[0:r, t, :], rstd[0:r, t:t + 1], None, ALU.mult).then_inc(s.normed, 1)
                for t in range(3):
                    r = ROWS[t]
                    for k4 in range(4):
                        if tp[0] == 4:
                            dve.wait_ge(s.tp_free, 4)
                        evac(hT[:, 4 * k4:4 * k4 + 4, t * P:t * P + r],
                             lambda p, r=r: p.rearrange("p (k t) -> p k t", k=4)[:, :, 0:r],
                             bcast(gT[:, which, 4 * k4:4 * k4 + 4].unsqueeze(2), [P, 4, r]))

            norm(0, 1)

            def kv_odd(i):
                dve.wait_ge(s.w_used, chunk_done(i, 1))
                V.tensor_copy(kv[:, 0:2, ds(i * 512 + 256, 256)], ps[:, 3:5, 0:256])
                V.tensor_copy(kv[0:NS, 2, ds(i * 512 + 256, 256)], ps[0:NS, 5, 0:256]).then_inc(s.kv_ev_dve, 1)

            loop(dve, ch, KV_IT, kv_odd)
            dve.wait_ge(s.kv_ev_act, KV_IT)
            dve.wait_ge(s.kv_ev_dve, KV_IT)
            for t in range(3):
                r = ROWS[t]
                keys = kv[0:r, t].rearrange("p (b x h d) -> p b x h d", b=3, x=2, h=KVH)[:, :, 0]
                x1, x2 = keys[:, :, :, 0:HALF], keys[:, :, :, HALF:RD]
                co = bcast(c_("cos", r)[:, t * HALF:(t + 1) * HALF].unsqueeze(1).unsqueeze(1), [r, 3, KVH, HALF])
                si = bcast(c_("sin", r)[:, t * HALF:(t + 1) * HALF].unsqueeze(1).unsqueeze(1), [r, 3, KVH, HALF])
                tm = [rtmp[0:r, k].rearrange("p (b h d) -> p b h d", b=3, h=KVH) for k in range(4)]
                V.tensor_tensor(tm[0], x1, co, ALU.mult)
                V.tensor_tensor(tm[1], x2, si, ALU.mult)
                V.tensor_tensor(tm[2], x2, co, ALU.mult)
                link(V.tensor_tensor(tm[3], x1, si, ALU.mult))
                V.tensor_tensor(x1, tm[0], tm[1], ALU.subtract)
                ins = V.tensor_tensor(x2, tm[2], tm[3], ALU.add)
                link(ins)
            link(V.memset(stt[:], 0.0))
            dve.sem_inc(s.roped, 1)
            dve.wait_ge(s.br_done, 9)
            link(V.tensor_tensor(gbr[:, :, :, 2], gbr[:, :, :, 2], bcast(c_("anyvalid").unsqueeze(2), [P, 3, NH]), ALU.mult))
            dve.sem_inc(s.gates_done, 1)

            for br in range(2):
                for t in range(3):
                    r = ROWS[t]
                    evac(kT[:, br, :, t * P:t * P + r], lambda p, r=r: p.rearrange("p (k t) -> p k t", k=4)[:, :, 0:r])
            dve.wait_ge(s.tp_free, tp[0])
            dve.sem_inc(s.kT_ready, 1)

            for n in range(2):
                if n == 1:
                    dve.wait_ge(s.cmp_hid_full, 1)
                pe_b = bcast(peT[:, n].unsqueeze(1), [P, 16, CB])

                def pages(i, n=n, pe_b=pe_b):
                    for b in range(2):
                        dve.wait_ge(s.page_T, n * PAGES + (i * 2 + (b + 1)))
                        V.tensor_tensor(rowsT[:, ds(i * 1024 + b * 512, 512)].rearrange("p (a j) -> p a j", j=CB),
                                        ps[:, 6 + b].rearrange("p (a j) -> p a j", j=CB), pe_b, ALU.add).then_inc(s.page_ev, 1)

                loop(dve, ch, PAGES // 2, pages)
                for t in range(2):
                    dve.wait_ge(s.tp_full, tp[0] + 1)
                    V.tensor_tensor(rowsT[:, (16 + t) * 512:(17 + t) * 512].rearrange("p (a j) -> p a j", j=CB),
                                    ps[:, 6 + tp[0] % 2].rearrange("p (a j) -> p a j", j=CB), pe_b, ALU.add).then_inc(s.tp_free, 1)
                    tp[0] += 1
                if n == 0:
                    dve.wait_ge(s.kc_full, 1)
                    V.tensor_copy(kcT[:], ps[:, 2, 0:288]).then_inc(s.kc_ready, 1)
                else:
                    dve.wait_ge(s.vc_full, 1)
                    V.tensor_copy(vc_st, ps[0:NCB, 3]).then_inc(s.vc_ready, 1)

            def q_odd(i):
                dve.wait_ge(s.w_used, chunk_done(i + IT_Q, 1))
                V.tensor_copy(qT[:, ds(i * 4 + 2, 2), :], ps[:, 3:5, 0:TOK]).then_inc(s.q_ev_dve, 1)

            loop(dve, ch, Q_IT, q_odd)
            dve.wait_ge(s.q_ev_act, Q_IT)
            dve.wait_ge(s.q_ev_dve, Q_IT)
            cosb = bcast(c_("cosT", RD).unsqueeze(1), [RD, 4, TOK])
            sinb = bcast(c_("sinT", RD).unsqueeze(1), [RD, 4, TOK])

            def rope_q(i):
                dve.wait_ge(s.rot_full, i + 1)
                q4 = qT[0:RD, ds(i * 4, 4), :]
                part = scr2[0:RD].rearrange("p (h t) -> p h t", h=4)
                V.tensor_tensor(q4, q4, cosb, ALU.mult)
                link(V.tensor_tensor(part, ps[0:RD, 0:4, 0:TOK], sinb, ALU.mult))
                dve.sem_inc(s.rot_done, 1)
                link(V.tensor_tensor(q4, q4, part, ALU.add))

            loop(dve, ch, 4, rope_q)
            dve.sem_inc(s.q_ready, 1)
            dve.wait_ge(s.vc_ready, 1)
            dve.wait_ge(s.kc_ready, 1)

            def heads(kh):
                apart(dve, s.pv_done, kh * 8, s.dve_passed)
                V.tensor_copy(q_st, qT[:, ds(kh * 4, 4), 0:SEQ])
                V.tensor_copy(vch_st, vc_st[:, ds(kh * HD, HD)])
                for c, br in enumerate((3, 5)):
                    ins = V.tensor_copy(v_st[:, :, c], kv[:, 0:2, ds(kh * HD + br * KVC, HD)])
                link(ins)
                dve.sem_inc(s.st_ready, 1)

                def scores(u):
                    g, qt = u // 2, u % 2
                    n = kh * 8 + u
                    nk = P * (qt + 1)
                    b = qt
                    st = stt[:, b]
                    dve.wait_ge(s.s_full, n + 1)
                    after(dve, s.pt_full, n - 1)
                    S2 = ps[:, 2 * b:2 * b + 2]
                    sc = pr[:, b, 0:512].rearrange("p (w k) -> p w k", w=2)
                    V.scalar_tensor_tensor(out=sc[:, :, 0:nk], in0=S2[:, :, 0:nk], scalar=SCALE,
                                           in1=bcast(c_("pmask")[:, 2 * P - nk:2 * P].unsqueeze(1), [P, 2, nk]),
                                           op0=ALU.mult, op1=ALU.add)
                    link(V.scalar_tensor_tensor(out=pr[:, b, 512:520], in0=S2[:, 0, 256:264], scalar=SCALE,
                                                in1=c_("cmask")[:, qt * NCB:(qt + 1) * NCB], op0=ALU.mult, op1=ALU.add))
                    dve.sem_inc(s.s_free, 1)
                    V.tensor_reduce(st[:, 0:2], sc[:, :, 0:nk], AX_X, ALU.max)
                    link(V.tensor_reduce(st[:, 2:3], pr[:, b, 512:520], AX_X, ALU.max))
                    V.tensor_scalar(st[:, 3:6], st[:, 0:3], -1.0, None, ALU.mult).then_inc(s.sc_ready, 1)

                def weigh(u):
                    g, qt = u // 2, u % 2
                    n = kh * 8 + u
                    nk = P * (qt + 1)
                    b = qt
                    st = stt[:, b]
                    dve.wait_ge(s.p_exp, n + 1)
                    link(V.reciprocal(st[:, 9:12], st[:, 6:9]))
                    link(V.tensor_tensor(st[:, 6:9], st[:, 9:12], gbr[:, qt, ds(kh * 4 + g, 1), :].rearrange("p a c -> p (a c)"), ALU.mult))
                    V.tensor_scalar(pr[:, b, 0:nk], pr[:, b, 0:nk], st[:, 6:7], None, ALU.mult)
                    V.tensor_scalar(pr[:, b, 256:256 + nk], pr[:, b, 256:256 + nk], st[:, 7:8], None, ALU.mult)
                    V.tensor_scalar(pr[:, b, 512:520], pr[:, b, 512:520], st[:, 8:9], None, ALU.mult).then_inc(s.p_ready, 1)

                def leave(u):
                    g, qt = u // 2, u % 2
                    n = kh * 8 + u
                    b = qt
                    apart(dve, s.pv_done, n + 1, s.dve_passed)
                    V.tensor_copy(qT[:, ds(kh * 4 + g, 1), qt * P:(qt + 1) * P].rearrange("p a t -> p (a t)"), ps[:, 6 + b, 0:P]).then_inc(s.o_ev, 1)

                def cmp_out(u):
                    n = kh * 8 + u
                    b = u % 2
                    dve.wait_ge(s.pt_full, n + 1)
                    after(dve, s.pv_done, n - 1)
                    V.tensor_copy(pcT[0:NCB, b, 0:P], ps[0:NCB, 5, 0:P]).then_inc(s.pt_dve, 1)

                scores(0)
                for u in range(8):
                    if u < 7:
                        scores(u + 1)
                    weigh(u)
                    if u:
                        leave(u - 1)
                    cmp_out(u)
                leave(7)

            loop(dve, ch, KVH, heads)

            dve.wait_ge(s.o_ev, 8 * KVH)
            dve.wait_ge(s.gate_in, 16 * NH)
            link(V.memset(qpad, 0.0))
            qpv = qpad.rearrange("p (h r) -> p h r", h=KVH)[:, :, 0:16].rearrange("p h (g t) -> p h g t", g=GQ)

            def sample(i):
                for b in range(2):
                    n = i * 2 + b
                    st = stt[0:64, 0]
                    apart(dve, s.tpv_done, n, s.dve_passed)
                    for h in range(KVH):
                        V.tensor_copy(qpv[:, h], qT[:, 4 * h:4 * h + 4, ds(n * DT + SEQ, DT)])
                    link(V.tensor_copy(hidc_st, hidcT[:, 1, ds(n * (KVH * NCB), KVH * NCB)]))
                    dve.sem_inc(s.qp_ready, 1)
                    for h in (1, 3):
                        dve.wait_ge(s.kxT_full, n * 4 + (h + 1))
                        V.tensor_copy(kxT[:, h], ps[:, 7]).then_inc(s.kx_ev_d, 1)
                    dve.wait_ge(s.t_full, n + 1)
                    sc = pr[0:64, 0, 0:576].rearrange("p (w k) -> p w k", w=2)
                    V.tensor_scalar(sc[:, :, 0:256], ps[0:64, 0:2, 0:256], SCALE, None, ALU.mult)
                    V.scalar_tensor_tensor(out=sc[:, :, 256:288], in0=ps[0:64, 0:2, 256:288], scalar=SCALE,
                                           in1=bcast(c_("smask", 64)[:, ds(n * NS, NS)].unsqueeze(1), [64, 2, NS]),
                                           op0=ALU.mult, op1=ALU.add)
                    link(V.tensor_scalar(pr[0:64, 0, 576:584], ps[0:64, 0, 288:296], SCALE, None, ALU.mult))
                    V.tensor_reduce(st[:, 0:2], sc, AX_X, ALU.max)
                    link(V.tensor_reduce(st[:, 2:3], pr[0:64, 0, 576:584], AX_X, ALU.max))
                    V.tensor_scalar(st[:, 3:6], st[:, 0:3], -1.0, None, ALU.mult).then_inc(s.tsc_ready, 1)
                    dve.wait_ge(s.tp_exp, n + 1)
                    link(V.reciprocal(st[:, 9:12], st[:, 6:9]))
                    link(V.tensor_tensor(st[:, 6:9], st[:, 9:12], gsm[:, ds(n, 1), :].rearrange("p a c -> p (a c)"), ALU.mult))
                    for c, (lo, hi) in enumerate(((0, 288), (288, 576), (576, 584))):
                        ins = V.tensor_scalar(pr[0:64, 0, lo:hi], pr[0:64, 0, lo:hi], st[:, 6 + c:7 + c], None, ALU.mult)
                    ins.then_inc(s.tp_ready, 1)
                    dve.wait_ge(s.tpt_full, n + 1)
                    V.tensor_copy(vcs_st, ps[0:NCB, 5])
                    V.tensor_copy(pcT[0:NS, 0, 0:P], ps[0:NS, 3, 0:P])
                    V.tensor_copy(pcT[0:NCB, 0, P:P + 64], ps[0:NCB, 3, P:P + 64]).then_inc(s.tpt_dve, 1)
                    apart(dve, s.tpv_done, n + 1, s.dve_passed)
                    V.tensor_copy(qT[:, :, ds(n * DT + SEQ, DT)], ps[:, 4, 0:64].rearrange("p (h t) -> p h t", t=DT)).then_inc(s.to_ev, 1)

            loop(dve, ch, DB // 2, sample)

            for half in range(2):
                evac(wsT[:, 4 * half:4 * half + 4, :], lambda p: p.rearrange("p (g i) -> p g i", g=4))
            evac(wssT, lambda p: p[0:NS, 0:256].rearrange("p (g i) -> p g i", g=AG))
            dve.wait_ge(s.v_ev, 2 * V_IT)
            for t in range(3):
                for c in range(4):
                    ins = V.bn_stats(bn[0:ROWS[t], t, c, :], v_tok[0:ROWS[t], t, c * 512:(c + 1) * 512])
            link(ins)
            for t in range(3):
                ins = V.bn_aggr(mv[0:ROWS[t], t, :], bn[0:ROWS[t], t].rearrange("p c s -> p (c s)"))
            link(ins)
            dve.sem_inc(s.rstd_sq, 1)
            dve.wait_ge(s.rstd_sq, 3)
            link(V.reciprocal(rstd[:], rstd[:]))
            dve.wait_ge(s.ln_in, 16 * (4 + DB))
            for t in range(3):
                r = ROWS[t]
                vt = v_tok[0:r, t, :]
                link(V.tensor_scalar(vt, vt, mv[0:r, t, 0:1], rstd[0:r, t:t + 1], ALU.subtract, ALU.mult))
                link(V.tensor_tensor(vt, vt, ln_g[0:r], ALU.mult))
                link(V.tensor_tensor(vt, vt, ln_b[0:r], ALU.add))
            dve.sem_inc(s.v_ready, 1)
            dve.wait_ge(s.u_ev, 2 * U_IT)
            for k in range(KT):
                dve.wait_ge(s.sp_full, k + 1)
                t_ = scr2[:, (k % 2) * TOK:(k % 2) * TOK + TOK]
                link(V.tensor_tensor(t_, ps[:, k % 2, 0:TOK], sbias[:, k // 2, :], ALU.add))
                V.tensor_tensor(uT[:, k, :], uT[:, k, :], t_, ALU.mult).then_inc(s.sp_done, 1)

            def merge(c):
                for half in range(2):
                    n = c * 2 + half
                    dve.wait_ge(s.w_used, chunk_done(n + IT_M, 1))
                    dve.wait_ge(s.m_ev_act, n + 1)
                    m2 = mT[:, ds(c * 2, 2), :]
                    if half == 0:
                        link(V.tensor_tensor(m2, ps[:, 3:5, 0:TOK], sig[:, 0], ALU.mult))
                        dve.sem_inc(s.m_ev_dve, 1)
                    else:
                        link(V.tensor_tensor(sig[:, 1], ps[:, 3:5, 0:TOK], sig[:, 1], ALU.mult))
                        link(V.tensor_tensor(m2, m2, sig[:, 1], ALU.add))
                        dve.sem_inc(s.m_ev_dve, 1)

            loop(dve, ch, M_IT, merge)

            def w_o(i):
                for b in range(2):
                    dve.wait_ge(s.w_used, chunk_done(i + IT_O, b))
                    x2_ = xt[:, 0:2, ds(i * 512 + b * 256, 256)]
                    x1_ = xt[0:NS, 2, ds(i * 512 + b * 256, 256)]
                    V.tensor_tensor(x2_, x2_, ps[:, 3 * b:3 * b + 2, 0:256], ALU.add)
                    V.tensor_tensor(x1_, x1_, ps[0:NS, 3 * b + 2, 0:256], ALU.add).then_inc(s.wo_ev, 1)

            dve.wait_ge(s.x_in, 96)
            loop(dve, ch, O_IT, w_o)
            norm(1, 4)

            dve.wait_ge(s.lg_full, 1)
            for t in range(3):
                r = ROWS[t]
                ins = V.tensor_tensor(lg[0:r, t, :], ps[0:r, 0, t * 36:(t + 1) * 36], rb[0:r], ALU.add)
            link(ins)
            link(V.tensor_copy(g8[:, :, 0:NG], lg[:, :, 0:NG]))
            for t in range(3):
                ins = V.max(mx8[:, t], g8[:, t])
            link(ins)
            for t in range(3):
                V.max_index(mi8[:, t], mx8[:, t], g8[:, t])
            link(V.tensor_scalar(rs[:, 0], mx8[:, :, 0], -1.0, None, ALU.mult))
            dve.sem_inc(s.zsq, 1)
            link(V.tensor_copy(mif[:], mi8[:]))
            link(V.tensor_copy(rs[:, 4], mif[:, :, 0]))
            link(V.tensor_tensor(goh[:], bcast(c_("iota8").unsqueeze(1), [P, 3, 8]), bcast(rs[:, 4].unsqueeze(2), [P, 3, 8]), ALU.is_equal))
            for t in range(3):
                ins = V.tensor_tensor(le4[:, t], lg[:, t, NG:].rearrange("p (g e) -> p e g", g=NG),
                                      bcast(goh[:, t, 0:NG].unsqueeze(1), [P, EPG, NG]), ALU.mult)
            link(ins)
            link(V.tensor_reduce(le[:], le4[:], AX_X, ALU.add))
            for t in range(3):
                ins = V.max(mx8[:, t], le[:, t])
            link(ins)
            for t in range(3):
                V.max_index(mi8[:, t], mx8[:, t], le[:, t])
            link(V.tensor_tensor(rs[:, 2], mx8[:, :, 1], mx8[:, :, 0], ALU.subtract))
            dve.sem_inc(s.zsq, 1)
            link(V.tensor_copy(mif[:], mi8[:]))
            for k in range(2):
                link(V.scalar_tensor_tensor(out=rs[:, 5 + k], in0=rs[:, 4], scalar=float(EPG), in1=mif[:, :, k], op0=ALU.mult, op1=ALU.add))
                link(V.tensor_tensor(oh[:, :, k], bcast(c_("iota32").unsqueeze(1), [P, 3, NE]), bcast(rs[:, 5 + k].unsqueeze(2), [P, 3, NE]), ALU.is_equal))
            V.tensor_tensor(selm[:], oh[:, :, 0], oh[:, :, 1], ALU.add).then_inc(s.rank_done, 1)
            dve.wait_ge(s.lg_done, 4)
            link(V.tensor_scalar(rs[:, 7], rs[:, 3], 1.0, None, ALU.add))
            link(V.tensor_tensor(rs[:, 7], rs[:, 7], rs[:, 1], ALU.mult))
            link(V.reciprocal(rs[:, 8], rs[:, 7]))
            link(V.tensor_tensor(rs[:, 9], rs[:, 8], rs[:, 3], ALU.mult))
            dve.wait_ge(s.rank_full, 1)
            link(V.tensor_copy(cnt[:], ps[:, 1, 96:128]))
            link(V.tensor_scalar(novf[:, 0], cnt[:], float(CAP), None, ALU.is_gt))
            for m in range(2, MAXCH):
                link(V.scalar_tensor_tensor(out=novf[:, 0], in0=cnt[:], scalar=float(CAP * m), in1=novf[:, 0], op0=ALU.is_gt, op1=ALU.add))
            link(V.tensor_copy(novf[:, 1], novf[:, 0]))
            cur = 1
            for sh in (1, 2, 4, 8, 16):
                nxt = 3 - cur
                V.tensor_copy(novf[:, nxt, 0:sh], novf[:, cur, 0:sh])
                link(V.tensor_tensor(novf[:, nxt, sh:], novf[:, cur, sh:], novf[:, cur, 0:NE - sh], ALU.add))
                cur = nxt
            incl = novf[:, cur]
            excl = novf[:, 3 - cur]
            link(V.tensor_tensor(excl, incl, novf[:, 0], ALU.subtract))
            link(V.tensor_tensor(ovf_cmp, bcast(incl.unsqueeze(1), [P, NOVF, NE]),
                                 c_("ovf_no").rearrange("p (o e) -> p o e", o=NOVF), ALU.is_le))
            link(V.tensor_reduce(ovf_ef[:, 0:NOVF], ovf_cmp, AX_X, ALU.add))
            link(V.tensor_scalar(ovf_ef[:, 0:NOVF], ovf_ef[:, 0:NOVF], float(NE - 1), None, ALU.min))
            link(V.tensor_copy(ovf_ef[:, NOVF:NOVF + 1], incl[:, NE - 1:NE]))
            link(V.tensor_copy(ovf_e[:], ovf_ef[:]))
            for t in range(3):
                ins = V.tensor_copy(posn[0:ROWS[t], t], ps[0:ROWS[t], 1, t * NE:(t + 1) * NE])
            link(ins)
            link(V.scalar_tensor_tensor(out=excl, in0=excl, scalar=float(CAP), in1=c_("base32"), op0=ALU.mult, op1=ALU.subtract))
            link(V.tensor_scalar(excl, excl, float((NE - 1) * CAP), None, ALU.add))
            link(V.tensor_scalar(posn2[:], posn[:], float(CAP), None, ALU.is_ge))
            link(V.tensor_tensor(posn2[:], posn2[:], bcast(excl.unsqueeze(1), [P, 3, NE]), ALU.mult))
            link(V.tensor_tensor(posn[:], posn[:], bcast(c_("base32").unsqueeze(1), [P, 3, NE]), ALU.add))
            link(V.tensor_tensor(posn[:], posn[:], posn2[:], ALU.add))
            for k in range(2):
                link(V.tensor_tensor(posn2[:], posn[:], oh[:, :, k], ALU.mult))
                link(V.tensor_reduce(slotf[:, :, k], posn2[:], AX_X, ALU.add))
            V.tensor_copy(sloti[:], slotf[:])
            V.tensor_copy(ids[:, :, :, 0], bcast(c_("token").unsqueeze(2), [P, 3, 2]))
            link(V.tensor_copy(ids[:, :, :, 1], c_("pair").rearrange("p (t k) -> p t k", t=3)))
            dve.sem_inc(s.slots_rdy, 1)
            dve.sem_inc(s.ids_ready, 1)

            def xgT_out(item_no, b, full, ready, used):
                dve.wait_ge(full, item_no + 1)
                if used is not None:
                    after(dve, used, item_no - 1)
                for half in range(2):
                    ins = V.tensor_tensor(xgT[b][:, 8 * half:8 * half + 8, :], ps[:, half, 0:8 * CAP].rearrange("p (k r) -> p k r", k=8),
                                          bcast(gT[:, 1, 8 * half:8 * half + 8].unsqueeze(2), [P, 8, CAP]), ALU.mult)
                ins.then_inc(ready, 1)

            dve.wait_ge(s.lg_full, 1)
            xgT_out(0, 0, s.xt_done, s.xgT_ready, None)

            def item(j):
                for b in range(2):
                    e = j * 2 + b
                    dve.wait_ge(s.hg_done, e + 1)
                    after(dve, s.ht_done, e)
                    V.tensor_tensor(hid, hgate, ps[0:CAP, 2, ED:2 * ED], ALU.mult).then_inc(s.hid_done, 1)
                    xgT_out(e + 1, 1 - b, s.xt_done, s.xgT_ready, s.gu_done)
                    dve.wait_ge(s.dn_done, e + 1)
                    after(dve, y_sems[b], j * 16)
                    V.tensor_copy(y_sb[b][:, 1024:2048].rearrange("p (n c) -> p n c", n=2), ps[0:CAP, 6:8]).then_inc(s.y_dve, 1)

            loop(dve, ch, NE // 2, item)
            n_ovf = dve.value_load(ovf_e[0:1, NOVF:NOVF + 1], min_val=0, max_val=NOVF)
            with dve.If(n_ovf > 0):
                with dve.Fori(0, n_ovf) as o:
                    xgT_out(o, 0, s.o_xt, s.o_xgT, None)
                    dve.wait_ge(s.o_hg, o + 1)
                    V.tensor_tensor(hid, hgate, ps[0:CAP, 2, ED:2 * ED], ALU.mult).then_inc(s.o_hid, 1)

            dve.wait_ge(s.yp_in, 16 * 7)
            for k in range(2):
                for t in range(3):
                    r = ROWS[t]
                    xr = xt[0:r, t, :]
                    ins = V.scalar_tensor_tensor(out=xr, in0=yp[2 * t + k][0:r], scalar=rs[0:r, 8 + k, t:t + 1], in1=xr, op0=ALU.mult, op1=ALU.add)
                    if k == 0:
                        if t == 2:
                            link(ins)
                    else:
                        ins.then_inc(s.x2_done, 1)
            dve.wait_ge(s.rstd_sq, 5)
            link(V.reciprocal(rstd[:], rstd[:]))
            for t in range(3):
                r = ROWS[t]
                V.scalar_tensor_tensor(out=fin[t][0:r], in0=xt[0:r, t, :], scalar=rstd[0:r, t:t + 1], in1=gfin[0:r], op0=ALU.mult, op1=ALU.mult).then_inc(s.fin_ready, 1)

        @block.tensor
        def _(pe):
            M = nc.tensor.matmul
            T = nc.tensor.transpose
            tp = [0]

            def group(parts):
                n = tp[0]
                if n >= 2:
                    pe.wait_ge(s.tp_free, n - 1)
                for col, src in parts:
                    rows, cols = src.shape
                    ins = T(ps[0:cols, 6 + n % 2, col:col + rows], src, ident[0:rows, 0:rows])
                ins.then_inc(s.tp_full, 1)
                tp[0] += 1

            pe.wait_ge(s.consts_in, 16)
            pe.wait_ge(s.small_in_in, 64)
            group([(0, small_in[0:KT, 0])])
            group([(0, small_in[0:KT, 1])])
            group([(0, small_in[:, 2])])
            group([(0, small_in[:, 3])])

            def norm_T(which):
                hn, base = hn_at[which], 3 * which
                for t in range(3):
                    pe.wait_ge(s.normed, base + t + 1)
                    for k4 in range(4):
                        group([(q * P, hn[t][0:ROWS[t], (4 * k4 + q) * P:(4 * k4 + q + 1) * P]) for q in range(4)])
                pe.wait_ge(s.tp_free, tp[0])

            norm_T(0)

            def weights_in(it, u):
                pe.wait_ge(w_sems[u], it * 16 + 16)

            def used(ins):
                ins.then_inc(s.w_used, 1)

            def rows_chunk(it, b, lhs):
                for half in range(2):
                    u = 2 * b + half
                    weights_in(it, u)
                    for k in range(8):
                        kk = 8 * half + k
                        for t in range(3):
                            r = ROWS[t]
                            ins = M(ps[0:r, 3 * b + t, 0:256], lhs[:, kk, t * P:t * P + r], ring[:, u, k, :],
                                    start=(kk == 0), stop=(kk == KT - 1))
                    if half == 0:
                        used(ins)
                used(ins)

            def cols_chunk(it, b, rhs):
                for half in range(2):
                    u = 2 * b + half
                    weights_in(it, u)
                    for k in range(8):
                        kk = 8 * half + k
                        for c in range(2):
                            ins = M(ps[:, 3 * b + c, 0:TOK], ring[:, u, k, c * P:(c + 1) * P], rhs[:, kk, :],
                                    start=(kk == 0), stop=(kk == KT - 1))
                    if half == 0:
                        used(ins)
                used(ins)

            def kv_(i):
                after(pe, s.kv_ev_act, i)
                rows_chunk(i, 0, hT)
                after(pe, s.kv_ev_dve, i)
                rows_chunk(i, 1, hT)

            loop(pe, None, KV_IT, kv_)
            pe.wait_ge(s.wbr_in, 16)
            for t in range(3):
                for k in range(KT):
                    ins = M(ps[0:ROWS[t], 6, t * 48:(t + 1) * 48], hT[:, k, t * P:t * P + ROWS[t]], wbr[:, k, :],
                            start=(k == 0), stop=(k == KT - 1))
            ins.then_inc(s.br_full, 1)
            pe.wait_ge(s.roped, 1)
            pe.wait_ge(s.br_done, 9)
            for br in range(2):
                for t in range(3):
                    group([(h * P, kv[0:ROWS[t], t, (2 + 2 * br) * KVC + h * HD:(2 + 2 * br) * KVC + (h + 1) * HD]) for h in range(KVH)])

            rv = rowsT.rearrange("p (n j) -> p n j", j=CB)
            for n in range(2):
                def pages(i, n=n):
                    for b in range(2):
                        k = n * PAGES + i * 2 + b
                        pe.wait_ge(page_sems[b], n * (16 * PAGES // 2) + (i * 16 + 16))
                        if n or not isinstance(i, int):
                            pe.wait_ge(s.page_ev, k - 1)
                        for h in range(KVH):
                            ins = T(ps[:, 6 + b, h * P:(h + 1) * P], page_rows[:, b, h * P:(h + 1) * P], ident)
                        ins.then_inc(s.page_T, 1)

                pe.wait_ge(s.tp_free, tp[0])
                loop(pe, None, PAGES // 2, pages)
                pe.wait_ge(s.page_ev, (n + 1) * PAGES)
                for t in range(2):
                    group([(h * P, kv[:, t, n * KVC + h * HD:n * KVC + (h + 1) * HD]) for h in range(KVH)])
                pe.wait_ge(s.tp_free, tp[0])
                pe.wait_ge((s.w1k_in, s.w1v_in)[n], 16)
                for j in range(CB):
                    ins = M(ps[:, n, 0:288], w1[:, j, :], rv[:, :, j], start=(j == 0), stop=(j == CB - 1))
                ins.then_inc(s.cmp_hid_full, 1)
                pe.wait_ge(s.cmp_hid, n + 1)
                pe.wait_ge(s.w_aux_in, 96)
                if n == 0:
                    M(ps[:, 2, 0:288], w2[:, 0], hidcT[:, 0], start=True, stop=True).then_inc(s.kc_full, 1)
                else:
                    for h in range(KVH):
                        c = (DB * KVH + h) * NCB
                        ins = M(ps[0:NCB, 3, h * HD:(h + 1) * HD], hidcT[:, 1, c:c + NCB], w2[:, 1], start=True, stop=True)
                    ins.then_inc(s.vc_full, 1)
            pe.wait_ge(s.vc_ready, 1)
            pe.wait_ge(s.kc_ready, 1)

            def q_(i):
                for b in range(2):
                    after(pe, (s.q_ev_act, s.q_ev_dve)[b], i)
                    cols_chunk(i + IT_Q, b, hT)

            loop(pe, None, Q_IT, q_)
            pe.wait_ge(s.q_ev_act, Q_IT)
            pe.wait_ge(s.q_ev_dve, Q_IT)

            def rot(i):
                after(pe, s.rot_done, i)
                for h in range(4):
                    ins = M(ps[0:RD, h, 0:TOK], c_("swap"), qT[:, ds(i * 4 + h, 1), :].rearrange("p a t -> p (a t)"), start=True, stop=True)
                ins.then_inc(s.rot_full, 1)

            loop(pe, None, 4, rot)
            pe.wait_ge(s.q_ready, 1)

            def heads(kh):
                pe.wait_ge(s.st_ready, kh + 1)

                def scores(u):
                    g, qt = u // 2, u % 2
                    n = kh * 8 + u
                    nk = P * (qt + 1)
                    after(pe, s.s_free, n - 1)
                    q_ = q_st[:, g, qt * P:(qt + 1) * P]
                    for w in range(2):
                        M(ps[:, 2 * qt + w, 0:nk], q_, kT[:, w, ds(kh, 1), 0:nk].rearrange("p a t -> p (a t)"), start=True, stop=True)
                    M(ps[:, 2 * qt, 256:264], q_, kcT[:, ds(kh * NCB + DB * KVH * NCB, NCB)], start=True, stop=True).then_inc(s.s_full, 1)

                def values(u):
                    g, qt = u // 2, u % 2
                    n = kh * 8 + u
                    b = qt
                    pe.wait_ge(s.p_ready, n + 1)
                    after(pe, s.pt_act, n)
                    after(pe, s.pt_dve, n)
                    for w in range(2):
                        for k in range(qt + 1):
                            T(ps[:, 4, w * 256 + k * P:w * 256 + (k + 1) * P], pr[:, b, w * 256 + k * P:w * 256 + (k + 1) * P], ident)
                    T(ps[0:NCB, 5, 0:P], pr[:, b, 512:520], ident).then_inc(s.pt_full, 1)
                    pe.wait_ge(s.pt_act, n + 1)
                    pe.wait_ge(s.pt_dve, n + 1)
                    after(pe, s.o_ev, n - 1)
                    first = True
                    for w in range(2):
                        for k in range(qt + 1):
                            M(ps[:, 6 + b, 0:P], v_st[:, k, w, :], pT[:, b, w * 256 + k * P:w * 256 + (k + 1) * P], start=first, stop=False)
                            first = False
                    M(ps[:, 6 + b, 0:P], vch_st, pcT[0:NCB, b, 0:P], start=False, stop=True).then_inc(s.pv_done, 1)

                scores(0)
                for u in range(8):
                    if u < 7:
                        scores(u + 1)
                    values(u)

            loop(pe, None, KVH, heads)
            pe.wait_ge(s.o_ev, 8 * KVH)

            def sample(i):
                for b in range(2):
                    n = i * 2 + b
                    pe.wait_ge(kvx_sems[b], i * 96 + 96)
                    for h in range(KVH):
                        if h < 2:
                            after(pe, (s.kx_ev_a, s.kx_ev_d)[h], n * 2)
                        else:
                            pe.wait_ge((s.kx_ev_a, s.kx_ev_d)[h - 2], n * 2 + 1)
                        for t in range(4):
                            ins = T(ps[:, 6 + h % 2, t * P:(t + 1) * P], kx[:, b, t, h * HD:(h + 1) * HD], ident)
                        ins.then_inc(s.kxT_full, 1)
                    pe.wait_ge(s.qp_ready, n + 1)
                    for h in range(KVH):
                        M(ps[0:NCB, 5, h * HD:(h + 1) * HD], hidc_st[:, h * NCB:(h + 1) * NCB], w2[:, 1], start=True, stop=True)
                    pe.wait_ge(s.kx_ev_a, n * 2 + 2)
                    pe.wait_ge(s.kx_ev_d, n * 2 + 2)
                    for w in range(2):
                        for h in range(KVH):
                            M(ps[0:64, w, 0:256], qpad[:, h * 64:(h + 1) * 64], kxT[:, h, w * 256:(w + 1) * 256], start=(h == 0), stop=(h == KVH - 1))
                        for h in range(KVH):
                            ins = M(ps[0:64, w, 256:288], qpad[:, h * 64:(h + 1) * 64], kT[:, w, h, SEQ:TOK], start=(h == 0), stop=(h == KVH - 1))
                    for h in range(KVH):
                        ins = M(ps[0:64, 0, 288:296], qpad[:, h * 64:(h + 1) * 64], kcT[:, ds(n * (KVH * NCB) + h * NCB, NCB)], start=(h == 0), stop=(h == KVH - 1))
                    ins.then_inc(s.t_full, 1)
                    apart(pe, s.tp_ready, n + 1, s.pe_passed)
                    for w in range(2):
                        for k in range(2):
                            T(ps[:, 2, (2 * w + k) * 64:(2 * w + k + 1) * 64], pr[0:64, 0, w * 288 + k * P:w * 288 + (k + 1) * P], ident[0:64, 0:64])
                        T(ps[0:NS, 3, w * 64:(w + 1) * 64], pr[0:64, 0, w * 288 + 256:w * 288 + 288], ident[0:64, 0:64])
                    T(ps[0:NCB, 3, 128:192], pr[0:64, 0, 576:584], ident[0:64, 0:64]).then_inc(s.tpt_full, 1)
                    pe.wait_ge(s.tpt_act, n + 1)
                    pe.wait_ge(s.tpt_dve, n + 1)
                    after(pe, s.to_ev, n)
                    for h in range(KVH):
                        out = ps[:, 4, h * 16:(h + 1) * 16]
                        for w in range(2):
                            for k in range(2):
                                c = (2 * w + k) * 64 + h * 16
                                M(out, vx[:, b, 2 * w + k, h * HD:(h + 1) * HD], pT[:, 0, c:c + 16], start=(w == 0 and k == 0), stop=False)
                            c = (3 + 2 * w) * KVC + h * HD
                            M(out, kv[0:NS, 2, c:c + HD], pcT[0:NS, 0, w * 64 + h * 16:w * 64 + h * 16 + 16], start=False, stop=False)
                        ins = M(out, vcs_st[:, h * HD:(h + 1) * HD], pcT[0:NCB, 0, 128 + h * 16:128 + h * 16 + 16], start=False, stop=True)
                    ins.then_inc(s.tpv_done, 1)

            loop(pe, None, DB // 2, sample)
            pe.wait_ge(s.to_ev, DB)

            def v_(i):
                for b in range(2):
                    if not (isinstance(i, int)):
                        pe.wait_ge(s.v_ev, i * 2 + (b - 1))
                    rows_chunk(i + IT_V, b, hT)

            loop(pe, None, V_IT, v_)
            pe.wait_ge(s.ws_masked, 2)
            for half in range(2):
                group([(q * P, ws_raw[:, 4 * half + q, :]) for q in range(4)])
            group([(g * NS, wss_raw[:, g, :]) for g in range(AG)])
            pe.wait_ge(s.v_ev, 2 * V_IT)

            def u_(i):
                for b in range(2):
                    if not (isinstance(i, int)):
                        pe.wait_ge(s.u_ev, i * 2 + (b - 1))
                    cols_chunk(i + IT_U, b, hT)

            loop(pe, None, U_IT, u_)
            pe.wait_ge(s.u_ev, 2 * U_IT)
            pe.wait_ge(s.v_ready, 1)
            pe.wait_ge(s.tp_free, tp[0])
            for k in range(KT):
                after(pe, s.sp_done, k - 1)
                g = k // 2
                for t in range(2):
                    M(ps[:, k % 2, t * P:(t + 1) * P], v_tok[:, t, k * P:(k + 1) * P], wsT[:, g, :], start=True, stop=True)
                M(ps[:, k % 2, SEQ:TOK], v_tok[0:NS, 2, k * P:(k + 1) * P], wssT[:, g, :], start=True, stop=True).then_inc(s.sp_full, 1)
            pe.wait_ge(s.sp_done, KT)

            def merge(c):
                for half in range(2):
                    n = c * 2 + half
                    it = n + IT_M
                    after(pe, s.m_ev_act, n)
                    cols_chunk(it, 0, hT)
                    after(pe, s.m_ev_dve, n)
                    cols_chunk(it, 1, (uT, qT)[half])

            loop(pe, None, M_IT, merge)
            pe.wait_ge(s.m_ev_act, 2 * M_IT)
            pe.wait_ge(s.m_ev_dve, 2 * M_IT)

            def w_o(i):
                for b in range(2):
                    if not isinstance(i, int):
                        pe.wait_ge(s.wo_ev, i * 2 + (b - 1))
                    rows_chunk(i + IT_O, b, mT)

            loop(pe, None, O_IT, w_o)
            norm_T(1)
            pe.wait_ge(s.wo_ev, 2 * O_IT)
            for t in range(3):
                for k in range(KT):
                    ins = M(ps[0:ROWS[t], 0, t * 36:(t + 1) * 36], hT[:, k, t * P:t * P + ROWS[t]], wr[:, k, :],
                            start=(k == 0), stop=(k == KT - 1))
            ins.then_inc(s.lg_full, 1)
            pe.wait_ge(s.rank_done, 1)
            for t in range(3):
                r = ROWS[t]
                for j in range(t):
                    M(ps[0:r, 1, t * NE:(t + 1) * NE], c_("ones")[:, 0:r], selm[:, j], start=(j == 0), stop=False)
                M(ps[0:r, 1, t * NE:(t + 1) * NE], c_("before", r)[:, 0:r], selm[0:r, t], start=(t == 0), stop=True)
            for t in range(3):
                r = ROWS[t]
                ins = M(ps[:, 1, 96:128], c_("ones", r), selm[0:r, t], start=(t == 0), stop=(t == 2))
            ins.then_inc(s.rank_full, 1)
            pe.wait_ge(s.ids_ready, 1)

            def rows_T(b, done):
                for k in range(KT):
                    ins = T(ps[:, k // 8, (k % 8) * CAP:(k % 8 + 1) * CAP], xg[b][:, k * P:(k + 1) * P], ident[0:CAP, 0:CAP])
                ins.then_inc(done, 1)

            def gate_up(b, done):
                for k in range(KT):
                    ins = M(ps[0:CAP, 2], xgT[b][:, k, :], wgu[b][:, k, :], start=(k == 0), stop=(k == KT - 1))
                ins.then_inc(done, 1)

            def hid_T(done):
                for f in range(2):
                    ins = T(ps[:, 3, f * CAP:(f + 1) * CAP], hid[:, f * P:(f + 1) * P], ident[0:CAP, 0:CAP])
                ins.then_inc(done, 1)

            def down(b, done):
                for f in range(2):
                    for n in range(4):
                        ins = M(ps[0:CAP, 4 + n], hidT[:, f, :], wdn[b][:, f, n * 512:(n + 1) * 512], start=(f == 0), stop=(f == 1))
                ins.then_inc(done, 1)

            pe.wait_ge(xg_sems[0], 16)
            rows_T(0, s.xt_done)

            def item(j):
                for b in range(2):
                    e = j * 2 + b
                    pe.wait_ge(wgu_sems[b], j * 32 + 32)
                    pe.wait_ge(s.xgT_ready, e + 1)
                    after(pe, s.hid_done, e)
                    gate_up(b, s.gu_done)
                    apart(pe, xg_sems[1 - b], (j + b) * 16 + 16, s.pe_passed)
                    rows_T(1 - b, s.xt_done)
                    after(pe, s.hidT_ready, e)
                    apart(pe, s.hid_done, e + 1, s.pe_passed)
                    hid_T(s.ht_done)
                    pe.wait_ge(wdn_sems[b], j * 16 + 16)
                    pe.wait_ge(s.hidT_ready, e + 1)
                    after(pe, s.y_act, e)
                    after(pe, s.y_dve, e)
                    down(b, s.dn_done)

            loop(pe, None, NE // 2, item)
            n_ovf = pe.value_load(ovf_e[0:1, NOVF:NOVF + 1], min_val=0, max_val=NOVF)
            with pe.If(n_ovf > 0):
                pe.wait_ge(s.xgT_ready, NE + 1)
                pe.wait_ge(s.y_act, NE)
                pe.wait_ge(s.y_dve, NE)
                pe.sem_inc(s.o_free, 1)
                with pe.Fori(0, n_ovf) as o:
                    apart(pe, s.o_xg, o * 16 + 16, s.pe_passed)
                    rows_T(0, s.o_xt)
                    pe.wait_ge(s.o_xgT, o + 1)
                    pe.wait_ge(s.o_w, o * 48 + 48)
                    gate_up(0, s.o_gu)
                    apart(pe, s.o_hid, o + 1, s.pe_passed)
                    hid_T(s.o_ht)
                    pe.wait_ge(s.o_hidT, o + 1)
                    down(0, s.o_dn)
                    pe.wait_ge(s.o_ya, o + 1)
                    pe.sem_inc(s.o_free, 1)


_INS = ['x_prompt', 'x_sample', 'cache_k_cmp', 'cache_v_cmp', 'cache_k_slc', 'cache_v_slc', 'state_k_win', 'state_v_win',
        'page_table', 'g_mix', 'w_in', 'a_ln_g', 'a_ln_b', 'a_w_s', 'a_b_s', 'cmp_pe_k', 'cmp_w1_k', 'cmp_w2_k',
        'cmp_pe_v', 'cmp_w1_v', 'cmp_w2_v', 'w_pa', 'w_pb', 'w_o', 'g_ffn', 'w_rg', 'b_rg', 'w_re', 'b_re',
        'w_gate', 'w_up', 'w_down', 'g_final']
_ROW = (KVH, HD)
_OUTS = ([(1, SEQ, D), (DB, DT, D)] + [(1, 1, SEQ) + _ROW] * 6 + [(1, DB, DT) + _ROW] * 4
         + [(1, DB, PAST) + _ROW] * 2 + [(1, DB, DT, D)])


def kernel(**inputs):
    import concourse.bacc as _bacc
    from concourse.bass_utils import run_bass_kernel_spmd as _run

    nc = _bacc.Bacc("TRN2", target_bir_lowering=False, num_devices=1)
    arrays, aps = {}, {}
    named = [(n, np.ascontiguousarray(inputs[n])) for n in _INS] + [("consts", constants())]
    for name, x in named:
        arrays[f"in_{name}"] = x
        aps[name] = nc.dram_tensor(f"in_{name}", x.shape, mybir.dt.from_np(x.dtype), kind="ExternalInput").ap()
    outs = [nc.dram_tensor(f"out_{i}", shape, F32, kind="ExternalOutput").ap() for i, shape in enumerate(_OUTS)]
    build(nc, aps, outs)
    r = _run(nc, [arrays], core_ids=[0])
    return tuple(r.results[0][f"out_{i}"] for i in range(len(_OUTS)))
```

```python
from contextlib import ExitStack

import numpy as np

import concourse.bass as bass
from concourse import mybir

F32 = mybir.dt.float32
F32R = mybir.dt.float32r
I32 = mybir.dt.int32
U32 = mybir.dt.uint32
ALU = mybir.AluOpType
ACT = mybir.ActivationFunctionType
AX_X = mybir.AxisListType.X
ds = bass.ds

P = 128
D = 2048
KT = D // P
SEQ, DB, DT = 256, 8, 4
NS = DB * DT
TOK = SEQ + NS
ROWS = (P, P, NS)
NH, KVH, GQ, HD = 16, 4, 4, 128
RD, HALF = 32, 16
PAST = 256
PAGES = DB * PAST // P
CB = 32
NSEQ = DB + 1
NCB = PAST // CB
SCALE = float(HD) ** -0.5
EPS = 1e-6
NEG = -1e30
AG = 8
NG, EPG = 4, 8
NE = NG * EPG
ED = 256
CAP = 64
MAXCH = -(-TOK // CAP)
NOVF = 2 * TOK // CAP
NITEM = NE + NOVF
NOWHERE = 1 << 20
C_U, C_V, C_Q, C_KV = 0, D, 2 * D, 3 * D
C_BR = C_KV + 6 * KVH * HD
C_GA = C_BR + 3 * NH
C_GB = C_GA + D
KVC = KVH * HD

CONSTS = {}
CW = 0
for _n, _w in (("ident", P), ("before", P), ("ones", P), ("pmask", 2 * P), ("cmask", 2 * NCB), ("anyvalid", 3),
               ("smask", DB * NS), ("cosT", TOK), ("sinT", TOK), ("swap", RD), ("cos", 3 * HALF), ("sin", 3 * HALF),
               ("iota32", NE), ("base32", NE), ("iota8", 8), ("ovf_no", NOVF * NE), ("token", 3), ("pair", 6)):
    CONSTS[_n] = (CW, _w)
    CW += _w


def constants():
    f = np.float32
    c = np.zeros((P, CW), f)

    def put(name, a):
        o, w = CONSTS[name]
        a = np.asarray(a, f).reshape(a.shape[0], -1)
        c[:a.shape[0], o:o + w] = a

    r = np.arange(P)
    put("ident", np.eye(P))
    put("before", (r[:, None] < r[None, :]))
    put("ones", np.ones((P, P)))
    put("pmask", np.concatenate([np.zeros((P, P)), np.where(r[None, :] <= r[:, None], 0, NEG)], 1))
    ends = (np.arange(NCB) + 1) * CB - 1
    put("cmask", np.stack([np.where((ends[None] <= (r + q * P)[:, None]) | ((r + q * P) < CB - 1)[:, None], 0, NEG)
                           for q in range(2)], 1))
    av = np.ones((P, 3))
    av[:CB - 1, 0] = 0
    put("anyvalid", av)
    row_t = np.arange(NH * DT) % DT
    k = np.arange(NS)
    put("smask", np.where((k // DT)[None, None] == np.arange(DB)[None, :, None],
                          np.where((k % DT)[None, None] <= row_t[:, None, None], 0, NEG), NEG))
    inv = np.power(f(500000.0), -np.arange(0, RD, 2, dtype=f) / f(RD))
    pos = np.concatenate([np.arange(SEQ), PAST + np.arange(NS) % DT]).astype(f)
    ang = (pos[:, None] * inv[None]).astype(f)
    cos, sin = np.cos(ang), np.sin(ang)
    put("cosT", np.concatenate([cos, cos], 1).T)
    put("sinT", np.concatenate([-sin, sin], 1).T)
    put("swap", np.roll(np.eye(RD), HALF, 1))
    tiles = np.zeros((2, P, 3, HALF))
    for t in range(3):
        tiles[0, :ROWS[t], t] = cos[t * P:t * P + ROWS[t]]
        tiles[1, :ROWS[t], t] = sin[t * P:t * P + ROWS[t]]
    put("cos", tiles[0])
    put("sin", tiles[1])
    put("iota32", np.tile(np.arange(NE), (P, 1)))
    put("base32", np.tile(np.arange(NE) * CAP, (P, 1)))
    put("iota8", np.tile(np.arange(8), (P, 1)))
    put("ovf_no", np.tile(np.repeat(np.arange(NOVF), NE), (P, 1)))
    tok = r[:, None] + P * np.arange(3)[None]
    put("token", tok)
    put("pair", tok[:, :, None] + TOK * np.arange(2)[None, None])
    return c


def bcast(ap, shape):
    return ap.broadcast_to(shape)


class Chain:

    def __init__(self, eng, sem):
        self.eng, self.sem, self.n, self.lead = eng, sem, 0, None

    def value(self):
        return self.n if self.lead is None else self.lead + self.n

    def link(self, ins):
        ins.then_inc(self.sem, 1)
        self.n += 1
        self.eng.wait_ge(self.sem, self.value())


def apart(eng, sem, value, passed):
    if not (isinstance(value, int) and value <= 0):
        eng.wait_ge(sem, value)
        eng.sem_inc(passed, 1)


def loop(eng, chain, count, body, last=False):
    start = chain.n if chain else 0
    body(0)
    if chain:
        per = chain.n - start
        chain.n = start
    with eng.Fori(1, count - last) as i:
        if chain and per:
            chain.lead = i * per
        body(i)
    if chain:
        assert chain.n == start + per
        chain.lead = None
        chain.n = start + per * (count - last)
    if last:
        body(count - 1)


def after(eng, sem, value):
    if not (isinstance(value, int) and value <= 0):
        eng.wait_ge(sem, value)


def before(e, q):
    n = e * 6 + (4 + q)
    return n - 4 if isinstance(e, int) and e == NE - 1 else n


def build(nc, a, outs, cap_debug=None):
    (y_prompt, y_sample, o_kcp, o_vcp, o_ksp, o_vsp, o_kwp, o_vwp,
     o_kcs, o_vcs, o_kss, o_vss, o_kws, o_vws, o_vchunk) = outs
    with ExitStack() as ctx:
        def sb(name, shape, dt=F32):
            return ctx.enter_context(nc.sbuf_tensor(name, shape, dt))

        def sem(name):
            return ctx.enter_context(nc.semaphore(name))

        gate_d = nc.dram_tensor("gate_d", (NS, 3 * NH), F32, kind="Internal").ap()
        h2_d = nc.dram_tensor("h2_d", (TOK, D), F32, kind="Internal").ap()
        slot_d = nc.dram_tensor("slot_d", (NITEM * CAP, 2), I32, kind="Internal").ap()
        ypair_d = nc.dram_tensor("ypair_d", (2 * TOK, D), F32, kind="Internal").ap()

        H0, Q0 = 0, KT * TOK
        U0 = Q0 + KT * TOK
        K0 = U0 + 3 * D + KT * TOK
        W0 = K0 + 3 * 6 * KVC
        END = W0 + 4 * 8 * 256 + 1024
        base = -(-nc.sbuf_base // 32) * 32
        mem = sb("mem", [P, END])

        def rounded(name, shape, col):
            return nc.alloc_sbuf_tensor_at(name, shape, F32R, offset=base + 4 * col)

        hT = mem[:, H0:Q0].rearrange("p (k t) -> p k t", k=KT)
        qT = mem[:, Q0:Q0 + KT * TOK].rearrange("p (k t) -> p k t", k=KT)
        v_tok = mem[:, U0:U0 + 3 * D].rearrange("p (t c) -> p t c", t=3)
        uT = mem[:, U0 + 3 * D:K0].rearrange("p (k t) -> p k t", k=KT)
        kv = mem[:, K0:W0].rearrange("p (t c) -> p t c", t=3)
        ring = mem[:, W0:W0 + 4 * 8 * 256].rearrange("p (s k c) -> p s k c", s=4, k=8)
        rowsT = mem[:, U0:U0 + 18 * 512]
        w1 = mem[:, Q0:Q0 + CB * P].rearrange("p (j e) -> p j e", j=CB)
        kx = mem[:, U0:U0 + 2 * 2048].rearrange("p (b t c) -> p b t c", b=2, t=4)
        vx = mem[:, U0 + 4096:U0 + 8192].rearrange("p (b t c) -> p b t c", b=2, t=4)
        kxT = mem[:, U0 + 8192:U0 + 8192 + 2048].rearrange("p (h c) -> p h c", h=KVH)
        mT = mem[:, K0:K0 + KT * TOK].rearrange("p (k t) -> p k t", k=KT)
        ln_g = mem[:, K0:K0 + D]
        ln_b = mem[:, K0 + D:K0 + 2 * D]
        ws_raw = mem[:, K0 + 4096:K0 + 5120].rearrange("p (g j) -> p g j", g=AG)
        wsT = mem[:, K0 + 5120:K0 + 6144].rearrange("p (g j) -> p g j", g=AG)
        sbias = mem[:, K0 + 6144:K0 + 6144 + AG * TOK].rearrange("p (g t) -> p g t", g=AG)
        wss_raw = mem[0:NS, K0 + 8448:K0 + 8704].rearrange("p (g j) -> p g j", g=AG)
        wssT = mem[0:NS, K0 + 8704:K0 + 8960].rearrange("p (g j) -> p g j", g=AG)
        PIECE = 4 * 2 * ED
        staging = [mem[:, Q0 + PIECE * q:Q0 + PIECE * (q + 1)] for q in range(6)]
        X0 = Q0 + 6 * PIECE
        xg = mem[0:CAP, X0:X0 + D]
        g_ffn = mem[:, X0:X0 + D]
        SP0 = K0
        split = [rounded(f"split{n}", [P, 2, PIECE], SP0 + 2 * PIECE * n) for n in range(4)]
        y_sb = mem[0:CAP, SP0 + 8 * PIECE:SP0 + 8 * PIECE + D]
        assert X0 + D <= SP0 and SP0 + 8 * PIECE + D <= END
        XGW = KT * CAP + P - CAP
        xgT = [rounded(f"xgT{b}", [P, 2, XGW], H0 + 2 * XGW * b) for b in range(2)]
        yp = [mem[:, D * b:D * (b + 1)] for b in range(6)]
        gfin = mem[:, 6 * D:7 * D]
        fin = [mem[:, (7 + b) * D:(8 + b) * D] for b in range(3)]

        xt = sb("xt", [P, 3, D])
        cst = sb("cst", [P, CW])
        gT = sb("gT", [P, KT])
        small_in = sb("small_in", [CB, 3, P])
        peT = sb("peT", [P, 2, CB])
        w2 = sb("w2", [P, 2, P])
        kT = sb("kT", [P, 2, KVH, TOK])
        hidcT = sb("hidcT", [P, 2, NSEQ * KVH * NCB])
        kcT = sb("kcT", [P, NSEQ * KVH * NCB])
        ptab = sb("ptab", [1, PAGES], I32)
        ss = sb("ss", [P, 3])
        rstd = sb("rstd", [P, 3])
        epsb = sb("epsb", [P, 1])
        gbr = sb("gbr", [P, 3, NH, 3])
        gsm = sb("gsm", [NH * DT, DB, 3])
        att = xt[:].rearrange("p t d -> p (t d)")
        page_rows = att[:, 0:1024].rearrange("p (b c) -> p b c", b=2)
        rtmp = att[:, 1024:1024 + 48 * HALF].rearrange("p (k c) -> p k c", k=4)
        q_st = att[:, 0:1024].rearrange("p (g t) -> p g t", g=GQ)
        v_st = att[:, 1024:1536].rearrange("p (t r d) -> p t r d", t=2, r=2)
        vc_st = att[0:NCB, 1536:2048]
        PR = 6 * P + 2 * NCB
        pr = att[:, 2048:2048 + 2 * PR].rearrange("p (b c) -> p b c", b=2)
        pT = att[:, 3616:3616 + 6 * P]
        pcT = att[0:NCB, 4384:4384 + 2 * P]
        tpr = att[0:NH * DT, 2048:2048 + 584]
        tpT = att[:, 3616:3616 + 256]
        tpcT = att[0:NS, 4384:4384 + 192]
        o_st = att[0:NH * DT, 1024:1024 + KVC]
        qpad = att[:, 4640:4640 + 320]
        vcs_st = att[0:NCB, 0:2 * KVC].rearrange("p (b c) -> p b c", b=2)
        vch_st = att[0:NCB, 5504:5504 + HD]
        hidc_st = att[:, 5472:5472 + KVH * NCB]
        scr2 = att[:, D:D + 1152]
        squares_at = [mem[:, K0:K0 + D], mem[:, W0 + 3 * D:W0 + 4 * D], mem[:, 10 * D:11 * D]]
        hn_at = [[mem[:, o + D * t:o + D * (t + 1)] for t in range(3)] for o in (U0, W0)]
        stt = sb("stt", [P, 2, 24])
        bn = sb("bn", [P, 3, 4, 6])
        mv = sb("mv", [P, 3, 2])
        hgate = kT[:].rearrange("p b h t -> p (b h t)")[0:CAP, KT * CAP:KT * CAP + ED]
        hid = kT[:].rearrange("p b h t -> p (b h t)")[0:CAP, KT * CAP + ED:KT * CAP + 2 * ED]
        hidT = sb("hidT", [P, 2, 2 * CAP + P - CAP], F32R)
        sig = kT[:].rearrange("p b h t -> p (b h t)")[:, 0:4 * TOK].rearrange("p (a c t) -> p a c t", a=2, c=2)
        wbr = att[:, 4096:4096 + KT * 48].rearrange("p (k c) -> p k c", k=KT)
        wr = sb("wr", [P, KT, NG + NE])
        rb = sb("rb", [P, NG + NE])
        lg = sb("lg", [P, 3, NG + NE])
        g8 = sb("g8", [P, 3, 8])
        mx8 = sb("mx8", [P, 3, 8])
        mi8 = sb("mi8", [P, 3, 8], U32)
        mif = sb("mif", [P, 3, 8])
        goh = sb("goh", [P, 3, 8])
        le4 = kT[:].rearrange("p b h t -> p (b h t)")[:, 1152:1248].rearrange("p (t i g) -> p t i g", t=3, i=EPG)
        le = sb("le", [P, 3, 8])
        rs = sb("rs", [P, 12, 3])
        oh = kT[:].rearrange("p b h t -> p (b h t)")[:, 1248:1440].rearrange("p (t k e) -> p t k e", t=3, k=2)
        selm = sb("selm", [P, 3, NE])
        cnt = sb("cnt", [P, NE])
        novf = kT[:].rearrange("p b h t -> p (b h t)")[:, 1536:1632].rearrange("p (t e) -> p t e", t=3)
        posn = sb("posn", [P, 3, NE])
        posn2 = kT[:].rearrange("p b h t -> p (b h t)")[:, 1440:1536].rearrange("p (t e) -> p t e", t=3)
        slotf = sb("slotf", [P, 3, 2])
        sloti = sb("sloti", [P, 3, 2], I32)
        ids = sb("ids", [P, 3, 2, 2], I32)
        ovf_cmp = kT[:].rearrange("p b h t -> p (b h t)")[:, 0:NOVF * NE].rearrange("p (o e) -> p o e", o=NOVF)
        ovf_ef = sb("ovf_ef", [P, NOVF + 1])
        ovf_e = sb("ovf_e", [P, NOVF + 1], I32)
        slots = sb("slots", [CAP, NITEM, 2], I32)
        idx_in = sb("idx_in", [CAP, 1], I32)
        idx_out = sb("idx_out", [CAP, 1], I32)

        def c_(name, rows=P):
            o, w = CONSTS[name]
            return cst[0:rows, o:o + w]

        ident = c_("ident")
        ps = ctx.enter_context(nc.psum_tensor("ps", [P, 8, 512], F32))

        def score_parts(b):
            for c, (w, at, wide) in enumerate(((0, 0, P), (1, 0, P), (0, 1, 2 * P), (1, 1, 2 * P), (0, 0, NCB), (1, 0, NCB))):
                src = (2 * P if c >= 4 else 0) + w * wide
                dst = (0, 2 * P, 6 * P)[c // 2] + w * wide
                yield ps[:, 2 * b + at, src:src + wide], pr[:, b, dst:dst + wide], c

        def kv_heads(eng, chain, heads):
            def body(kh):
                heads(kh, isinstance(kh, int) and kh == KVH - 1)

            loop(eng, chain, KVH, body, last=True)

        S = {}
        for n in ("x_in consts_in small_in_in w_aux_in w1k_in w1v_in wbr_in br_in rows_out ln_in ws_in wss_in ptab_in "
                  "page_in0 page_in1 kx_in0 kx_in1 vx_in0 vx_in1 gate_out gate_in h2_out slot_fill_out slot_out slots_in yp_in "
                  "stores_a stores_g stores_s "
                  "w_in0 w_in1 w_in2 w_in3 w_used "
                  "act_chain dve_chain pe_passed dve_passed pool_passed sp_passed "
                  "squares rstd_sq normed tp_full tp_free "
                  "kv_ev_act kv_ev_dve br_full br_done gates_done roped kT_ready "
                  "page_T page_ev cmp_hid_full cmp_hid kc_full kc_ready vc_full vc_ready "
                  "q_ev_act q_ev_dve rot_full rot_done q_ready "
                  "q_staged v_staged s_full sc_ready p_exp p_ready pt_full pt_act pt_dve pv_done o_ev "
                  "kx_ev vcs_full vcs_ev o_rows oT_full qp_ready t_full t_free tsc_ready tp_exp tp_ready tpt_full tpt_act tpt_dve tpv_done to_ev "
                  "pool_init v_ev v_ready u_ev sp_full sp_done "
                  "ws_masked m_ev_act m_ev_dve wo_ev zsq lg_full lg_done rank_full rank_done "
                  "ids_ready slots_rdy xg_in xt_done xgh_done xgT_ready hg_done hid_done ht_done hidTh_done hidT_ready "
                  "y_act y_dve y_out piece_in0 piece_in1 piece_in2 piece_in3 piece_in4 piece_in5 hi_done lo_done piece_used "
                  "idx_ready out_idx_ready g_ffn_in o_idx o_xg o_w o_xt o_xgh o_xgT o_hg o_hid o_ht o_hidTh o_hidT o_hi o_lo o_used o_ya o_free o_yout "
                  "x2_done fin_sq fin_ready init_done dve_init kxT_full").split():
            S[n] = sem(n)
        s = type("Sems", (), S)

        w_view = a["w_in"].rearrange("l (k p) c -> p (l k) c", p=P)
        block = ctx.enter_context(nc.Block())

        N_STORES_KV = 6 + 4 + 2 * DB
        N_STORES_A = N_STORES_KV + 1
        KV_IT, Q_IT, V_IT, U_IT, M_IT, O_IT = 6, 4, 4, 4, 8, 4
        IT_Q = KV_IT
        IT_V = IT_Q + Q_IT
        IT_U = IT_V + V_IT
        IT_M = IT_U + U_IT
        IT_O = IT_M + 2 * M_IT
        IT_END = IT_O + O_IT

        def chunk_done(it, b):
            return it * 4 + (2 * b + 2)

        w_sems = [s.w_in0, s.w_in1, s.w_in2, s.w_in3]
        piece_sems = [s.piece_in0, s.piece_in1, s.piece_in2, s.piece_in3, s.piece_in4, s.piece_in5]
        page_sems = [s.page_in0, s.page_in1]
        kx_sems, vx_sems = [s.kx_in0, s.kx_in1], [s.vx_in0, s.vx_in1]

        @block.sync
        def _(sp):
            def load_x():
                for t in range(2):
                    sp.dma_start(xt[:, t, :], a["x_prompt"][0, t * P:(t + 1) * P, :]).then_inc(s.x_in, 16)
                sp.dma_start(xt[0:NS, 2, :], a["x_sample"].rearrange("b t d -> (b t) d")).then_inc(s.x_in, 16)

            load_x()

            def load(it, u, src, col):
                if not isinstance(it, int) or it > 0:
                    apart(sp, s.w_used, it * 4 + (u - 3), s.sp_passed)
                h = u % 2
                sp.dma_start(ring[:, u], src[:, 8 * h:8 * h + 8, ds(col, 256)]).then_inc(w_sems[u], 16)

            def stream(first, count, src, col0):
                def body(it):
                    for u in range(4):
                        load(it, u, src, (it - first) * 512 + (col0 + 256 * (u // 2)))
                if first == 0:
                    body(0)
                with sp.Fori(max(first, 1), first + count) as it:
                    body(it)

            wv = {n: a[n].rearrange("l (k p) c -> p (l k) c", p=P) for n in ("w_pa", "w_pb", "w_o")}
            stream(0, KV_IT, w_view, C_KV)
            stream(IT_Q, Q_IT, w_view, C_Q)
            stream(IT_V, V_IT, w_view, C_V)
            stream(IT_U, U_IT, w_view, C_U)
            with sp.Fori(0, M_IT) as c:
                for half, (g_col, w_p) in enumerate(((C_GA, "w_pa"), (C_GB, "w_pb"))):
                    it = c * 2 + (IT_M + half)
                    for u in range(2):
                        load(it, u, w_view, c * 256 + g_col)
                    for u in range(2, 4):
                        load(it, u, wv[w_p], c * 256)
            sp.wait_ge(s.sp_done, KT)
            load_x()
            stream(IT_O, O_IT, wv["w_o"], 0)

            wg = a["w_gate"].rearrange("l e (k p) f -> p (l e) k f", p=P)
            wu = a["w_up"].rearrange("l e (k p) f -> p (l e) k f", p=P)
            wd = a["w_down"].rearrange("l e (f p) d -> p (l e) f d", p=P)

            def load_piece(e, q, done):
                if q < 4:
                    st = staging[q].rearrange("p (k c) -> p k c", k=4)
                    for c, view in enumerate((wg, wu)):
                        sp.dma_start(st[:, :, c * ED:(c + 1) * ED],
                                     view[:, ds(e, 1), 4 * q:4 * q + 4].rearrange("p a k f -> p (a k) f")).then_inc(done, 16)
                else:
                    sp.dma_start(staging[q], wd[:, ds(e, 1), q - 4].rearrange("p a f -> p (a f)")).then_inc(done, 16)

            sp.wait_ge(s.m_ev_dve, 2 * M_IT)
            sp.wait_ge(s.stores_a, 16 * N_STORES_A)

            sp.dma_start(g_ffn, a["g_ffn"][0].partition_broadcast(P)).then_inc(s.g_ffn_in, 16)
            for q in range(4):
                load_piece(0, q, piece_sems[q])

            def experts(j):
                for b in range(2):
                    e = j * 2 + b
                    for q in range(6):
                        last = isinstance(e, int) and e == NE - 1
                        if q < 4 and last:
                            continue
                        if isinstance(e, int) and e == 0:
                            if q < 4:
                                apart(sp, s.lo_done, q + 1, s.sp_passed)
                        else:
                            apart(sp, s.lo_done, before(e - 1, q) + 1, s.sp_passed)
                        load_piece(e + (1 if q < 4 else 0), q, piece_sems[q])

            loop(sp, None, NE // 2, experts, last=True)

            sp.wait_ge(s.slots_rdy, 1)
            n_ovf = sp.value_load(ovf_e[0:1, NOVF:NOVF + 1], min_val=0, max_val=NOVF)
            with sp.If(n_ovf > 0):
                with sp.Fori(0, n_ovf) as o:
                    apart(sp, s.o_free, o + 1, s.sp_passed)
                    e = sp.value_load(ovf_e[0:1, ds(o, 1)], min_val=0, max_val=NE - 1)
                    for q in range(6):
                        load_piece(e, q, s.o_w)

            sp.wait_ge(s.pool_init, 3)
            for k in range(2):
                for t in range(3):
                    r = ROWS[t]
                    sp.dma_start(yp[2 * t + k][0:r], ypair_d[k * TOK + t * P:k * TOK + t * P + r, :]).then_inc(s.yp_in, 16)
            sp.dma_start(gfin, a["g_final"].partition_broadcast(P)).then_inc(s.yp_in, 16)
            for t in range(3):
                sp.wait_ge(s.fin_ready, t + 1)
                dst = y_prompt[0, t * P:(t + 1) * P, :] if t < 2 else y_sample.rearrange("b t d -> (b t) d")
                sp.dma_start(dst, fin[t][0:ROWS[t]]).then_inc(s.stores_s, 16)
            sp.wait_ge(s.stores_s, 48)
            sp.wait_ge(s.stores_a, 16 * N_STORES_A)
            sp.wait_ge(s.stores_g, 32)

        @block.gpsimd
        def _(pool):
            nc.gpsimd.memset(slots[:], NOWHERE).then_inc(s.init_done, 1)
            pool.dma_start(ptab[:], a["page_table"].rearrange("b n -> (b n)").rearrange("(o n) -> o n", o=1)).then_inc(s.ptab_in, 16)
            pool.wait_ge(s.init_done, 1)
            pool.dma_start(slot_d.rearrange("(c i) k -> c i k", c=CAP), slots[:]).then_inc(s.slot_fill_out, 16)
            for src, dst in ((a["state_k_win"], o_kws), (a["state_v_win"], o_vws)):
                pool.dma_start(dst[0, :, 0:PAST - DT], src[0, :, DT:PAST]).then_inc(s.stores_g, 16)
            pool.wait_ge(s.ptab_in, 16)

            pool.wait_ge(s.normed, 3)
            for n, cache in enumerate(("cache_k_cmp", "cache_v_cmp")):
                rows = a[cache].rearrange("l n t h d -> t (l n) (h d)")

                def pages(i, n=n, rows=rows):
                    for b in range(2):
                        k = n * PAGES + i * 2 + b
                        if n or not isinstance(i, int):
                            apart(pool, s.page_T, k - 1, s.pool_passed)
                        page = pool.value_load(ptab[0:1, ds(i * 2 + b, 1)], min_val=0, max_val=a[cache].shape[1] - 1)
                        pool.dma_start(page_rows[:, b], rows[:, ds(page, 1)].rearrange("p a c -> p (a c)")).then_inc(page_sems[b], 16)

                loop(pool, None, PAGES // 2, pages)

            ks = a["cache_k_slc"].rearrange("l n t h d -> t (l n) (h d)")
            vs = a["cache_v_slc"].rearrange("l n t h d -> t (l n) (h d)")
            kw = a["state_k_win"].rearrange("l b (u t) h d -> t (l b) u (h d)", t=P)
            vw = a["state_v_win"].rearrange("l b (u t) h d -> t (l b) u (h d)", t=P)
            pool.wait_ge(s.cmp_hid, 2)

            def sequences(i):
                for b in range(2):
                    n = i * 2 + b
                    pages = [pool.value_load(ptab[0:1, ds(i * 4 + (2 * b + u), 1)], min_val=0, max_val=a["cache_k_slc"].shape[1] - 1)
                             for u in range(2)]
                    apart(pool, s.kxT_full, i * 8 + 4 * (b - 1), s.pool_passed)
                    for u in range(2):
                        pool.dma_start(kx[:, b, u], ks[:, ds(pages[u], 1)].rearrange("p a c -> p (a c)")).then_inc(kx_sems[b], 16)
                    pool.dma_start(kx[:, b, 2:4], kw[:, ds(n, 1)].rearrange("p a u c -> p (a u) c")).then_inc(kx_sems[b], 16)
                    apart(pool, s.tpv_done, i * 2 + (b - 1), s.pool_passed)
                    for u in range(2):
                        pool.dma_start(vx[:, b, u], vs[:, ds(pages[u], 1)].rearrange("p a c -> p (a c)")).then_inc(vx_sems[b], 16)
                    pool.dma_start(vx[:, b, 2:4], vw[:, ds(n, 1)].rearrange("p a u c -> p (a u) c")).then_inc(vx_sems[b], 16)

            loop(pool, None, DB // 2, sequences)

            pool.wait_ge(s.tpv_done, DB)
            pool.wait_ge(s.stores_a, 16 * N_STORES_KV)
            nc.gpsimd.memset(wss_raw, 0.0).then_inc(s.pool_init, 1)
            pool.dma_start(ws_raw, a["a_w_s"][0].rearrange("g i j -> i g j")).then_inc(s.ws_in, 16)
            pool.wait_ge(s.pool_init, 1)
            for b in range(DB):
                r = slice(DT * b, DT * b + DT)
                pool.dma_start(wss_raw[r, :, r], a["a_w_s"][0, :, 0:DT, 0:DT].rearrange("g i j -> i g j")).then_inc(s.ws_in, 16)
            for t in range(2):
                pool.dma_start(sbias[:, :, t * P:(t + 1) * P], a["a_b_s"][0].partition_broadcast(P)).then_inc(s.ln_in, 16)
            for b in range(DB):
                pool.dma_start(sbias[:, :, SEQ + DT * b:SEQ + DT * b + DT], a["a_b_s"][0, :, 0:DT].partition_broadcast(P)).then_inc(s.ln_in, 16)
            pool.dma_start(ln_g, a["a_ln_g"][0].partition_broadcast(P)).then_inc(s.ln_in, 16)
            pool.dma_start(ln_b, a["a_ln_b"][0].partition_broadcast(P)).then_inc(s.ln_in, 16)
            pool.wait_ge(s.ws_in, 16 * (1 + DB))
            nc.gpsimd.affine_select(out=ws_raw, in_=ws_raw, compare_op=ALU.is_ge, fill=0.0, base=0,
                                    pattern=[[0, AG], [-1, P]], channel_multiplier=1).then_inc(s.ws_masked, 1)
            nc.gpsimd.affine_select(out=wss_raw, in_=wss_raw, compare_op=ALU.is_ge, fill=0.0, base=0,
                                    pattern=[[0, AG], [-1, NS]], channel_multiplier=1).then_inc(s.ws_masked, 1)

            pool.wait_ge(s.normed, 6)
            nc.gpsimd.memset(xg, 0.0).then_inc(s.pool_init, 1)
            pool.wait_ge(s.ids_ready, 1)
            pool.wait_ge(s.slot_fill_out, 16)
            for t in range(3):
                for k in range(2):
                    pool.indirect_dma_start(out=slot_d, out_offset=bass.IndirectOffsetOnAxis(ap=sloti[0:ROWS[t], t, k:k + 1], axis=0),
                                            in_=ids[0:ROWS[t], t, k, :], in_offset=None).then_inc(s.slot_out, 16)
            pool.wait_ge(s.slot_out, 96)
            pool.dma_start(slots[:], slot_d.rearrange("(i c) k -> c i k", c=CAP)).then_inc(s.slots_in, 16)
            pool.wait_ge(s.slots_in, 16)
            pool.wait_ge(s.h2_out, 48)
            pool.wait_ge(s.pool_init, 2)

            def fetch(item, copied, n, arrived):
                nc.gpsimd.tensor_copy(idx_in[:], slots[:, ds(item, 1), 0:1].rearrange("p a k -> p (a k)")).then_inc(copied, 1)
                apart(pool, copied, n, s.pool_passed)
                pool.indirect_dma_start(out=xg, out_offset=None, in_=h2_d,
                                        in_offset=bass.IndirectOffsetOnAxis(ap=idx_in[:, 0:1], axis=0),
                                        bounds_check=TOK - 1, oob_is_err=False).then_inc(arrived, 16)

            def scatter(item, copied, n, done):
                nc.gpsimd.tensor_copy(idx_out[:], slots[:, ds(item, 1), 1:2].rearrange("p a k -> p (a k)")).then_inc(copied, 1)
                apart(pool, copied, n, s.pool_passed)
                pool.indirect_dma_start(out=ypair_d, out_offset=bass.IndirectOffsetOnAxis(ap=idx_out[:, 0:1], axis=0),
                                        in_=y_sb, in_offset=None,
                                        bounds_check=2 * TOK - 1, oob_is_err=False).then_inc(done, 16)

            fetch(0, s.idx_ready, 1, s.xg_in)
            pool.wait_ge(s.xg_in, 16)
            pool.wait_ge(s.xt_done, 1)
            fetch(1, s.idx_ready, 2, s.xg_in)

            def items(j):
                for b in range(2):
                    e = j * 2 + b
                    if not (isinstance(e, int) and e >= NE - 2):
                        apart(pool, s.xg_in, (e + 2) * 16, s.pool_passed)
                        apart(pool, s.xt_done, e + 2, s.pool_passed)
                        fetch(e + 2, s.idx_ready, e + 3, s.xg_in)
                    if not (isinstance(e, int) and e == 0):
                        y_rows_out(e - 1)

            def y_rows_out(e):
                apart(pool, s.y_out, e * 16, s.pool_passed)
                apart(pool, s.y_act, e + 1, s.pool_passed)
                apart(pool, s.y_dve, e + 1, s.pool_passed)
                scatter(e, s.out_idx_ready, e + 1, s.y_out)

            loop(pool, None, NE // 2, items, last=True)
            y_rows_out(NE - 1)
            pool.wait_ge(s.y_out, 16 * NE)

            n_ovf = pool.value_load(ovf_e[0:1, NOVF:NOVF + 1], min_val=0, max_val=NOVF)
            with pool.If(n_ovf > 0):
                with pool.Fori(0, n_ovf) as o:
                    fetch(o + NE, s.o_idx, o * 2 + 1, s.o_xg)
                    apart(pool, s.o_ya, o + 1, s.pool_passed)
                    scatter(o + NE, s.o_idx, o * 2 + 2, s.o_yout)
                    apart(pool, s.o_yout, (o + 1) * 16, s.pool_passed)
            pool.sem_inc(s.pool_init, 1)

        @block.scalar
        def _(act):
            ch = Chain(act, s.act_chain)
            A = nc.scalar.activation
            act.dma_start(cst[:], a["consts"]).then_inc(s.consts_in, 16)
            act.dma_start(small_in[0:KT, 0], a["g_mix"][0].rearrange("(k p) -> k p", p=P)).then_inc(s.small_in_in, 16)
            act.dma_start(small_in[:, 1], a["cmp_pe_k"][0]).then_inc(s.small_in_in, 16)
            act.dma_start(small_in[:, 2], a["cmp_pe_v"][0]).then_inc(s.small_in_in, 16)
            act.dma_start(w2[:, 0], a["cmp_w2_k"][0]).then_inc(s.w_aux_in, 16)
            act.dma_start(w2[:, 1], a["cmp_w2_v"][0]).then_inc(s.w_aux_in, 16)
            act.dma_start(wr[:, :, 0:NG], a["w_rg"][0].rearrange("(k p) g -> p k g", p=P)).then_inc(s.w_aux_in, 16)
            act.dma_start(wr[:, :, NG:], a["w_re"][0].rearrange("(k p) g -> p k g", p=P)).then_inc(s.w_aux_in, 16)
            act.dma_start(rb[:, 0:NG], a["b_rg"][0].partition_broadcast(P)).then_inc(s.w_aux_in, 16)
            act.dma_start(rb[:, NG:], a["b_re"][0].partition_broadcast(P)).then_inc(s.w_aux_in, 16)
            act.dma_start(w1, a["cmp_w1_k"][0].rearrange("j d e -> d j e")).then_inc(s.w1k_in, 16)

            def sum_squares(which, t, wait_sem, value):
                if wait_sem is not None:
                    act.wait_ge(wait_sem, value)
                after(act, s.squares, 3 * which + t)
                A(squares_at[which][0:ROWS[t]], xt[0:ROWS[t], t, :], ACT.Square, accum_out=ss[0:ROWS[t], t:t + 1]).then_inc(s.squares, 1)

            act.wait_ge(s.x_in, 48)
            act.wait_ge(s.dve_init, 1)
            for t in range(3):
                sum_squares(0, t, None, 0)
            act.wait_ge(s.squares, 3)
            A(rstd[:], ss[:], ACT.Sqrt, bias=epsb[:, 0:1], scale=1.0 / D).then_inc(s.rstd_sq, 1)

            act.wait_ge(s.normed, 3)
            act.dma_start(wbr, w_view[:, :, C_BR:C_BR + 48]).then_inc(s.wbr_in, 16)

            def kv_even(i):
                act.wait_ge(s.w_used, chunk_done(i, 0))
                nc.scalar.copy(kv[:, 0:2, ds(i * 512, 256)], ps[:, 0:2, 0:256])
                nc.scalar.copy(kv[0:NS, 2, ds(i * 512, 256)], ps[0:NS, 2, 0:256]).then_inc(s.kv_ev_act, 1)

            loop(act, None, KV_IT, kv_even)
            act.wait_ge(s.br_full, 1)
            act.wait_ge(s.dve_init, 2)
            for t in range(3):
                r = ROWS[t]
                for c, src in enumerate((1, 2, 0)):
                    A(gbr[0:r, t, :, c], ps[0:r, 6, t * 48:(t + 1) * 48].rearrange("p (h c) -> p h c", c=3)[:, :, src], ACT.Sigmoid).then_inc(s.br_done, 1)
            act.wait_ge(s.roped, 1)
            for br, (op, os) in enumerate(((o_kcp, o_kcs), (o_vcp, o_vcs), (o_ksp, o_kss), (o_vsp, o_vss), (o_kwp, None), (o_vwp, None))):
                act.dma_start(op[0, 0].rearrange("(t p) h d -> p t (h d)", p=P), kv[:, 0:2, br * KVC:(br + 1) * KVC]).then_inc(s.stores_a, 16)
                if os is not None:
                    act.dma_start(os[0].rearrange("b t h d -> (b t) (h d)"), kv[0:NS, 2, br * KVC:(br + 1) * KVC]).then_inc(s.stores_a, 16)
                else:
                    dst = (o_kws, o_vws)[br - 4]
                    for b in range(DB):
                        act.dma_start(dst[0, b, PAST - DT:PAST].rearrange("t h d -> t (h d)"),
                                      kv[b * DT:(b + 1) * DT, 2, br * KVC:(br + 1) * KVC]).then_inc(s.stores_a, 16)
            act.wait_ge(s.gates_done, 1)
            act.dma_start(gate_d, gbr[0:NS, 2].rearrange("p h c -> p (h c)")).then_inc(s.gate_out, 16)
            act.wait_ge(s.gate_out, 16)
            for h in range(NH):
                act.dma_start(gsm[h * DT:(h + 1) * DT], gate_d.rearrange("(b t) (h c) -> t b h c", t=DT, c=3)[:, :, h, :]).then_inc(s.gate_in, 16)

            for n in range(2):
                act.wait_ge(s.cmp_hid_full, n + 1)
                if n == 0:
                    act.dma_start(w1, a["cmp_w1_v"][0].rearrange("j d e -> d j e")).then_inc(s.w1v_in, 16)
                src = ps[:, n, 0:288].rearrange("p (s g h k) -> p s g h k", s=NSEQ, g=2, h=KVH)
                dst = hidcT[:, n].rearrange("p (s h g k) -> p s g h k", s=NSEQ, g=2, h=KVH)
                A(dst[:, :, 0], src[:, :, 0], ACT.Gelu_apprx_tanh)
                A(dst[:, :, 1], src[:, :, 1], ACT.Gelu_apprx_tanh).then_inc(s.cmp_hid, 1)

            def q_even(i):
                act.wait_ge(s.w_used, chunk_done(i + IT_Q, 0))
                nc.scalar.copy(qT[:, ds(i * 4, 2), :], ps[:, 0:2, 0:TOK]).then_inc(s.q_ev_act, 1)

            loop(act, None, Q_IT, q_even)

            def exps(n, b):
                act.wait_ge(s.sc_ready, n + 1)
                after(act, s.pt_full, n - 1)
                for in_, out, c in score_parts(b):
                    ins = A(out, in_, ACT.Exp, scale=SCALE, bias=stt[:, b, 6 + c:7 + c], accum_out=stt[:, b, 12 + c:13 + c])
                ins.then_inc(s.p_exp, 1)

            def heads(kh, last):
                for g in range(GQ):
                    n = kh * GQ + g
                    if not (last and g == GQ - 1):
                        exps(n + 1, (g + 1) % 2)
                    act.wait_ge(s.pt_full, n + 1)
                    after(act, s.pv_done, n)
                    nc.scalar.copy(pT[:, 0:4 * P], ps[:, 4]).then_inc(s.pt_act, 1)

            exps(0, 0)
            kv_heads(act, None, heads)

            def keys_left(n, h):
                act.wait_ge(s.kxT_full, n * 4 + (h + 1))
                nc.scalar.copy(kxT[:, h], ps[:, 6 + h % 2]).then_inc(s.kx_ev, 1)

            for h in range(KVH):
                keys_left(0, h)

            def sample(i):
                for b in range(2):
                    n = i * 2 + b
                    more = not (isinstance(n, int) and n == DB - 1)
                    act.wait_ge(s.t_full, n + 1)
                    if more:
                        for h in range(3):
                            keys_left(n + 1, h)
                    act.wait_ge(s.tsc_ready, n + 1)
                    after(act, s.tpt_full, n)
                    st = stt[0:64, 0]
                    for c, (in_, out) in enumerate(((ps[0:64, 0, 0:288], tpr[:, 0:288]), (ps[0:64, 1, 0:288], tpr[:, 288:576]),
                                                    (ps[0:64, 0, 288:296], tpr[:, 576:584]))):
                        ins = A(out, in_, ACT.Exp, scale=SCALE, bias=st[:, 3 + c:4 + c], accum_out=st[:, 6 + c:7 + c])
                    ins.then_inc(s.tp_exp, 1)
                    if more:
                        keys_left(n + 1, 3)
                    act.wait_ge(s.tpt_full, n + 1)
                    after(act, s.tpv_done, n)
                    nc.scalar.copy(tpT, ps[:, 2, 0:256]).then_inc(s.tpt_act, 1)

            loop(act, None, DB // 2, sample, last=True)

            def v_act(i):
                for b in range(2):
                    act.wait_ge(s.w_used, chunk_done(i + IT_V, b))
                    A(v_tok[:, 0:2, ds(i * 512 + b * 256, 256)], ps[:, 3 * b:3 * b + 2, 0:256], ACT.Gelu_apprx_tanh)
                    A(v_tok[0:NS, 2, ds(i * 512 + b * 256, 256)], ps[0:NS, 3 * b + 2, 0:256], ACT.Gelu_apprx_tanh).then_inc(s.v_ev, 1)

            loop(act, None, V_IT, v_act)
            act.wait_ge(s.rstd_sq, 2)
            A(rstd[:], mv[:, :, 1], ACT.Sqrt, bias=epsb[:, 0:1]).then_inc(s.rstd_sq, 1)
            act.wait_ge(s.v_ready, 1)
            act.dma_start(o_vchunk[0].rearrange("b t c -> (b t) c"), v_tok[0:NS, 2, :]).then_inc(s.stores_a, 16)

            def u_act(i):
                for b in range(2):
                    act.wait_ge(s.w_used, chunk_done(i + IT_U, b))
                    A(uT[:, ds(i * 4 + 2 * b, 2), :], ps[:, 3 * b:3 * b + 2, 0:TOK], ACT.Gelu_apprx_tanh).then_inc(s.u_ev, 1)

            loop(act, None, U_IT, u_act)

            def m_act(c):
                for half in range(2):
                    n = c * 2 + half
                    act.wait_ge(s.w_used, chunk_done(n + IT_M, 0))
                    after(act, s.m_ev_dve, n - 1)
                    A(sig[:, half], ps[:, 0:2, 0:TOK], ACT.Sigmoid).then_inc(s.m_ev_act, 1)

            loop(act, None, M_IT, m_act)

            for t in range(3):
                sum_squares(1, t, s.wo_ev, 2 * O_IT)
            act.wait_ge(s.squares, 6)
            A(rstd[:], ss[:], ACT.Sqrt, bias=epsb[:, 0:1], scale=1.0 / D).then_inc(s.rstd_sq, 1)
            for t in range(3):
                act.wait_ge(s.normed, 3 + t + 1)
                act.dma_start(h2_d[t * P:t * P + ROWS[t], :], hn_at[1][t][0:ROWS[t]]).then_inc(s.h2_out, 16)
            act.wait_ge(s.zsq, 1)
            for t in range(3):
                A(g8[:, t, 0:NG], lg[:, t, 0:NG], ACT.Exp, bias=rs[:, 0, t:t + 1], accum_out=rs[:, 1, t:t + 1]).then_inc(s.lg_done, 1)
            act.wait_ge(s.zsq, 2)
            A(rs[:, 3], rs[:, 2], ACT.Exp).then_inc(s.lg_done, 1)

            def round_weights(slot, q, arrived, n, done):
                act.wait_ge(arrived, n)
                nc.scalar.copy(split[slot][:, 0], staging[q]).then_inc(done, 1)

            def piece_hi(e, b, q):
                if q > 5:
                    e, b, q = e + 1, 1 - b, q - 6
                if isinstance(e, int) and (e == NE or (e == NE - 1 and q < 4)):
                    return
                n = before(e, q)
                act.wait_ge(s.piece_used, n - 3)
                round_weights((6 * b + q) % 4, q, piece_sems[q], (e + 2) * 32 if q < 4 else (e + 1) * 16, s.hi_done)

            def rows_hi(b, full, n, done):
                act.wait_ge(full, n)
                nc.scalar.copy(xgT[b][:, 0, 0:KT * CAP].rearrange("p (n c) -> p n c", n=2), ps[:, 0:2, 0:8 * CAP]).then_inc(done, 1)

            def hidT_hi(bank, full, n, done):
                act.wait_ge(full, n)
                nc.scalar.copy(hidT[:, 0, 0:2 * CAP], ps[:, bank, 0:2 * CAP]).then_inc(done, 1)

            def y_left(e):
                act.wait_ge(s.piece_used, before(e, 5) + 1)
                after(act, s.y_out, e * 16)
                nc.scalar.copy(y_sb[:, 0:1024].rearrange("p (n c) -> p n c", n=2), ps[0:CAP, 4:6]).then_inc(s.y_act, 1)

            act.wait_ge(s.w_used, 4 * IT_END)
            round_weights(0, 0, piece_sems[0], 32, s.hi_done)
            round_weights(1, 1, piece_sems[1], 32, s.hi_done)
            act.wait_ge(s.h2_out, 48)
            act.wait_ge(s.lg_full, 1)
            round_weights(2, 2, piece_sems[2], 32, s.hi_done)
            round_weights(3, 3, piece_sems[3], 32, s.hi_done)
            rows_hi(0, s.xt_done, 1, s.xgh_done)
            piece_hi(0, 0, 0)
            piece_hi(0, 0, 1)
            rows_hi(1, s.xt_done, 2, s.xgh_done)

            def item(j):
                for b in range(2):
                    e = j * 2 + b
                    first = isinstance(e, int) and e == 0
                    act.wait_ge(s.piece_used, 4 if first else e * 6 + 2)
                    after(act, s.hid_done, e)
                    A(hgate, ps[0:CAP, 2 + b, 0:ED], ACT.Silu).then_inc(s.hg_done, 1)
                    piece_hi(e, b, 2)
                    piece_hi(e, b, 3)
                    if not first:
                        y_left(e - 1)
                    piece_hi(e, b, 4)
                    piece_hi(e, b, 5)
                    piece_hi(e, b, 6)
                    after(act, s.piece_used, e * 6)
                    hidT_hi(2 + b, s.ht_done, e + 1, s.hidTh_done)
                    if not (isinstance(e, int) and e >= NE - 2):
                        rows_hi(b, s.xt_done, e + 3, s.xgh_done)
                    piece_hi(e, b, 7)

            loop(act, None, NE // 2, item, last=True)
            y_left(NE - 1)
            n_ovf = act.value_load(ovf_e[0:1, NOVF:NOVF + 1], min_val=0, max_val=NOVF)
            with act.If(n_ovf > 0):
                with act.Fori(0, n_ovf) as o:
                    rows_hi(0, s.o_xt, o + 1, s.o_xgh)
                    for q in range(6):
                        if q >= 4:
                            act.wait_ge(s.o_used, o * 6 + (q - 3))
                        round_weights(q % 4, q, s.o_w, (o + 1) * 160, s.o_hi)
                    act.wait_ge(s.o_used, o * 6 + 4)
                    A(hgate, ps[0:CAP, 2, 0:ED], ACT.Silu).then_inc(s.o_hg, 1)
                    hidT_hi(2, s.o_ht, o + 1, s.o_hidTh)
                    act.wait_ge(s.o_used, o * 6 + 6)
                    nc.scalar.copy(y_sb.rearrange("p (n c) -> p n c", n=4), ps[0:CAP, 4:8]).then_inc(s.o_ya, 1)
            for t in range(3):
                act.wait_ge(s.x2_done, t + 1)
                sum_squares(2, t, None, 0)
            act.wait_ge(s.squares, 9)
            A(rstd[:], ss[:], ACT.Sqrt, bias=epsb[:, 0:1], scale=1.0 / D).then_inc(s.rstd_sq, 1)

        @block.vector
        def _(dve):
            ch = Chain(dve, s.dve_chain)
            V = nc.vector
            link = ch.link
            V.memset(epsb[:], EPS)
            V.memset(ss[:], 1.0).then_inc(s.dve_init, 1)
            V.memset(gbr[:], 0.0).then_inc(s.dve_init, 1)
            V.memset(lg[:], 0.0)
            V.memset(mv[:], 1.0)
            V.memset(posn[:], 0.0)
            link(V.memset(g8[:], NEG))
            tp = [0]

            def evac(out, in_, gain=None):
                dve.wait_ge(s.tp_full, tp[0] + 1)
                bank = 6 + tp[0] % 2
                src = in_(ps[:, bank])
                if gain is None:
                    V.tensor_copy(out, src).then_inc(s.tp_free, 1)
                else:
                    V.tensor_tensor(out, src, gain, ALU.mult).then_inc(s.tp_free, 1)
                tp[0] += 1

            evac(gT[:], lambda p: p[:, 0:KT])
            evac(peT[:, 0], lambda p: p[:, 0:CB])
            evac(peT[:, 1], lambda p: p[:, 0:CB])

            def norm(which, sq_value):
                hn = hn_at[which]
                if which == 1:
                    dve.wait_ge(s.g_ffn_in, 16)
                dve.wait_ge(s.rstd_sq, sq_value)
                link(V.reciprocal(rstd[:], rstd[:]))
                for t in range(3):
                    r = ROWS[t]
                    if which == 0:
                        V.tensor_scalar(hn[t][0:r], xt[0:r, t, :], rstd[0:r, t:t + 1], None, ALU.mult).then_inc(s.normed, 1)
                    else:
                        V.scalar_tensor_tensor(out=hn[t][0:r], in0=xt[0:r, t, :], scalar=rstd[0:r, t:t + 1], in1=g_ffn[0:r],
                                               op0=ALU.mult, op1=ALU.mult).then_inc(s.normed, 1)
                for t in range(3):
                    r = ROWS[t]
                    for k4 in range(4):
                        if tp[0] == 3:
                            dve.wait_ge(s.tp_free, 3)
                        evac(hT[:, 4 * k4:4 * k4 + 4, t * P:t * P + r],
                             lambda p, r=r: p.rearrange("p (k t) -> p k t", k=4)[:, :, 0:r],
                             bcast(gT[:, 4 * k4:4 * k4 + 4].unsqueeze(2), [P, 4, r]) if which == 0 else None)

            norm(0, 1)

            def kv_odd(i):
                dve.wait_ge(s.w_used, chunk_done(i, 1))
                V.tensor_copy(kv[:, 0:2, ds(i * 512 + 256, 256)], ps[:, 3:5, 0:256])
                V.tensor_copy(kv[0:NS, 2, ds(i * 512 + 256, 256)], ps[0:NS, 5, 0:256]).then_inc(s.kv_ev_dve, 1)

            loop(dve, ch, KV_IT, kv_odd)
            dve.wait_ge(s.kv_ev_act, KV_IT)
            dve.wait_ge(s.kv_ev_dve, KV_IT)
            for t in range(3):
                r = ROWS[t]
                keys = kv[0:r, t].rearrange("p (b x h d) -> p b x h d", b=3, x=2, h=KVH)[:, :, 0]
                x1, x2 = keys[:, :, :, 0:HALF], keys[:, :, :, HALF:RD]
                co = bcast(c_("cos", r)[:, t * HALF:(t + 1) * HALF].unsqueeze(1).unsqueeze(1), [r, 3, KVH, HALF])
                si = bcast(c_("sin", r)[:, t * HALF:(t + 1) * HALF].unsqueeze(1).unsqueeze(1), [r, 3, KVH, HALF])
                tm = [rtmp[0:r, k].rearrange("p (b h d) -> p b h d", b=3, h=KVH) for k in range(4)]
                V.tensor_tensor(tm[0], x1, co, ALU.mult)
                V.tensor_tensor(tm[1], x2, si, ALU.mult)
                V.tensor_tensor(tm[2], x2, co, ALU.mult)
                link(V.tensor_tensor(tm[3], x1, si, ALU.mult))
                V.tensor_tensor(x1, tm[0], tm[1], ALU.subtract)
                ins = V.tensor_tensor(x2, tm[2], tm[3], ALU.add)
                link(ins)
            link(V.memset(stt[:], 0.0))
            dve.sem_inc(s.roped, 1)
            dve.wait_ge(s.br_done, 9)
            link(V.tensor_tensor(gbr[:, :, :, 2], gbr[:, :, :, 2], bcast(c_("anyvalid").unsqueeze(2), [P, 3, NH]), ALU.mult))
            dve.sem_inc(s.gates_done, 1)

            for br in range(2):
                for t in range(3):
                    r = ROWS[t]
                    evac(kT[:, br, :, t * P:t * P + r], lambda p, r=r: p.rearrange("p (k t) -> p k t", k=4)[:, :, 0:r])
            dve.wait_ge(s.tp_free, tp[0])
            dve.sem_inc(s.kT_ready, 1)

            for n in range(2):
                if n == 1:
                    dve.wait_ge(s.cmp_hid_full, 1)
                pe_b = bcast(peT[:, n].unsqueeze(1), [P, 16, CB])

                def pages(i, n=n, pe_b=pe_b):
                    for b in range(2):
                        dve.wait_ge(s.page_T, n * PAGES + (i * 2 + (b + 1)))
                        V.tensor_tensor(rowsT[:, ds(i * 1024 + b * 512, 512)].rearrange("p (a j) -> p a j", j=CB),
                                        ps[:, 6 + b].rearrange("p (a j) -> p a j", j=CB), pe_b, ALU.add).then_inc(s.page_ev, 1)

                loop(dve, ch, PAGES // 2, pages)
                for t in range(2):
                    dve.wait_ge(s.tp_full, tp[0] + 1)
                    V.tensor_tensor(rowsT[:, (16 + t) * 512:(17 + t) * 512].rearrange("p (a j) -> p a j", j=CB),
                                    ps[:, 6 + tp[0] % 2].rearrange("p (a j) -> p a j", j=CB), pe_b, ALU.add).then_inc(s.tp_free, 1)
                    tp[0] += 1
                if n == 0:
                    dve.wait_ge(s.kc_full, 1)
                    V.tensor_copy(kcT[:], ps[:, 2, 0:288]).then_inc(s.kc_ready, 1)
                else:
                    dve.wait_ge(s.vc_full, 1)
                    V.tensor_copy(vc_st, ps[0:NCB, 3]).then_inc(s.vc_ready, 1)

            def q_odd(i):
                dve.wait_ge(s.w_used, chunk_done(i + IT_Q, 1))
                V.tensor_copy(qT[:, ds(i * 4 + 2, 2), :], ps[:, 3:5, 0:TOK]).then_inc(s.q_ev_dve, 1)

            loop(dve, ch, Q_IT, q_odd)
            dve.wait_ge(s.q_ev_act, Q_IT)
            dve.wait_ge(s.q_ev_dve, Q_IT)
            cosb = bcast(c_("cosT", RD).unsqueeze(1), [RD, 4, TOK])
            sinb = bcast(c_("sinT", RD).unsqueeze(1), [RD, 4, TOK])

            def rope_q(i):
                dve.wait_ge(s.rot_full, i + 1)
                q4 = qT[0:RD, ds(i * 4, 4), :]
                part = scr2[0:RD].rearrange("p (h t) -> p h t", h=4)
                V.tensor_tensor(q4, q4, cosb, ALU.mult)
                link(V.tensor_tensor(part, ps[0:RD, 0:4, 0:TOK], sinb, ALU.mult))
                dve.sem_inc(s.rot_done, 1)
                link(V.tensor_tensor(q4, q4, part, ALU.add))

            loop(dve, ch, 4, rope_q)
            dve.sem_inc(s.q_ready, 1)
            dve.wait_ge(s.vc_ready, 1)
            dve.wait_ge(s.kc_ready, 1)

            def maxima(n, b):
                dve.wait_ge(s.s_full, n + 1)
                st = stt[:, b]
                lo, hi = ps[:, 2 * b], ps[:, 2 * b + 1]
                V.tensor_reduce(st[:, 2:4], hi.rearrange("p (w k) -> p w k", w=2), AX_X, ALU.max)
                V.tensor_reduce(st[:, 0:2], lo[:, 0:2 * P].rearrange("p (w k) -> p w k", w=2), AX_X, ALU.max)
                link(V.tensor_reduce(st[:, 4:6], lo[:, 2 * P:2 * P + 2 * NCB].rearrange("p (q k) -> p q k", q=2), AX_X, ALU.max))
                V.tensor_scalar(st[:, 6:12], st[:, 0:6], -SCALE, None, ALU.mult).then_inc(s.sc_ready, 1)

            def weigh(n, b):
                dve.wait_ge(s.p_exp, n + 1)
                st = stt[:, b]
                link(V.reciprocal(st[:, 18:24], st[:, 12:18]))
                gate = gbr[:, 0:2, ds(n, 1), :].rearrange("p q a c -> p q (a c)")
                V.tensor_tensor(st[:, 0:4].rearrange("p (q w) -> p q w", q=2), st[:, 18:22].rearrange("p (q w) -> p q w", q=2), gate[:, :, 0:2], ALU.mult)
                link(V.tensor_tensor(st[:, 4:6].unsqueeze(2), st[:, 22:24].unsqueeze(2), gate[:, :, 2:3], ALU.mult))
                for c, m, k in ((0, 2, P), (2, 2, 2 * P), (4, 2, NCB)):
                    part = pr[:, b, (0, 2 * P, 6 * P)[c // 2]:][:, 0:m * k].rearrange("p (w k) -> p w k", w=m)
                    ins = V.tensor_tensor(part, part, bcast(st[:, c:c + 2].unsqueeze(2), [P, m, k]), ALU.mult)
                ins.then_inc(s.p_ready, 1)

            def leave(n, b):
                apart(dve, s.pv_done, n + 1, s.dve_passed)
                V.tensor_copy(qT[:, ds(n, 1), 0:SEQ].rearrange("p a t -> p (a t)"), ps[:, 6 + b, 0:SEQ]).then_inc(s.o_ev, 1)

            def stage_q(kh):
                V.tensor_copy(q_st, qT[:, ds(kh * GQ, GQ), 0:SEQ]).then_inc(s.q_staged, 1)

            def stage_v(kh):
                V.tensor_copy(vch_st, vc_st[:, ds(kh * HD, HD)])
                for c, br in enumerate((3, 5)):
                    ins = V.tensor_copy(v_st[:, :, c], kv[:, 0:2, ds(kh * HD + br * KVC, HD)])
                ins.then_inc(s.v_staged, 1)

            def heads(kh, last):
                for g in range(GQ):
                    n = kh * GQ + g
                    b = g % 2
                    weigh(n, b)
                    if not (last and g == GQ - 1):
                        maxima(n + 1, 1 - b)
                    if g == GQ - 2 and not last:
                        stage_q(kh + 1)
                    if not (isinstance(n, int) and n == 0):
                        leave(n - 1, 1 - b)
                        if g == 0:
                            stage_v(kh)
                    dve.wait_ge(s.pt_full, n + 1)
                    after(dve, s.pv_done, n)
                    V.tensor_copy(pT[:, 4 * P:6 * P], ps[:, 5, 0:2 * P])
                    V.tensor_copy(pcT, ps[0:NCB, 5, 2 * P:4 * P]).then_inc(s.pt_dve, 1)

            stage_q(0)
            maxima(0, 0)
            stage_v(0)
            kv_heads(dve, ch, heads)
            leave(NH - 1, 1)

            dve.wait_ge(s.o_ev, NH)
            dve.wait_ge(s.gate_in, 16 * NH)
            link(V.memset(qpad, 0.0))
            qpv = qpad.rearrange("p (h r) -> p h r", h=KVH)[:, :, 0:16].rearrange("p h (g t) -> p h g t", g=GQ)

            def stage_sample(n):
                for h in range(KVH):
                    V.tensor_copy(qpv[:, h], qT[:, 4 * h:4 * h + 4, ds(n * DT + SEQ, DT)])
                V.tensor_copy(hidc_st, hidcT[:, 1, ds(n * (KVH * NCB), KVH * NCB)]).then_inc(s.qp_ready, 1)

            def cmp_values_left(n, b):
                dve.wait_ge(s.vcs_full, n + 1)
                V.tensor_copy(vcs_st[:, b], ps[0:NCB, 5]).then_inc(s.vcs_ev, 1)

            def rows_left(n):
                dve.wait_ge(s.tpv_done, n + 1)
                after(dve, s.oT_full, n)
                V.tensor_copy(o_st, ps[0:NH * DT, 4]).then_inc(s.o_rows, 1)

            def out_left(n):
                apart(dve, s.oT_full, n + 1, s.dve_passed)
                own = ps[:, 4, 0:KVH * 80].rearrange("p (h c) -> p h c", h=KVH)[:, :, 0:16].rearrange("p h (g t) -> p h g t", g=GQ)
                V.tensor_copy(qT[:, :, ds(n * DT + SEQ, DT)].rearrange("p (h g) t -> p h g t", h=KVH), own).then_inc(s.to_ev, 1)

            stage_sample(0)
            cmp_values_left(0, 0)

            def sample(i):
                for b in range(2):
                    n = i * 2 + b
                    more = not (isinstance(n, int) and n == DB - 1)
                    st = stt[0:64, 0]
                    dve.wait_ge(s.t_full, n + 1)
                    V.tensor_reduce(st[:, 0:2], ps[0:64, 0:2, 0:288], AX_X, ALU.max)
                    link(V.tensor_reduce(st[:, 2:3], ps[0:64, 0, 288:296], AX_X, ALU.max))
                    V.tensor_scalar(st[:, 3:6], st[:, 0:3], -SCALE, None, ALU.mult).then_inc(s.tsc_ready, 1)
                    if not (isinstance(n, int) and n == 0):
                        rows_left(n - 1)
                    if more:
                        stage_sample(n + 1)
                    dve.wait_ge(s.tp_exp, n + 1)
                    link(V.reciprocal(st[:, 9:12], st[:, 6:9]))
                    link(V.tensor_tensor(st[:, 0:3], st[:, 9:12], gsm[:, ds(n, 1), :].rearrange("p a c -> p (a c)"), ALU.mult))
                    sc = tpr[:, 0:576].rearrange("p (w k) -> p w k", w=2)
                    V.tensor_tensor(sc, sc, bcast(st[:, 0:2].unsqueeze(2), [64, 2, 288]), ALU.mult)
                    V.tensor_scalar(tpr[:, 576:584], tpr[:, 576:584], st[:, 2:3], None, ALU.mult).then_inc(s.tp_ready, 1)
                    dve.wait_ge(s.tpt_full, n + 1)
                    V.tensor_copy(tpcT[0:NS, 0:P], ps[0:NS, 3, 0:P])
                    V.tensor_copy(tpcT[0:NCB, P:P + 64], ps[0:NCB, 3, P:P + 64]).then_inc(s.tpt_dve, 1)
                    if not (isinstance(n, int) and n == 0):
                        out_left(n - 1)
                    if more:
                        cmp_values_left(n + 1, 1 - b)

            loop(dve, ch, DB // 2, sample, last=True)
            rows_left(DB - 1)
            out_left(DB - 1)

            for half in range(2):
                evac(wsT[:, 4 * half:4 * half + 4, :], lambda p: p.rearrange("p (g i) -> p g i", g=4))
            evac(wssT, lambda p: p[0:NS, 0:256].rearrange("p (g i) -> p g i", g=AG))
            dve.wait_ge(s.v_ev, 2 * V_IT)
            for t in range(3):
                for c in range(4):
                    ins = V.bn_stats(bn[0:ROWS[t], t, c, :], v_tok[0:ROWS[t], t, c * 512:(c + 1) * 512])
            link(ins)
            for t in range(3):
                ins = V.bn_aggr(mv[0:ROWS[t], t, :], bn[0:ROWS[t], t].rearrange("p c s -> p (c s)"))
            link(ins)
            dve.sem_inc(s.rstd_sq, 1)
            dve.wait_ge(s.rstd_sq, 3)
            link(V.reciprocal(rstd[:], rstd[:]))
            dve.wait_ge(s.ln_in, 16 * (4 + DB))
            for t in range(3):
                r = ROWS[t]
                vt = v_tok[0:r, t, :]
                link(V.tensor_scalar(vt, vt, mv[0:r, t, 0:1], rstd[0:r, t:t + 1], ALU.subtract, ALU.mult))
                link(V.tensor_tensor(vt, vt, ln_g[0:r], ALU.mult))
                link(V.tensor_tensor(vt, vt, ln_b[0:r], ALU.add))
            dve.sem_inc(s.v_ready, 1)
            dve.wait_ge(s.u_ev, 2 * U_IT)
            for k in range(KT):
                dve.wait_ge(s.sp_full, k + 1)
                t_ = scr2[:, (k % 2) * TOK:(k % 2) * TOK + TOK]
                link(V.tensor_tensor(t_, ps[:, k % 2, 0:TOK], sbias[:, k // 2, :], ALU.add))
                V.tensor_tensor(uT[:, k, :], uT[:, k, :], t_, ALU.mult).then_inc(s.sp_done, 1)

            def merge(c):
                for half in range(2):
                    n = c * 2 + half
                    dve.wait_ge(s.w_used, chunk_done(n + IT_M, 1))
                    dve.wait_ge(s.m_ev_act, n + 1)
                    m2 = mT[:, ds(c * 2, 2), :]
                    if half == 0:
                        link(V.tensor_tensor(m2, ps[:, 3:5, 0:TOK], sig[:, 0], ALU.mult))
                        dve.sem_inc(s.m_ev_dve, 1)
                    else:
                        link(V.tensor_tensor(sig[:, 1], ps[:, 3:5, 0:TOK], sig[:, 1], ALU.mult))
                        link(V.tensor_tensor(m2, m2, sig[:, 1], ALU.add))
                        dve.sem_inc(s.m_ev_dve, 1)

            loop(dve, ch, M_IT, merge)

            def w_o(i):
                for b in range(2):
                    dve.wait_ge(s.w_used, chunk_done(i + IT_O, b))
                    x2_ = xt[:, 0:2, ds(i * 512 + b * 256, 256)]
                    x1_ = xt[0:NS, 2, ds(i * 512 + b * 256, 256)]
                    V.tensor_tensor(x2_, x2_, ps[:, 3 * b:3 * b + 2, 0:256], ALU.add)
                    V.tensor_tensor(x1_, x1_, ps[0:NS, 3 * b + 2, 0:256], ALU.add).then_inc(s.wo_ev, 1)

            dve.wait_ge(s.x_in, 96)
            loop(dve, ch, O_IT, w_o)
            norm(1, 4)

            dve.wait_ge(s.lg_full, 1)
            for t in range(3):
                r = ROWS[t]
                ins = V.tensor_tensor(lg[0:r, t, :], ps[0:r, 0, t * 36:(t + 1) * 36], rb[0:r], ALU.add)
            link(ins)
            link(V.tensor_copy(g8[:, :, 0:NG], lg[:, :, 0:NG]))
            for t in range(3):
                ins = V.max(mx8[:, t], g8[:, t])
            link(ins)
            for t in range(3):
                V.max_index(mi8[:, t], mx8[:, t], g8[:, t])
            link(V.tensor_scalar(rs[:, 0], mx8[:, :, 0], -1.0, None, ALU.mult))
            dve.sem_inc(s.zsq, 1)
            link(V.tensor_copy(mif[:], mi8[:]))
            link(V.tensor_copy(rs[:, 4], mif[:, :, 0]))
            link(V.tensor_tensor(goh[:], bcast(c_("iota8").unsqueeze(1), [P, 3, 8]), bcast(rs[:, 4].unsqueeze(2), [P, 3, 8]), ALU.is_equal))
            for t in range(3):
                ins = V.tensor_tensor(le4[:, t], lg[:, t, NG:].rearrange("p (g e) -> p e g", g=NG),
                                      bcast(goh[:, t, 0:NG].unsqueeze(1), [P, EPG, NG]), ALU.mult)
            link(ins)
            link(V.tensor_reduce(le[:], le4[:], AX_X, ALU.add))
            for t in range(3):
                ins = V.max(mx8[:, t], le[:, t])
            link(ins)
            for t in range(3):
                V.max_index(mi8[:, t], mx8[:, t], le[:, t])
            link(V.tensor_tensor(rs[:, 2], mx8[:, :, 1], mx8[:, :, 0], ALU.subtract))
            dve.sem_inc(s.zsq, 1)
            link(V.tensor_copy(mif[:], mi8[:]))
            for k in range(2):
                link(V.scalar_tensor_tensor(out=rs[:, 5 + k], in0=rs[:, 4], scalar=float(EPG), in1=mif[:, :, k], op0=ALU.mult, op1=ALU.add))
                link(V.tensor_tensor(oh[:, :, k], bcast(c_("iota32").unsqueeze(1), [P, 3, NE]), bcast(rs[:, 5 + k].unsqueeze(2), [P, 3, NE]), ALU.is_equal))
            V.tensor_tensor(selm[:], oh[:, :, 0], oh[:, :, 1], ALU.add).then_inc(s.rank_done, 1)
            dve.wait_ge(s.lg_done, 4)
            link(V.tensor_scalar(rs[:, 7], rs[:, 3], 1.0, None, ALU.add))
            link(V.tensor_tensor(rs[:, 7], rs[:, 7], rs[:, 1], ALU.mult))
            link(V.reciprocal(rs[:, 8], rs[:, 7]))
            link(V.tensor_tensor(rs[:, 9], rs[:, 8], rs[:, 3], ALU.mult))
            dve.wait_ge(s.rank_full, 1)
            link(V.tensor_copy(cnt[:], ps[:, 1, 96:128]))
            link(V.tensor_scalar(novf[:, 0], cnt[:], float(CAP), None, ALU.is_gt))
            for m in range(2, MAXCH):
                link(V.scalar_tensor_tensor(out=novf[:, 0], in0=cnt[:], scalar=float(CAP * m), in1=novf[:, 0], op0=ALU.is_gt, op1=ALU.add))
            link(V.tensor_copy(novf[:, 1], novf[:, 0]))
            cur = 1
            for sh in (1, 2, 4, 8, 16):
                nxt = 3 - cur
                V.tensor_copy(novf[:, nxt, 0:sh], novf[:, cur, 0:sh])
                link(V.tensor_tensor(novf[:, nxt, sh:], novf[:, cur, sh:], novf[:, cur, 0:NE - sh], ALU.add))
                cur = nxt
            incl = novf[:, cur]
            excl = novf[:, 3 - cur]
            link(V.tensor_tensor(excl, incl, novf[:, 0], ALU.subtract))
            link(V.tensor_tensor(ovf_cmp, bcast(incl.unsqueeze(1), [P, NOVF, NE]),
                                 c_("ovf_no").rearrange("p (o e) -> p o e", o=NOVF), ALU.is_le))
            link(V.tensor_reduce(ovf_ef[:, 0:NOVF], ovf_cmp, AX_X, ALU.add))
            link(V.tensor_scalar(ovf_ef[:, 0:NOVF], ovf_ef[:, 0:NOVF], float(NE - 1), None, ALU.min))
            link(V.tensor_copy(ovf_ef[:, NOVF:NOVF + 1], incl[:, NE - 1:NE]))
            link(V.tensor_copy(ovf_e[:], ovf_ef[:]))
            for t in range(3):
                ins = V.tensor_copy(posn[0:ROWS[t], t], ps[0:ROWS[t], 1, t * NE:(t + 1) * NE])
            link(ins)
            link(V.scalar_tensor_tensor(out=excl, in0=excl, scalar=float(CAP), in1=c_("base32"), op0=ALU.mult, op1=ALU.subtract))
            link(V.tensor_scalar(excl, excl, float((NE - 1) * CAP), None, ALU.add))
            link(V.tensor_scalar(posn2[:], posn[:], float(CAP), None, ALU.is_ge))
            link(V.tensor_tensor(posn2[:], posn2[:], bcast(excl.unsqueeze(1), [P, 3, NE]), ALU.mult))
            link(V.tensor_tensor(posn[:], posn[:], bcast(c_("base32").unsqueeze(1), [P, 3, NE]), ALU.add))
            link(V.tensor_tensor(posn[:], posn[:], posn2[:], ALU.add))
            for k in range(2):
                link(V.tensor_tensor(posn2[:], posn[:], oh[:, :, k], ALU.mult))
                link(V.tensor_reduce(slotf[:, :, k], posn2[:], AX_X, ALU.add))
            V.tensor_copy(sloti[:], slotf[:])
            V.tensor_copy(ids[:, :, :, 0], bcast(c_("token").unsqueeze(2), [P, 3, 2]))
            link(V.tensor_copy(ids[:, :, :, 1], c_("pair").rearrange("p (t k) -> p t k", t=3)))
            dve.sem_inc(s.slots_rdy, 1)
            dve.sem_inc(s.ids_ready, 1)

            def rest_of_weights(slot, q, hi, n, done):
                dve.wait_ge(hi, n)
                V.tensor_tensor(split[slot][:, 1], staging[q], split[slot][:, 0].bitcast(F32), ALU.subtract).then_inc(done, 1)

            def piece_lo(e, b, q):
                if q > 5:
                    e, b, q = e + 1, 1 - b, q - 6
                if isinstance(e, int) and (e == NE or (e == NE - 1 and q < 4)):
                    return
                rest_of_weights((6 * b + q) % 4, q, s.hi_done, before(e, q) + 1, s.lo_done)

            def rows_lo(b, hi, n, done):
                dve.wait_ge(hi, n)
                V.tensor_tensor(xgT[b][:, 1, 0:KT * CAP].rearrange("p (n c) -> p n c", n=2), ps[:, 0:2, 0:8 * CAP],
                                xgT[b][:, 0, 0:KT * CAP].bitcast(F32).rearrange("p (n c) -> p n c", n=2), ALU.subtract).then_inc(done, 1)

            def hidT_lo(bank, hi, n, done):
                dve.wait_ge(hi, n)
                V.tensor_tensor(hidT[:, 1, 0:2 * CAP], ps[:, bank, 0:2 * CAP], hidT[:, 0, 0:2 * CAP].bitcast(F32), ALU.subtract).then_inc(done, 1)

            def y_right(e):
                dve.wait_ge(s.piece_used, before(e, 5) + 1)
                after(dve, s.y_out, e * 16)
                V.tensor_copy(y_sb[:, 1024:2048].rearrange("p (n c) -> p n c", n=2), ps[0:CAP, 6:8]).then_inc(s.y_dve, 1)

            for b in range(2):
                V.memset(xgT[b][:, :, KT * CAP:].bitcast(F32), 0.0)
            link(V.memset(hidT[:, :, 2 * CAP:].bitcast(F32), 0.0))
            for q in range(4):
                rest_of_weights(q, q, s.hi_done, q + 1, s.lo_done)
            rows_lo(0, s.xgh_done, 1, s.xgT_ready)
            piece_lo(0, 0, 0)
            piece_lo(0, 0, 1)
            rows_lo(1, s.xgh_done, 2, s.xgT_ready)

            def item(j):
                for b in range(2):
                    e = j * 2 + b
                    dve.wait_ge(s.hg_done, e + 1)
                    after(dve, s.ht_done, e)
                    V.tensor_tensor(hid, hgate, ps[0:CAP, 2 + b, ED:2 * ED], ALU.mult).then_inc(s.hid_done, 1)
                    piece_lo(e, b, 2)
                    piece_lo(e, b, 3)
                    if not (isinstance(e, int) and e == 0):
                        y_right(e - 1)
                    piece_lo(e, b, 4)
                    piece_lo(e, b, 5)
                    piece_lo(e, b, 6)
                    hidT_lo(2 + b, s.hidTh_done, e + 1, s.hidT_ready)
                    if not (isinstance(e, int) and e >= NE - 2):
                        rows_lo(b, s.xgh_done, e + 3, s.xgT_ready)
                    piece_lo(e, b, 7)

            loop(dve, ch, NE // 2, item, last=True)
            y_right(NE - 1)
            n_ovf = dve.value_load(ovf_e[0:1, NOVF:NOVF + 1], min_val=0, max_val=NOVF)
            with dve.If(n_ovf > 0):
                with dve.Fori(0, n_ovf) as o:
                    rows_lo(0, s.o_xgh, o + 1, s.o_xgT)
                    for q in range(6):
                        rest_of_weights(q % 4, q, s.o_hi, o * 6 + (q + 1), s.o_lo)
                    dve.wait_ge(s.o_hg, o + 1)
                    V.tensor_tensor(hid, hgate, ps[0:CAP, 2, ED:2 * ED], ALU.mult).then_inc(s.o_hid, 1)
                    hidT_lo(2, s.o_hidTh, o + 1, s.o_hidT)

            dve.wait_ge(s.yp_in, 16 * 7)
            for k in range(2):
                for t in range(3):
                    r = ROWS[t]
                    xr = xt[0:r, t, :]
                    ins = V.scalar_tensor_tensor(out=xr, in0=yp[2 * t + k][0:r], scalar=rs[0:r, 8 + k, t:t + 1], in1=xr, op0=ALU.mult, op1=ALU.add)
                    if k == 0:
                        if t == 2:
                            link(ins)
                    else:
                        ins.then_inc(s.x2_done, 1)
            dve.wait_ge(s.rstd_sq, 5)
            link(V.reciprocal(rstd[:], rstd[:]))
            for t in range(3):
                r = ROWS[t]
                V.scalar_tensor_tensor(out=fin[t][0:r], in0=xt[0:r, t, :], scalar=rstd[0:r, t:t + 1], in1=gfin[0:r], op0=ALU.mult, op1=ALU.mult).then_inc(s.fin_ready, 1)

        @block.tensor
        def _(pe):
            M = nc.tensor.matmul
            T = nc.tensor.transpose
            tp = [0]

            def group(parts):
                n = tp[0]
                if n >= 2:
                    pe.wait_ge(s.tp_free, n - 1)
                for col, src in parts:
                    rows, cols = src.shape
                    ins = T(ps[0:cols, 6 + n % 2, col:col + rows], src, ident[0:rows, 0:rows])
                ins.then_inc(s.tp_full, 1)
                tp[0] += 1

            pe.wait_ge(s.consts_in, 16)
            pe.wait_ge(s.small_in_in, 48)
            group([(0, small_in[0:KT, 0])])
            group([(0, small_in[:, 1])])
            group([(0, small_in[:, 2])])

            def norm_T(which):
                hn, base = hn_at[which], 3 * which
                for t in range(3):
                    pe.wait_ge(s.normed, base + t + 1)
                    for k4 in range(4):
                        group([(q * P, hn[t][0:ROWS[t], (4 * k4 + q) * P:(4 * k4 + q + 1) * P]) for q in range(4)])
                pe.wait_ge(s.tp_free, tp[0])

            norm_T(0)

            def weights_in(it, u):
                pe.wait_ge(w_sems[u], it * 16 + 16)

            def used(ins):
                ins.then_inc(s.w_used, 1)

            def rows_chunk(it, b, lhs):
                for half in range(2):
                    u = 2 * b + half
                    weights_in(it, u)
                    for k in range(8):
                        kk = 8 * half + k
                        for t in range(3):
                            r = ROWS[t]
                            ins = M(ps[0:r, 3 * b + t, 0:256], lhs[:, kk, t * P:t * P + r], ring[:, u, k, :],
                                    start=(kk == 0), stop=(kk == KT - 1))
                    if half == 0:
                        used(ins)
                used(ins)

            def cols_chunk(it, b, rhs):
                for half in range(2):
                    u = 2 * b + half
                    weights_in(it, u)
                    for k in range(8):
                        kk = 8 * half + k
                        for c in range(2):
                            ins = M(ps[:, 3 * b + c, 0:TOK], ring[:, u, k, c * P:(c + 1) * P], rhs[:, kk, :],
                                    start=(kk == 0), stop=(kk == KT - 1))
                    if half == 0:
                        used(ins)
                used(ins)

            def kv_(i):
                after(pe, s.kv_ev_act, i)
                rows_chunk(i, 0, hT)
                after(pe, s.kv_ev_dve, i)
                rows_chunk(i, 1, hT)

            loop(pe, None, KV_IT, kv_)
            pe.wait_ge(s.wbr_in, 16)
            for t in range(3):
                for k in range(KT):
                    ins = M(ps[0:ROWS[t], 6, t * 48:(t + 1) * 48], hT[:, k, t * P:t * P + ROWS[t]], wbr[:, k, :],
                            start=(k == 0), stop=(k == KT - 1))
            ins.then_inc(s.br_full, 1)
            pe.wait_ge(s.roped, 1)
            pe.wait_ge(s.br_done, 9)
            for br in range(2):
                for t in range(3):
                    group([(h * P, kv[0:ROWS[t], t, (2 + 2 * br) * KVC + h * HD:(2 + 2 * br) * KVC + (h + 1) * HD]) for h in range(KVH)])

            rv = rowsT.rearrange("p (n j) -> p n j", j=CB)
            for n in range(2):
                def pages(i, n=n):
                    for b in range(2):
                        k = n * PAGES + i * 2 + b
                        pe.wait_ge(page_sems[b], n * (16 * PAGES // 2) + (i * 16 + 16))
                        if n or not isinstance(i, int):
                            pe.wait_ge(s.page_ev, k - 1)
                        for h in range(KVH):
                            ins = T(ps[:, 6 + b, h * P:(h + 1) * P], page_rows[:, b, h * P:(h + 1) * P], ident)
                        ins.then_inc(s.page_T, 1)

                pe.wait_ge(s.tp_free, tp[0])
                loop(pe, None, PAGES // 2, pages)
                pe.wait_ge(s.page_ev, (n + 1) * PAGES)
                for t in range(2):
                    group([(h * P, kv[:, t, n * KVC + h * HD:n * KVC + (h + 1) * HD]) for h in range(KVH)])
                pe.wait_ge(s.tp_free, tp[0])
                pe.wait_ge((s.w1k_in, s.w1v_in)[n], 16)
                for j in range(CB):
                    ins = M(ps[:, n, 0:288], w1[:, j, :], rv[:, :, j], start=(j == 0), stop=(j == CB - 1))
                ins.then_inc(s.cmp_hid_full, 1)
                pe.wait_ge(s.cmp_hid, n + 1)
                pe.wait_ge(s.w_aux_in, 96)
                if n == 0:
                    M(ps[:, 2, 0:288], w2[:, 0], hidcT[:, 0], start=True, stop=True).then_inc(s.kc_full, 1)
                else:
                    for h in range(KVH):
                        c = (DB * KVH + h) * NCB
                        ins = M(ps[0:NCB, 3, h * HD:(h + 1) * HD], hidcT[:, 1, c:c + NCB], w2[:, 1], start=True, stop=True)
                    ins.then_inc(s.vc_full, 1)
            pe.wait_ge(s.vc_ready, 1)
            pe.wait_ge(s.kc_ready, 1)

            def q_(i):
                for b in range(2):
                    after(pe, (s.q_ev_act, s.q_ev_dve)[b], i)
                    cols_chunk(i + IT_Q, b, hT)

            loop(pe, None, Q_IT, q_)
            pe.wait_ge(s.q_ev_act, Q_IT)
            pe.wait_ge(s.q_ev_dve, Q_IT)

            def rot(i):
                after(pe, s.rot_done, i)
                for h in range(4):
                    ins = M(ps[0:RD, h, 0:TOK], c_("swap"), qT[:, ds(i * 4 + h, 1), :].rearrange("p a t -> p (a t)"), start=True, stop=True)
                ins.then_inc(s.rot_full, 1)

            loop(pe, None, 4, rot)
            pe.wait_ge(s.q_ready, 1)

            def scores(n, kh, g):
                b = g % 2
                if g == 0:
                    pe.wait_ge(s.q_staged, kh + 1)
                after(pe, s.p_exp, n - 1)
                for qt, (in_tile, tri) in enumerate(((P, 0), (2 * P, P))):
                    q_ = q_st[:, g, qt * P:(qt + 1) * P]
                    for w in range(2):
                        out = ps[:, 2 * b + qt, w * in_tile:(w + 1) * in_tile]
                        M(out, q_, kT[:, w, ds(kh, 1), 0:in_tile].rearrange("p a t -> p (a t)"), start=True, stop=False)
                        M(out[:, tri:tri + P], ident, c_("pmask")[:, P:2 * P], start=False, stop=True)
                    out = ps[:, 2 * b, 2 * P + qt * NCB:2 * P + (qt + 1) * NCB]
                    M(out, q_, kcT[:, ds(kh * NCB + DB * KVH * NCB, NCB)], start=True, stop=False)
                    ins = M(out, ident, c_("cmask")[:, qt * NCB:(qt + 1) * NCB], start=False, stop=True)
                ins.then_inc(s.s_full, 1)

            def values(n, b):
                pe.wait_ge(s.pt_act, n + 1)
                pe.wait_ge(s.pt_dve, n + 1)
                after(pe, s.o_ev, n - 1)
                out = ps[:, 6 + b, 0:2 * P]
                for w in range(2):
                    M(out, v_st[:, 0, w, :], pT[:, w * 2 * P:(w + 1) * 2 * P], start=(w == 0), stop=False)
                M(out, vch_st, pcT, start=False, stop=False)
                for w in range(2):
                    ins = M(out[:, P:2 * P], v_st[:, 1, w, :], pT[:, (4 + w) * P:(5 + w) * P], start=False, stop=(w == 1))
                ins.then_inc(s.pv_done, 1)

            def transposes(n, b):
                pe.wait_ge(s.p_ready, n + 1)
                after(pe, s.pt_act, n)
                after(pe, s.pt_dve, n)
                for w in range(2):
                    T(ps[:, 4, 2 * w * P:(2 * w + 1) * P], pr[:, b, w * P:(w + 1) * P], ident)
                    for k in range(2):
                        c = (2 + 2 * w + k) * P
                        out = ps[:, 4, (2 * w + 1) * P:(2 * w + 2) * P] if k == 0 else ps[:, 5, w * P:(w + 1) * P]
                        T(out, pr[:, b, c:c + P], ident)
                for qt in range(2):
                    ins = T(ps[0:NCB, 5, (2 + qt) * P:(3 + qt) * P], pr[:, b, 6 * P + qt * NCB:6 * P + (qt + 1) * NCB], ident)
                ins.then_inc(s.pt_full, 1)

            def heads(kh, last):
                for g in range(GQ):
                    n = kh * GQ + g
                    b = g % 2
                    if g < GQ - 1:
                        scores(n + 1, kh, g + 1)
                    elif not last:
                        scores(n + 1, kh + 1, 0)
                    if not (isinstance(n, int) and n == 0):
                        if g == 1:
                            pe.wait_ge(s.v_staged, kh + 1)
                        values(n - 1, 1 - b)
                    transposes(n, b)

            scores(0, 0, 0)
            kv_heads(pe, None, heads)
            values(NH - 1, 1)
            pe.wait_ge(s.o_ev, NH)

            def keys_T(n, b, loads):
                pe.wait_ge(kx_sems[b], loads)
                for h in range(KVH):
                    after(pe, s.kx_ev, n * 4 + (h - 1))
                    for t in range(4):
                        ins = T(ps[:, 6 + h % 2, t * P:(t + 1) * P], kx[:, b, t, h * HD:(h + 1) * HD], ident)
                    ins.then_inc(s.kxT_full, 1)

            def cmp_values(n):
                pe.wait_ge(s.qp_ready, n + 1)
                after(pe, s.vcs_ev, n)
                for h in range(KVH):
                    ins = M(ps[0:NCB, 5, h * HD:(h + 1) * HD], hidc_st[:, h * NCB:(h + 1) * NCB], w2[:, 1], start=True, stop=True)
                ins.then_inc(s.vcs_full, 1)

            def out_T(n):
                apart(pe, s.o_rows, n + 1, s.pe_passed)
                for h in range(KVH):
                    ins = T(ps[:, 4, h * 64:(h + 1) * 64], o_st[:, h * HD:(h + 1) * HD], ident[0:64, 0:64])
                ins.then_inc(s.oT_full, 1)

            keys_T(0, 0, 48)
            cmp_values(0)

            def sample(i):
                for b in range(2):
                    n = i * 2 + b
                    more = not (isinstance(n, int) and n == DB - 1)
                    pe.wait_ge(s.qp_ready, n + 1)
                    pe.wait_ge(s.kx_ev, n * 4 + 4)
                    after(pe, s.tp_exp, n)
                    for w in range(2):
                        for h in range(KVH):
                            M(ps[0:64, w, 0:256], qpad[:, h * 64:(h + 1) * 64], kxT[:, h, w * 256:(w + 1) * 256], start=(h == 0), stop=(h == KVH - 1))
                        for h in range(KVH):
                            M(ps[0:64, w, 256:288], qpad[:, h * 64:(h + 1) * 64], kT[:, w, h, SEQ:TOK], start=(h == 0), stop=False)
                        M(ps[0:64, w, 256:288], ident[:, 0:64], c_("smask")[:, ds(n * NS, NS)], start=False, stop=True)
                    for h in range(KVH):
                        ins = M(ps[0:64, 0, 288:296], qpad[:, h * 64:(h + 1) * 64], kcT[:, ds(n * (KVH * NCB) + h * NCB, NCB)], start=(h == 0), stop=(h == KVH - 1))
                    ins.then_inc(s.t_full, 1)
                    if more:
                        keys_T(n + 1, 1 - b, (i + b) * 48 + 48)
                    if not (isinstance(n, int) and n == 0):
                        out_T(n - 1)
                    apart(pe, s.tp_ready, n + 1, s.pe_passed)
                    for w in range(2):
                        for k in range(2):
                            T(ps[:, 2, (2 * w + k) * 64:(2 * w + k + 1) * 64], tpr[:, w * 288 + k * P:w * 288 + (k + 1) * P], ident[0:64, 0:64])
                        T(ps[0:NS, 3, w * 64:(w + 1) * 64], tpr[:, w * 288 + 256:w * 288 + 288], ident[0:64, 0:64])
                    T(ps[0:NCB, 3, 128:192], tpr[:, 576:584], ident[0:64, 0:64]).then_inc(s.tpt_full, 1)
                    if more:
                        cmp_values(n + 1)
                    pe.wait_ge(vx_sems[b], i * 48 + 48)
                    pe.wait_ge(s.tpt_act, n + 1)
                    pe.wait_ge(s.tpt_dve, n + 1)
                    pe.wait_ge(s.vcs_ev, n + 1)
                    after(pe, s.to_ev, n)
                    out = ps[0:NH * DT, 4]
                    for w in range(2):
                        for k in range(2):
                            c = (2 * w + k) * 64
                            M(out, tpT[:, c:c + 64], vx[:, b, 2 * w + k, :], start=(w == 0 and k == 0), stop=False)
                        M(out, tpcT[0:NS, w * 64:(w + 1) * 64], kv[0:NS, 2, (3 + 2 * w) * KVC:(4 + 2 * w) * KVC], start=False, stop=False)
                    ins = M(out, tpcT[0:NCB, 128:192], vcs_st[:, b], start=False, stop=True)
                    ins.then_inc(s.tpv_done, 1)

            loop(pe, None, DB // 2, sample, last=True)
            out_T(DB - 1)
            pe.wait_ge(s.to_ev, DB)

            def v_(i):
                for b in range(2):
                    if not (isinstance(i, int)):
                        pe.wait_ge(s.v_ev, i * 2 + (b - 1))
                    rows_chunk(i + IT_V, b, hT)

            loop(pe, None, V_IT, v_)
            pe.wait_ge(s.ws_masked, 2)
            for half in range(2):
                group([(q * P, ws_raw[:, 4 * half + q, :]) for q in range(4)])
            group([(g * NS, wss_raw[:, g, :]) for g in range(AG)])
            pe.wait_ge(s.v_ev, 2 * V_IT)

            def u_(i):
                for b in range(2):
                    if not (isinstance(i, int)):
                        pe.wait_ge(s.u_ev, i * 2 + (b - 1))
                    cols_chunk(i + IT_U, b, hT)

            loop(pe, None, U_IT, u_)
            pe.wait_ge(s.u_ev, 2 * U_IT)
            pe.wait_ge(s.v_ready, 1)
            pe.wait_ge(s.tp_free, tp[0])
            for k in range(KT):
                after(pe, s.sp_done, k - 1)
                g = k // 2
                for t in range(2):
                    M(ps[:, k % 2, t * P:(t + 1) * P], v_tok[:, t, k * P:(k + 1) * P], wsT[:, g, :], start=True, stop=True)
                M(ps[:, k % 2, SEQ:TOK], v_tok[0:NS, 2, k * P:(k + 1) * P], wssT[:, g, :], start=True, stop=True).then_inc(s.sp_full, 1)
            pe.wait_ge(s.sp_done, KT)

            def merge(c):
                for half in range(2):
                    n = c * 2 + half
                    it = n + IT_M
                    after(pe, s.m_ev_act, n)
                    cols_chunk(it, 0, hT)
                    after(pe, s.m_ev_dve, n)
                    cols_chunk(it, 1, (uT, qT)[half])

            loop(pe, None, M_IT, merge)
            pe.wait_ge(s.m_ev_act, 2 * M_IT)
            pe.wait_ge(s.m_ev_dve, 2 * M_IT)

            def w_o(i):
                for b in range(2):
                    if not isinstance(i, int):
                        pe.wait_ge(s.wo_ev, i * 2 + (b - 1))
                    rows_chunk(i + IT_O, b, mT)

            loop(pe, None, O_IT, w_o)
            norm_T(1)
            pe.wait_ge(s.wo_ev, 2 * O_IT)
            for t in range(3):
                for k in range(KT):
                    ins = M(ps[0:ROWS[t], 0, t * 36:(t + 1) * 36], hT[:, k, t * P:t * P + ROWS[t]], wr[:, k, :],
                            start=(k == 0), stop=(k == KT - 1))
            ins.then_inc(s.lg_full, 1)
            pe.wait_ge(s.rank_done, 1)
            for t in range(3):
                r = ROWS[t]
                for j in range(t):
                    M(ps[0:r, 1, t * NE:(t + 1) * NE], c_("ones")[:, 0:r], selm[:, j], start=(j == 0), stop=False)
                M(ps[0:r, 1, t * NE:(t + 1) * NE], c_("before", r)[:, 0:r], selm[0:r, t], start=(t == 0), stop=True)
            for t in range(3):
                r = ROWS[t]
                ins = M(ps[:, 1, 96:128], c_("ones", r), selm[0:r, t], start=(t == 0), stop=(t == 2))
            ins.then_inc(s.rank_full, 1)
            pe.wait_ge(s.ids_ready, 1)

            def rows_T(done):
                for k in range(KT):
                    ins = T(ps[:, k // 8, (k % 8) * CAP:(k % 8 + 1) * CAP], xg[:, k * P:(k + 1) * P], ident[0:CAP, 0:CAP])
                ins.then_inc(done, 1)

            def three(out, x, col, w, start, stop):
                M(out, x[:, 0, col:col + P], w[0], start=start, stop=False)
                M(out, x[:, 0, col:col + P], w[1], start=False, stop=False)
                return M(out, x[:, 1, col:col + P], w[0], start=False, stop=stop)

            def gate_up(x, bank, slot0, lo, n, done):
                for q in range(4):
                    pe.wait_ge(lo, n + (q + 1))
                    sl = split[(slot0 + q) % 4]
                    for k in range(4):
                        c = slice(2 * ED * k, 2 * ED * (k + 1))
                        ins = three(ps[:, bank], x, (4 * q + k) * CAP, (sl[:, 0, c], sl[:, 1, c]),
                                    start=(q == 0 and k == 0), stop=(q == 3 and k == 3))
                    ins.then_inc(done, 1)

            def hid_T(bank, done):
                for f in range(2):
                    ins = T(ps[:, bank, f * CAP:(f + 1) * CAP], hid[:, f * P:(f + 1) * P], ident[0:CAP, 0:CAP])
                ins.then_inc(done, 1)

            def down(slot0, lo, n, done):
                for f in range(2):
                    pe.wait_ge(lo, n + (f + 1))
                    sl = split[(slot0 + f) % 4]
                    for c4 in range(4):
                        c = slice(512 * c4, 512 * (c4 + 1))
                        ins = three(ps[:, 4 + c4], hidT, f * CAP, (sl[:, 0, c], sl[:, 1, c]), start=(f == 0), stop=(f == 1))
                    ins.then_inc(done, 1)

            pe.wait_ge(s.xg_in, 16)
            rows_T(s.xt_done)
            pe.wait_ge(s.xgT_ready, 1)
            gate_up(xgT[0], 2, 0, s.lo_done, 0, s.piece_used)
            pe.wait_ge(s.xg_in, 32)
            rows_T(s.xt_done)

            def item(j):
                for b in range(2):
                    e = j * 2 + b
                    last = isinstance(e, int) and e == NE - 1
                    after(pe, s.hidT_ready, e)
                    if not last:
                        pe.wait_ge(s.xgT_ready, e + 2)
                        gate_up(xgT[1 - b], 3 - b, 6 * b, s.lo_done, before(e, 0), s.piece_used)
                    apart(pe, s.hid_done, e + 1, s.pe_passed)
                    hid_T(2 + b, s.ht_done)
                    if not (isinstance(e, int) and e >= NE - 2):
                        apart(pe, s.xg_in, (e + 3) * 16, s.pe_passed)
                        rows_T(s.xt_done)
                    pe.wait_ge(s.hidT_ready, e + 1)
                    after(pe, s.y_act, e)
                    after(pe, s.y_dve, e)
                    down(6 * b + 4, s.lo_done, before(e, 4), s.piece_used)

            loop(pe, None, NE // 2, item, last=True)
            n_ovf = pe.value_load(ovf_e[0:1, NOVF:NOVF + 1], min_val=0, max_val=NOVF)
            with pe.If(n_ovf > 0):
                pe.wait_ge(s.y_act, NE)
                pe.wait_ge(s.y_dve, NE)
                pe.wait_ge(s.lo_done, 6 * NE)
                pe.sem_inc(s.o_free, 1)
                with pe.Fori(0, n_ovf) as o:
                    apart(pe, s.o_xg, o * 16 + 16, s.pe_passed)
                    rows_T(s.o_xt)
                    pe.wait_ge(s.o_xgT, o + 1)
                    gate_up(xgT[0], 2, 0, s.o_lo, o * 6, s.o_used)
                    apart(pe, s.o_hid, o + 1, s.pe_passed)
                    hid_T(2, s.o_ht)
                    pe.wait_ge(s.o_hidT, o + 1)
                    down(4, s.o_lo, o * 6 + 4, s.o_used)
                    pe.wait_ge(s.o_ya, o + 1)
                    pe.sem_inc(s.o_free, 1)


_INS = ['x_prompt', 'x_sample', 'cache_k_cmp', 'cache_v_cmp', 'cache_k_slc', 'cache_v_slc', 'state_k_win', 'state_v_win',
        'page_table', 'g_mix', 'w_in', 'a_ln_g', 'a_ln_b', 'a_w_s', 'a_b_s', 'cmp_pe_k', 'cmp_w1_k', 'cmp_w2_k',
        'cmp_pe_v', 'cmp_w1_v', 'cmp_w2_v', 'w_pa', 'w_pb', 'w_o', 'g_ffn', 'w_rg', 'b_rg', 'w_re', 'b_re',
        'w_gate', 'w_up', 'w_down', 'g_final']
_ROW = (KVH, HD)
_OUTS = ([(1, SEQ, D), (DB, DT, D)] + [(1, 1, SEQ) + _ROW] * 6 + [(1, DB, DT) + _ROW] * 4
         + [(1, DB, PAST) + _ROW] * 2 + [(1, DB, DT, D)])


def kernel(**inputs):
    import concourse.bacc as _bacc
    from concourse.bass_utils import run_bass_kernel_spmd as _run

    nc = _bacc.Bacc("TRN2", target_bir_lowering=False, num_devices=1)
    arrays, aps = {}, {}
    named = [(n, np.ascontiguousarray(inputs[n])) for n in _INS] + [("consts", constants())]
    for name, x in named:
        arrays[f"in_{name}"] = x
        aps[name] = nc.dram_tensor(f"in_{name}", x.shape, mybir.dt.from_np(x.dtype), kind="ExternalInput").ap()
    outs = [nc.dram_tensor(f"out_{i}", shape, F32, kind="ExternalOutput").ap() for i, shape in enumerate(_OUTS)]
    build(nc, aps, outs)
    r = _run(nc, [arrays], core_ids=[0])
    return tuple(r.results[0][f"out_{i}"] for i in range(len(_OUTS)))
```

```python
from contextlib import ExitStack

import numpy as np

import concourse.bass as bass
from concourse import mybir

F32 = mybir.dt.float32
F32R = mybir.dt.float32r
I32 = mybir.dt.int32
U32 = mybir.dt.uint32
ALU = mybir.AluOpType
ACT = mybir.ActivationFunctionType
AX_X = mybir.AxisListType.X
ds = bass.ds

P = 128
D = 2048
KT = D // P
SEQ, DB, DT = 256, 8, 4
NS = DB * DT
TOK = SEQ + NS
ROWS = (P, P, NS)
NH, KVH, GQ, HD = 16, 4, 4, 128
RD, HALF = 32, 16
PAST = 256
PAGES = DB * PAST // P
CB = 32
NSEQ = DB + 1
NCB = PAST // CB
SCALE = float(HD) ** -0.5
EPS = 1e-6
NEG = -1e30
AG = 8
NG, EPG = 4, 8
NE = NG * EPG
ED = 256
CAP = 64
MAXCH = -(-TOK // CAP)
NOVF = 2 * TOK // CAP
NITEM = NE + NOVF
NOWHERE = 1 << 20
C_U, C_V, C_Q, C_KV = 0, D, 2 * D, 3 * D
C_BR = C_KV + 6 * KVH * HD
C_GA = C_BR + 3 * NH
C_GB = C_GA + D
KVC = KVH * HD

CONSTS = {}
CW = 0
for _n, _w in (("ident", P), ("before", P), ("ones", P), ("pmask", 2 * P), ("cmask", 2 * NCB), ("anyvalid", 3),
               ("smask", DB * NS), ("cosT", TOK), ("sinT", TOK), ("swap", RD), ("cos", 3 * HALF), ("sin", 3 * HALF),
               ("iota32", NE), ("base32", NE), ("iota8", 8), ("ovf_no", NOVF * NE), ("token", 3), ("pair", 6)):
    CONSTS[_n] = (CW, _w)
    CW += _w


def constants():
    f = np.float32
    c = np.zeros((P, CW), f)

    def put(name, a):
        o, w = CONSTS[name]
        a = np.asarray(a, f).reshape(a.shape[0], -1)
        c[:a.shape[0], o:o + w] = a

    r = np.arange(P)
    put("ident", np.eye(P))
    put("before", (r[:, None] < r[None, :]))
    put("ones", np.ones((P, P)))
    put("pmask", np.concatenate([np.zeros((P, P)), np.where(r[None, :] <= r[:, None], 0, NEG)], 1))
    ends = (np.arange(NCB) + 1) * CB - 1
    put("cmask", np.stack([np.where((ends[None] <= (r + q * P)[:, None]) | ((r + q * P) < CB - 1)[:, None], 0, NEG)
                           for q in range(2)], 1))
    av = np.ones((P, 3))
    av[:CB - 1, 0] = 0
    put("anyvalid", av)
    row_t = np.arange(NH * DT) % DT
    k = np.arange(NS)
    put("smask", np.where((k // DT)[None, None] == np.arange(DB)[None, :, None],
                          np.where((k % DT)[None, None] <= row_t[:, None, None], 0, NEG), NEG))
    inv = np.power(f(500000.0), -np.arange(0, RD, 2, dtype=f) / f(RD))
    pos = np.concatenate([np.arange(SEQ), PAST + np.arange(NS) % DT]).astype(f)
    ang = (pos[:, None] * inv[None]).astype(f)
    cos, sin = np.cos(ang), np.sin(ang)
    put("cosT", np.concatenate([cos, cos], 1).T)
    put("sinT", np.concatenate([-sin, sin], 1).T)
    put("swap", np.roll(np.eye(RD), HALF, 1))
    tiles = np.zeros((2, P, 3, HALF))
    for t in range(3):
        tiles[0, :ROWS[t], t] = cos[t * P:t * P + ROWS[t]]
        tiles[1, :ROWS[t], t] = sin[t * P:t * P + ROWS[t]]
    put("cos", tiles[0])
    put("sin", tiles[1])
    put("iota32", np.tile(np.arange(NE), (P, 1)))
    put("base32", np.tile(np.arange(NE) * CAP, (P, 1)))
    put("iota8", np.tile(np.arange(8), (P, 1)))
    put("ovf_no", np.tile(np.repeat(np.arange(NOVF), NE), (P, 1)))
    tok = r[:, None] + P * np.arange(3)[None]
    put("token", tok)
    put("pair", tok[:, :, None] + TOK * np.arange(2)[None, None])
    return c


def bcast(ap, shape):
    return ap.broadcast_to(shape)


class Chain:

    def __init__(self, eng, sem):
        self.eng, self.sem, self.n, self.lead = eng, sem, 0, None

    def value(self):
        return self.n if self.lead is None else self.lead + self.n

    def link(self, ins):
        ins.then_inc(self.sem, 1)
        self.n += 1
        self.eng.wait_ge(self.sem, self.value())


def apart(eng, sem, value, passed):
    if not (isinstance(value, int) and value <= 0):
        eng.wait_ge(sem, value)
        eng.sem_inc(passed, 1)


def loop(eng, chain, count, body, last=False):
    start = chain.n if chain else 0
    body(0)
    if chain:
        per = chain.n - start
        chain.n = start
    with eng.Fori(1, count - last) as i:
        if chain and per:
            chain.lead = i * per
        body(i)
    if chain:
        assert chain.n == start + per
        chain.lead = None
        chain.n = start + per * (count - last)
    if last:
        body(count - 1)


def after(eng, sem, value):
    if not (isinstance(value, int) and value <= 0):
        eng.wait_ge(sem, value)


def before(e, q):
    n = e * 6 + (4 + q)
    return n - 4 if isinstance(e, int) and e == NE - 1 else n


def build(nc, a, outs, cap_debug=None):
    (y_prompt, y_sample, o_kcp, o_vcp, o_ksp, o_vsp, o_kwp, o_vwp,
     o_kcs, o_vcs, o_kss, o_vss, o_kws, o_vws, o_vchunk) = outs
    with ExitStack() as ctx:
        def sb(name, shape, dt=F32):
            return ctx.enter_context(nc.sbuf_tensor(name, shape, dt))

        def sem(name):
            return ctx.enter_context(nc.semaphore(name))

        gate_d = nc.dram_tensor("gate_d", (NS, 3 * NH), F32, kind="Internal").ap()
        h2_d = nc.dram_tensor("h2_d", (TOK, D), F32, kind="Internal").ap()
        slot_d = nc.dram_tensor("slot_d", (NITEM * CAP, 2), I32, kind="Internal").ap()
        ypair_d = nc.dram_tensor("ypair_d", (2 * TOK, D), F32, kind="Internal").ap()

        H0, Q0 = 0, KT * TOK
        U0 = Q0 + KT * TOK
        K0 = U0 + 3 * D + KT * TOK
        W0 = K0 + 3 * 6 * KVC
        END = W0 + 4 * 8 * 256 + 1024
        base = -(-nc.sbuf_base // 32) * 32
        mem = sb("mem", [P, END])

        def rounded(name, shape, col):
            return nc.alloc_sbuf_tensor_at(name, shape, F32R, offset=base + 4 * col)

        hT = mem[:, H0:Q0].rearrange("p (k t) -> p k t", k=KT)
        qT = mem[:, Q0:Q0 + KT * TOK].rearrange("p (k t) -> p k t", k=KT)
        v_tok = mem[:, U0:U0 + 3 * D].rearrange("p (t c) -> p t c", t=3)
        uT = mem[:, U0 + 3 * D:K0].rearrange("p (k t) -> p k t", k=KT)
        kv = mem[:, K0:W0].rearrange("p (t c) -> p t c", t=3)
        ring = mem[:, W0:W0 + 4 * 8 * 256].rearrange("p (s k c) -> p s k c", s=4, k=8)
        rowsT = mem[:, U0:U0 + 18 * 512]
        w1 = mem[:, Q0:Q0 + CB * P].rearrange("p (j e) -> p j e", j=CB)
        kx = mem[:, U0:U0 + 2 * 2048].rearrange("p (b t c) -> p b t c", b=2, t=4)
        vx = mem[:, U0 + 4096:U0 + 8192].rearrange("p (b t c) -> p b t c", b=2, t=4)
        kxT = mem[:, U0 + 8192:U0 + 8192 + 2048].rearrange("p (h c) -> p h c", h=KVH)
        mT = mem[:, K0:K0 + KT * TOK].rearrange("p (k t) -> p k t", k=KT)
        ln_g = mem[:, K0:K0 + D]
        ln_b = mem[:, K0 + D:K0 + 2 * D]
        ws_raw = mem[:, K0 + 4096:K0 + 5120].rearrange("p (g j) -> p g j", g=AG)
        wsT = mem[:, K0 + 5120:K0 + 6144].rearrange("p (g j) -> p g j", g=AG)
        sbias = mem[:, K0 + 6144:K0 + 6144 + AG * TOK].rearrange("p (g t) -> p g t", g=AG)
        wss_raw = mem[0:NS, K0 + 8448:K0 + 8704].rearrange("p (g j) -> p g j", g=AG)
        wssT = mem[0:NS, K0 + 8704:K0 + 8960].rearrange("p (g j) -> p g j", g=AG)
        PIECE = 4 * 2 * ED
        staging = [mem[:, Q0 + PIECE * q:Q0 + PIECE * (q + 1)] for q in range(6)]
        X0 = Q0 + 6 * PIECE
        xg = mem[0:CAP, X0:X0 + D]
        g_ffn = mem[:, X0:X0 + D]
        SP0 = K0
        split = [rounded(f"split{n}", [P, 2, PIECE], SP0 + 2 * PIECE * n) for n in range(4)]
        y_sb = mem[0:CAP, SP0 + 8 * PIECE:SP0 + 8 * PIECE + D]
        assert X0 + D <= SP0 and SP0 + 8 * PIECE + D <= END
        XGW = KT * CAP + P - CAP
        xgT = [rounded(f"xgT{b}", [P, 2, XGW], H0 + 2 * XGW * b) for b in range(2)]
        yp = [mem[:, D * b:D * (b + 1)] for b in range(6)]
        gfin = mem[:, 6 * D:7 * D]
        fin = [mem[:, (7 + b) * D:(8 + b) * D] for b in range(3)]

        xt = sb("xt", [P, 3, D])
        HALF_K = KT // 2
        XT0 = END
        h_lo = rounded("h_lo", [P, KT, TOK], H0)
        h_hi = rounded("h_hi", [P, KT, TOK], XT0)
        u_lo = rounded("u_lo", [P, KT, TOK], U0 + 3 * D)
        u_hi = rounded("u_hi", [P, KT, TOK], K0 + KT * TOK)
        q_lo = rounded("q_lo", [P, KT, TOK], Q0)
        q_hi = u_lo
        ring_lo = rounded("ring_lo", [P, 4, 8, 256], W0)
        ring_hi = [[(0, rounded(f"ring_hi{u}", [P, 8, 256], U0 + 2048 * u))] for u in range(3)]
        hkv_hi, hkv_lo = u_lo, q_lo
        hq_hi, hq_lo = u_lo, h_hi
        m_hi = rounded("m_hi", [P, KT, TOK], H0)
        m_lo = rounded("m_lo", [P, KT, TOK], K0)
        out_hi = [[(0, rounded(f"out_hi{u}", [P, 8, 256], at))] for u, at in
                  enumerate((K0 + KT * TOK, K0 + KT * TOK + 2048, Q0 + 4 * PIECE, Q0 + 5 * PIECE))]
        ring_hi.append([(0, rounded("ring_hi3a", [P, 4, 256], W0 + 4 * 8 * 256)), (4, rounded("ring_hi3b", [P, 4, 256], XT0 + KT * TOK))])
        cst = sb("cst", [P, CW])
        gT = sb("gT", [P, KT])
        small_in = sb("small_in", [CB, 3, P])
        peT = sb("peT", [P, 2, CB])
        w2 = sb("w2", [P, 2, P])
        kT_at = -(-nc.sbuf_base // 32) * 32
        kT = sb("kT", [P, 2, KVH, TOK])
        vu_hi = [[(0, rounded(f"vu_hi{n}{m}", [P, 4, 256], at)), (4, rounded(f"vu_hi{n}{m + 1}", [P, 4, 256], at2))]
                 for n, m, at, at2 in ((0, 0, XT0 + KT * TOK, W0 + 4 * 8 * 256), (1, 0, (kT_at - base) // 4, (kT_at - base) // 4 + 1024))] * 2
        hidcT = sb("hidcT", [P, 2, NSEQ * KVH * NCB])
        kcT = sb("kcT", [P, NSEQ * KVH * NCB])
        ptab = sb("ptab", [1, PAGES], I32)
        ss = sb("ss", [P, 3])
        rstd = sb("rstd", [P, 3])
        epsb = sb("epsb", [P, 1])
        gbr = sb("gbr", [P, 3, NH, 3])
        gsm = sb("gsm", [NH * DT, DB, 3])
        att = xt[:].rearrange("p t d -> p (t d)")
        page_rows = att[:, 2048:4096].rearrange("p (b c) -> p b c", b=4)
        rtmp = att[:, 1024:1024 + 48 * HALF].rearrange("p (k c) -> p k c", k=4)
        q_st = att[:, 0:1024].rearrange("p (g t) -> p g t", g=GQ)
        v_st = att[:, 1024:1536].rearrange("p (t r d) -> p t r d", t=2, r=2)
        vc_st = att[0:NCB, 5632:6144]
        PR = 6 * P + 2 * NCB
        pr = att[:, 2048:2048 + 2 * PR].rearrange("p (b c) -> p b c", b=2)
        pT = att[:, 3616:3616 + 6 * P]
        pcT = att[0:NCB, 4384:4384 + 2 * P]
        tpr = att[0:NH * DT, 2048:2048 + 584]
        tpT = att[:, 3616:3616 + 256]
        tpcT = att[0:NS, 4384:4384 + 192]
        o_st = att[0:NH * DT, 1024:1024 + KVC]
        qpad = att[:, 4640:4640 + 320]
        vcs_st = att[0:NCB, 0:2 * KVC].rearrange("p (b c) -> p b c", b=2)
        vch_st = att[0:NCB, 5504:5504 + HD]
        hidc_st = att[:, 5472:5472 + KVH * NCB]
        scr2 = att[:, D:D + 1152]
        sp_sum = kT[:].rearrange("p b h t -> p (b h t)")[:, 4 * TOK:6 * TOK]
        squares_at = [mem[:, K0:K0 + D], mem[:, W0 + 3 * D:W0 + 4 * D], mem[:, 10 * D:11 * D]]
        hn_at = [[mem[:, o + D * t:o + D * (t + 1)] for t in range(3)] for o in (U0, W0)]
        stt = sb("stt", [P, 2, 24])
        bn = sb("bn", [P, 3, 4, 6])
        mv = sb("mv", [P, 3, 2])
        hgate = kT[:].rearrange("p b h t -> p (b h t)")[0:CAP, KT * CAP:KT * CAP + ED]
        hid = kT[:].rearrange("p b h t -> p (b h t)")[0:CAP, KT * CAP + ED:KT * CAP + 2 * ED]
        hidT = sb("hidT", [P, 2, 2 * CAP + P - CAP], F32R)
        sig = kT[:].rearrange("p b h t -> p (b h t)")[:, 0:4 * TOK].rearrange("p (a c t) -> p a c t", a=2, c=2)
        wbr = att[:, 0:KT * 48].rearrange("p (k c) -> p k c", k=KT)
        wr = sb("wr", [P, KT, NG + NE])
        rb = sb("rb", [P, NG + NE])
        lg = sb("lg", [P, 3, NG + NE])
        g8 = sb("g8", [P, 3, 8])
        mx8 = sb("mx8", [P, 3, 8])
        mi8 = sb("mi8", [P, 3, 8], U32)
        mif = sb("mif", [P, 3, 8])
        goh = sb("goh", [P, 3, 8])
        le4 = kT[:].rearrange("p b h t -> p (b h t)")[:, 1152:1248].rearrange("p (t i g) -> p t i g", t=3, i=EPG)
        le = sb("le", [P, 3, 8])
        rs = sb("rs", [P, 12, 3])
        oh = kT[:].rearrange("p b h t -> p (b h t)")[:, 1248:1440].rearrange("p (t k e) -> p t k e", t=3, k=2)
        selm = sb("selm", [P, 3, NE])
        cnt = sb("cnt", [P, NE])
        novf = kT[:].rearrange("p b h t -> p (b h t)")[:, 1536:1632].rearrange("p (t e) -> p t e", t=3)
        posn = sb("posn", [P, 3, NE])
        posn2 = kT[:].rearrange("p b h t -> p (b h t)")[:, 1440:1536].rearrange("p (t e) -> p t e", t=3)
        slotf = sb("slotf", [P, 3, 2])
        sloti = sb("sloti", [P, 3, 2], I32)
        ids = sb("ids", [P, 3, 2, 2], I32)
        ovf_cmp = kT[:].rearrange("p b h t -> p (b h t)")[:, 0:NOVF * NE].rearrange("p (o e) -> p o e", o=NOVF)
        ovf_ef = sb("ovf_ef", [P, NOVF + 1])
        ovf_e = sb("ovf_e", [P, NOVF + 1], I32)
        slots = sb("slots", [CAP, NITEM, 2], I32)
        idx_in = sb("idx_in", [CAP, 1], I32)
        idx_out = sb("idx_out", [CAP, 1], I32)

        def c_(name, rows=P):
            o, w = CONSTS[name]
            return cst[0:rows, o:o + w]

        ident = c_("ident")
        ps = ctx.enter_context(nc.psum_tensor("ps", [P, 8, 512], F32))

        def score_parts(b):
            for c, (w, at, wide) in enumerate(((0, 0, P), (1, 0, P), (0, 1, 2 * P), (1, 1, 2 * P), (0, 0, NCB), (1, 0, NCB))):
                src = (2 * P if c >= 4 else 0) + w * wide
                dst = (0, 2 * P, 6 * P)[c // 2] + w * wide
                yield ps[:, 2 * b + at, src:src + wide], pr[:, b, dst:dst + wide], c

        def kv_heads(eng, chain, heads):
            def body(kh):
                heads(kh, isinstance(kh, int) and kh == KVH - 1)

            loop(eng, chain, KVH, body, last=True)

        S = {}
        for n in ("x_in consts_in small_in_in w_aux_in w1_in wbr_in ln_in ws_in ptab_in "
                  "page_in0 page_in1 page_in2 page_in3 kx_in0 kx_in1 vx_in0 vx_in1 gate_out gate_in h2_out slot_fill_out slot_out slots_in yp_in0 yp_in1 yp_in2 "
                  "stores_a stores_g stores_s "
                  "w_in0 w_in1 w_in2 w_in3 w_used "
                  "dve_chain pe_passed dve_passed pool_passed sp_passed "
                  "squares rstd_sq normed tp_full tp_free "
                  "kv_ev_act kv_ev_dve br_full br_done gates_done roped kT_ready "
                  "page_T page_ev cmp_hid_full cmp_hid kc_full kc_ready vc_full vc_ready "
                  "q_ev_act q_ev_dve rot_full rot_done q_ready "
                  "q_staged v_staged s_full sc_ready p_exp p_ready pt_full pt_act pt_dve pv_done o_ev "
                  "kx_ev vcs_full vcs_ev o_rows oT_full qp_ready t_full tsc_ready tp_exp tp_ready tpt_full tpt_act tpt_dve tpv_done to_ev "
                  "pool_init v_ev v_ready u_ev sp_full sp_done "
                  "ws_masked w_hi w_lo x_hi x_lo m_ev_act m_ev_dve wo_ev zsq lg_full lg_done rank_full rank_done "
                  "ids_ready slots_rdy xg_in xt_done xgh_done xgT_ready hg_done hid_done ht_done hidTh_done hidT_ready "
                  "y_act y_dve y_out piece_in0 piece_in1 piece_in2 piece_in3 piece_in4 piece_in5 hi_done lo_done piece_used "
                  "idx_ready out_idx_ready gain_in o_idx o_xg o_w o_xt o_xgh o_xgT o_hg o_hid o_ht o_hidTh o_hidT o_hi o_lo o_used o_ya o_free o_yout "
                  "x2_done fin_ready init_done dve_init kxT_full").split():
            S[n] = sem(n)
        s = type("Sems", (), S)

        w_view = a["w_in"].rearrange("l (k p) c -> p (l k) c", p=P)
        block = ctx.enter_context(nc.Block())

        N_STORES_KV = 6 + 4 + 2 * DB
        N_STORES_A = N_STORES_KV + 1
        KV_IT, Q_IT, V_IT, U_IT, M_IT, O_IT = 6, 4, 4, 4, 8, 4
        IT_Q = KV_IT
        IT_V = IT_Q + Q_IT
        IT_U = IT_V + V_IT
        IT_M = IT_U + U_IT
        IT_O = IT_M + 2 * M_IT
        IT_END = IT_O + O_IT

        N_SPLIT = 2 * M_IT + O_IT
        S_Q, S_V, S_U, S_M = (4 * n for n in (KV_IT, KV_IT + Q_IT, KV_IT + Q_IT + V_IT, KV_IT + Q_IT + V_IT + U_IT))

        def hi_slots(n, out_turns):
            return out_hi if out_turns or (isinstance(n, int) and n >= 2 * M_IT) else ring_hi

        def chunk_done(it, b):
            return it * 4 + (2 * b + 2)

        def load_x(eng):
            for t in range(2):
                eng.dma_start(xt[:, t, :], a["x_prompt"][0, t * P:(t + 1) * P, :]).then_inc(s.x_in, 16)
            eng.dma_start(xt[0:NS, 2, :], a["x_sample"].rearrange("b t d -> (b t) d")).then_inc(s.x_in, 16)

        w_sems = [s.w_in0, s.w_in1, s.w_in2, s.w_in3]
        piece_sems = [s.piece_in0, s.piece_in1, s.piece_in2, s.piece_in3, s.piece_in4, s.piece_in5]
        page_sems = [s.page_in0, s.page_in1, s.page_in2, s.page_in3]
        kx_sems, vx_sems = [s.kx_in0, s.kx_in1], [s.vx_in0, s.vx_in1]

        @block.sync
        def _(sp):
            load_x(sp)

            def load(it, u, src, col):
                if not isinstance(it, int) or it > 0:
                    apart(sp, s.w_used, it * 4 + (u - 3), s.sp_passed)
                h = u % 2
                sp.dma_start(ring[:, u], src[:, 8 * h:8 * h + 8, ds(col, 256)]).then_inc(w_sems[u], 16)

            def stream(first, count, src, col0):
                def body(it):
                    for u in range(4):
                        load(it, u, src, (it - first) * 512 + (col0 + 256 * (u // 2)))
                if first == 0:
                    body(0)
                with sp.Fori(max(first, 1), first + count) as it:
                    body(it)

            wv = {n: a[n].rearrange("l (k p) c -> p (l k) c", p=P) for n in ("w_pa", "w_pb", "w_o")}
            stream(0, KV_IT, w_view, C_KV)
            stream(IT_Q, Q_IT, w_view, C_Q)
            stream(IT_V, V_IT, w_view, C_V)
            stream(IT_U, U_IT, w_view, C_U)
            for first, g_col, w_p in ((0, C_GA, "w_pa"), (M_IT, C_GB, "w_pb")):
                with sp.Fori(0, M_IT) as c:
                    it = c + (IT_M + first)
                    for u in range(2):
                        load(it, u, w_view, c * 256 + g_col)
                    for u in range(2, 4):
                        load(it, u, wv[w_p], c * 256)
            stream(IT_O, O_IT, wv["w_o"], 0)

            wg = a["w_gate"].rearrange("l e (k p) f -> p (l e) k f", p=P)
            wu = a["w_up"].rearrange("l e (k p) f -> p (l e) k f", p=P)
            wd = a["w_down"].rearrange("l e (f p) d -> p (l e) f d", p=P)

            def load_piece(e, q, done):
                if q < 4:
                    st = staging[q].rearrange("p (k c) -> p k c", k=4)
                    for c, view in enumerate((wg, wu)):
                        sp.dma_start(st[:, :, c * ED:(c + 1) * ED],
                                     view[:, ds(e, 1), 4 * q:4 * q + 4].rearrange("p a k f -> p (a k) f")).then_inc(done, 16)
                else:
                    sp.dma_start(staging[q], wd[:, ds(e, 1), q - 4].rearrange("p a f -> p (a f)")).then_inc(done, 16)

            sp.wait_ge(s.m_ev_dve, 2 * M_IT)
            sp.wait_ge(s.stores_a, 16 * N_STORES_A)

            sp.dma_start(g_ffn, a["g_ffn"][0].partition_broadcast(P)).then_inc(s.gain_in, 16)
            for q in range(4):
                load_piece(0, q, piece_sems[q])
            sp.wait_ge(s.w_used, 4 * IT_END)
            for q in range(4, 6):
                load_piece(0, q, piece_sems[q])

            def experts(j):
                for b in range(2):
                    e = j * 2 + b
                    for q in range(6):
                        last = isinstance(e, int) and e == NE - 1
                        if q < 4 and last or q >= 4 and isinstance(e, int) and e == 0:
                            continue
                        if isinstance(e, int) and e == 0:
                            apart(sp, s.lo_done, q + 1, s.sp_passed)
                        else:
                            apart(sp, s.lo_done, before(e - 1, q) + 1, s.sp_passed)
                        load_piece(e + (1 if q < 4 else 0), q, piece_sems[q])

            loop(sp, None, NE // 2, experts, last=True)

            sp.wait_ge(s.slots_rdy, 1)
            n_ovf = sp.value_load(ovf_e[0:1, NOVF:NOVF + 1], min_val=0, max_val=NOVF)
            with sp.If(n_ovf > 0):
                with sp.Fori(0, n_ovf) as o:
                    apart(sp, s.o_free, o + 1, s.sp_passed)
                    e = sp.value_load(ovf_e[0:1, ds(o, 1)], min_val=0, max_val=NE - 1)
                    for q in range(6):
                        load_piece(e, q, s.o_w)

            yp_sems = [s.yp_in0, s.yp_in1, s.yp_in2]
            sp.wait_ge(s.pool_init, 3)
            for t in range(3):
                for k in range(2):
                    r = ROWS[t]
                    sp.dma_start(yp[2 * t + k][0:r], ypair_d[k * TOK + t * P:k * TOK + t * P + r, :]).then_inc(yp_sems[t], 16)
                if t == 0:
                    sp.dma_start(gfin, a["g_final"].partition_broadcast(P)).then_inc(s.gain_in, 16)
            for t in range(3):
                sp.wait_ge(s.fin_ready, t + 1)
                dst = y_prompt[0, t * P:(t + 1) * P, :] if t < 2 else y_sample.rearrange("b t d -> (b t) d")
                sp.dma_start(dst, fin[t][0:ROWS[t]]).then_inc(s.stores_s, 16)
            sp.wait_ge(s.stores_s, 48)
            sp.wait_ge(s.stores_a, 16 * N_STORES_A)
            sp.wait_ge(s.stores_g, 32)

        @block.gpsimd
        def _(pool):
            nc.gpsimd.memset(slots[:], NOWHERE).then_inc(s.init_done, 1)
            pool.dma_start(ptab[:], a["page_table"].rearrange("b n -> (b n)").rearrange("(o n) -> o n", o=1)).then_inc(s.ptab_in, 16)
            pool.wait_ge(s.init_done, 1)
            pool.dma_start(slot_d.rearrange("(c i) k -> c i k", c=CAP), slots[:]).then_inc(s.slot_fill_out, 16)
            pool.wait_ge(s.ptab_in, 16)

            pool.wait_ge(s.normed, 3)
            for n, cache in enumerate(("cache_k_cmp", "cache_v_cmp")):
                rows = a[cache].rearrange("l n t h d -> t (l n) (h d)")

                def pages(i, n=n, rows=rows):
                    for b in range(4):
                        k = n * PAGES + i * 4 + b
                        apart(pool, s.page_T, k - 3, s.pool_passed)
                        page = pool.value_load(ptab[0:1, ds(i * 4 + b, 1)], min_val=0, max_val=a[cache].shape[1] - 1)
                        pool.dma_start(page_rows[:, b], rows[:, ds(page, 1)].rearrange("p a c -> p (a c)")).then_inc(page_sems[b], 16)

                loop(pool, None, PAGES // 4, pages)

            ks = a["cache_k_slc"].rearrange("l n t h d -> t (l n) (h d)")
            vs = a["cache_v_slc"].rearrange("l n t h d -> t (l n) (h d)")
            kw = a["state_k_win"].rearrange("l b (u t) h d -> t (l b) u (h d)", t=P)
            vw = a["state_v_win"].rearrange("l b (u t) h d -> t (l b) u (h d)", t=P)
            pool.wait_ge(s.cmp_hid, 2)
            for src, dst in ((a["state_k_win"], o_kws), (a["state_v_win"], o_vws)):
                pool.dma_start(dst[0, :, 0:PAST - DT], src[0, :, DT:PAST]).then_inc(s.stores_g, 16)

            pool.wait_ge(s.w_used, 4 * (KV_IT + Q_IT))

            def sequences(i):
                for b in range(2):
                    n = i * 2 + b
                    pages = [pool.value_load(ptab[0:1, ds(i * 4 + (2 * b + u), 1)], min_val=0, max_val=a["cache_k_slc"].shape[1] - 1)
                             for u in range(2)]
                    apart(pool, s.kxT_full, i * 8 + 4 * (b - 1), s.pool_passed)
                    for u in range(2):
                        pool.dma_start(kx[:, b, u], ks[:, ds(pages[u], 1)].rearrange("p a c -> p (a c)")).then_inc(kx_sems[b], 16)
                    pool.dma_start(kx[:, b, 2:4], kw[:, ds(n, 1)].rearrange("p a u c -> p (a u) c")).then_inc(kx_sems[b], 16)
                    apart(pool, s.tpv_done, i * 2 + (b - 1), s.pool_passed)
                    for u in range(2):
                        pool.dma_start(vx[:, b, u], vs[:, ds(pages[u], 1)].rearrange("p a c -> p (a c)")).then_inc(vx_sems[b], 16)
                    pool.dma_start(vx[:, b, 2:4], vw[:, ds(n, 1)].rearrange("p a u c -> p (a u) c")).then_inc(vx_sems[b], 16)

            loop(pool, None, DB // 2, sequences)

            pool.wait_ge(s.tpv_done, DB)
            pool.wait_ge(s.stores_a, 16 * N_STORES_KV)
            nc.gpsimd.memset(wss_raw, 0.0).then_inc(s.pool_init, 1)
            pool.dma_start(ws_raw, a["a_w_s"][0].rearrange("g i j -> i g j")).then_inc(s.ws_in, 16)
            pool.wait_ge(s.pool_init, 1)
            for b in range(DB):
                r = slice(DT * b, DT * b + DT)
                pool.dma_start(wss_raw[r, :, r], a["a_w_s"][0, :, 0:DT, 0:DT].rearrange("g i j -> i g j")).then_inc(s.ws_in, 16)
            for t in range(2):
                pool.dma_start(sbias[:, :, t * P:(t + 1) * P], a["a_b_s"][0].partition_broadcast(P)).then_inc(s.ln_in, 16)
            for b in range(DB):
                pool.dma_start(sbias[:, :, SEQ + DT * b:SEQ + DT * b + DT], a["a_b_s"][0, :, 0:DT].partition_broadcast(P)).then_inc(s.ln_in, 16)
            pool.dma_start(ln_g, a["a_ln_g"][0].partition_broadcast(P)).then_inc(s.ln_in, 16)
            pool.dma_start(ln_b, a["a_ln_b"][0].partition_broadcast(P)).then_inc(s.ln_in, 16)
            pool.wait_ge(s.ws_in, 16 * (1 + DB))
            nc.gpsimd.affine_select(out=ws_raw, in_=ws_raw, compare_op=ALU.is_ge, fill=0.0, base=0,
                                    pattern=[[0, AG], [-1, P]], channel_multiplier=1).then_inc(s.ws_masked, 1)
            nc.gpsimd.affine_select(out=wss_raw, in_=wss_raw, compare_op=ALU.is_ge, fill=0.0, base=0,
                                    pattern=[[0, AG], [-1, NS]], channel_multiplier=1).then_inc(s.ws_masked, 1)

            pool.wait_ge(s.normed, 6)
            nc.gpsimd.memset(xg, 0.0).then_inc(s.pool_init, 1)
            pool.wait_ge(s.ids_ready, 1)
            pool.wait_ge(s.slot_fill_out, 16)
            for t in range(3):
                for k in range(2):
                    pool.indirect_dma_start(out=slot_d, out_offset=bass.IndirectOffsetOnAxis(ap=sloti[0:ROWS[t], t, k:k + 1], axis=0),
                                            in_=ids[0:ROWS[t], t, k, :], in_offset=None).then_inc(s.slot_out, 16)
            pool.wait_ge(s.slot_out, 96)
            pool.dma_start(slots[:], slot_d.rearrange("(i c) k -> c i k", c=CAP)).then_inc(s.slots_in, 16)
            pool.wait_ge(s.slots_in, 16)
            pool.wait_ge(s.h2_out, 48)
            pool.wait_ge(s.pool_init, 2)

            def fetch(item, copied, n, arrived):
                nc.gpsimd.tensor_copy(idx_in[:], slots[:, ds(item, 1), 0:1].rearrange("p a k -> p (a k)")).then_inc(copied, 1)
                apart(pool, copied, n, s.pool_passed)
                pool.indirect_dma_start(out=xg, out_offset=None, in_=h2_d,
                                        in_offset=bass.IndirectOffsetOnAxis(ap=idx_in[:, 0:1], axis=0),
                                        bounds_check=TOK - 1, oob_is_err=False).then_inc(arrived, 16)

            def scatter(item, copied, n, done):
                nc.gpsimd.tensor_copy(idx_out[:], slots[:, ds(item, 1), 1:2].rearrange("p a k -> p (a k)")).then_inc(copied, 1)
                apart(pool, copied, n, s.pool_passed)
                pool.indirect_dma_start(out=ypair_d, out_offset=bass.IndirectOffsetOnAxis(ap=idx_out[:, 0:1], axis=0),
                                        in_=y_sb, in_offset=None,
                                        bounds_check=2 * TOK - 1, oob_is_err=False).then_inc(done, 16)

            fetch(0, s.idx_ready, 1, s.xg_in)
            pool.wait_ge(s.xg_in, 16)
            pool.wait_ge(s.xt_done, 1)
            fetch(1, s.idx_ready, 2, s.xg_in)

            def items(j):
                for b in range(2):
                    e = j * 2 + b
                    if not (isinstance(e, int) and e >= NE - 2):
                        apart(pool, s.xg_in, (e + 2) * 16, s.pool_passed)
                        apart(pool, s.xt_done, e + 2, s.pool_passed)
                        fetch(e + 2, s.idx_ready, e + 3, s.xg_in)
                    if not (isinstance(e, int) and e == 0):
                        y_rows_out(e - 1)

            def y_rows_out(e):
                apart(pool, s.y_out, e * 16, s.pool_passed)
                apart(pool, s.y_act, e + 1, s.pool_passed)
                apart(pool, s.y_dve, e + 1, s.pool_passed)
                scatter(e, s.out_idx_ready, e + 1, s.y_out)

            loop(pool, None, NE // 2, items, last=True)
            y_rows_out(NE - 1)
            pool.wait_ge(s.y_out, 16 * NE)

            n_ovf = pool.value_load(ovf_e[0:1, NOVF:NOVF + 1], min_val=0, max_val=NOVF)
            with pool.If(n_ovf > 0):
                with pool.Fori(0, n_ovf) as o:
                    fetch(o + NE, s.o_idx, o * 2 + 1, s.o_xg)
                    apart(pool, s.o_ya, o + 1, s.pool_passed)
                    scatter(o + NE, s.o_idx, o * 2 + 2, s.o_yout)
                    apart(pool, s.o_yout, (o + 1) * 16, s.pool_passed)
            pool.sem_inc(s.pool_init, 1)

        @block.scalar
        def _(act):
            A = nc.scalar.activation
            act.dma_start(cst[:], a["consts"]).then_inc(s.consts_in, 16)
            act.dma_start(small_in[0:KT, 0], a["g_mix"][0].rearrange("(k p) -> k p", p=P)).then_inc(s.small_in_in, 16)
            act.dma_start(small_in[:, 1], a["cmp_pe_k"][0]).then_inc(s.small_in_in, 16)
            act.dma_start(small_in[:, 2], a["cmp_pe_v"][0]).then_inc(s.small_in_in, 16)
            act.dma_start(w2[:, 0], a["cmp_w2_k"][0]).then_inc(s.w_aux_in, 16)
            act.dma_start(w2[:, 1], a["cmp_w2_v"][0]).then_inc(s.w_aux_in, 16)
            act.dma_start(wr[:, :, 0:NG], a["w_rg"][0].rearrange("(k p) g -> p k g", p=P)).then_inc(s.w_aux_in, 16)
            act.dma_start(wr[:, :, NG:], a["w_re"][0].rearrange("(k p) g -> p k g", p=P)).then_inc(s.w_aux_in, 16)
            act.dma_start(rb[:, 0:NG], a["b_rg"][0].partition_broadcast(P)).then_inc(s.w_aux_in, 16)
            act.dma_start(rb[:, NG:], a["b_re"][0].partition_broadcast(P)).then_inc(s.w_aux_in, 16)

            def sum_squares(which, t, wait_sem, value):
                if wait_sem is not None:
                    act.wait_ge(wait_sem, value)
                after(act, s.squares, 3 * which + t)
                A(squares_at[which][0:ROWS[t]], xt[0:ROWS[t], t, :], ACT.Square, accum_out=ss[0:ROWS[t], t:t + 1]).then_inc(s.squares, 1)

            act.wait_ge(s.x_in, 48)
            act.wait_ge(s.dve_init, 1)
            for t in range(3):
                sum_squares(0, t, None, 0)
            act.wait_ge(s.squares, 3)
            A(rstd[:], ss[:], ACT.Sqrt, bias=epsb[:, 0:1], scale=1.0 / D).then_inc(s.rstd_sq, 1)

            act.wait_ge(s.normed, 3)
            act.dma_start(wbr, w_view[:, :, C_BR:C_BR + 48]).then_inc(s.wbr_in, 16)

            def round_slot(slots, u, arrived):
                act.wait_ge(w_sems[u], arrived)
                for k0, hi in slots[u]:
                    ins = nc.scalar.copy(hi[:], ring[:, u, k0:k0 + hi.shape[1]])
                ins.then_inc(s.w_hi, 1)

            for t in range(3):
                act.wait_ge(s.tp_free, 3 + 4 * (t + 1))
                rows = slice(t * P, t * P + ROWS[t])
                nc.scalar.copy(hkv_hi[:, :, rows], hT[:, :, rows]).then_inc(s.x_hi, 1)
            for u in range(4):
                round_slot(ring_hi, u, 16)

            def kv_even(i):
                more = not (isinstance(i, int) and i == KV_IT - 1)
                if more:
                    round_slot(ring_hi, 0, i * 16 + 32)
                    round_slot(ring_hi, 1, i * 16 + 32)
                act.wait_ge(s.w_used, chunk_done(i, 0))
                nc.scalar.copy(kv[:, 0:2, ds(i * 512, 256)], ps[:, 0:2, 0:256])
                nc.scalar.copy(kv[0:NS, 2, ds(i * 512, 256)], ps[0:NS, 2, 0:256]).then_inc(s.kv_ev_act, 1)
                if more:
                    round_slot(ring_hi, 2, i * 16 + 32)
                    round_slot(ring_hi, 3, i * 16 + 32)

            loop(act, None, KV_IT, kv_even, last=True)
            act.wait_ge(s.w_used, 4 * KV_IT)
            act.dma_start(w1, a["cmp_w1_k"][0].rearrange("j d e -> d j e")).then_inc(s.w1_in, 16)
            act.wait_ge(s.br_full, 1)
            act.wait_ge(s.dve_init, 2)
            for t in range(3):
                r = ROWS[t]
                for c, src in enumerate((1, 2, 0)):
                    A(gbr[0:r, t, :, c], ps[0:r, 6, t * 48:(t + 1) * 48].rearrange("p (h c) -> p h c", c=3)[:, :, src], ACT.Sigmoid).then_inc(s.br_done, 1)
            act.wait_ge(s.roped, 1)
            for br, (op, os) in enumerate(((o_kcp, o_kcs), (o_vcp, o_vcs), (o_ksp, o_kss), (o_vsp, o_vss), (o_kwp, None), (o_vwp, None))):
                act.dma_start(op[0, 0].rearrange("(t p) h d -> p t (h d)", p=P), kv[:, 0:2, br * KVC:(br + 1) * KVC]).then_inc(s.stores_a, 16)
                if os is not None:
                    act.dma_start(os[0].rearrange("b t h d -> (b t) (h d)"), kv[0:NS, 2, br * KVC:(br + 1) * KVC]).then_inc(s.stores_a, 16)
                else:
                    dst = (o_kws, o_vws)[br - 4]
                    for b in range(DB):
                        act.dma_start(dst[0, b, PAST - DT:PAST].rearrange("t h d -> t (h d)"),
                                      kv[b * DT:(b + 1) * DT, 2, br * KVC:(br + 1) * KVC]).then_inc(s.stores_a, 16)
            act.wait_ge(s.gates_done, 1)
            act.dma_start(gate_d, gbr[0:NS, 2].rearrange("p h c -> p (h c)")).then_inc(s.gate_out, 16)
            act.wait_ge(s.gate_out, 16)
            for h in range(NH):
                act.dma_start(gsm[h * DT:(h + 1) * DT], gate_d.rearrange("(b t) (h c) -> t b h c", t=DT, c=3)[:, :, h, :]).then_inc(s.gate_in, 16)

            for n in range(2):
                act.wait_ge(s.cmp_hid_full, n + 1)
                if n == 0:
                    act.dma_start(w1, a["cmp_w1_v"][0].rearrange("j d e -> d j e")).then_inc(s.w1_in, 16)
                src = ps[:, n, 0:288].rearrange("p (s g h k) -> p s g h k", s=NSEQ, g=2, h=KVH)
                dst = hidcT[:, n].rearrange("p (s h g k) -> p s g h k", s=NSEQ, g=2, h=KVH)
                A(dst[:, :, 0], src[:, :, 0], ACT.Gelu_apprx_tanh)
                A(dst[:, :, 1], src[:, :, 1], ACT.Gelu_apprx_tanh).then_inc(s.cmp_hid, 1)

            def x_rounded(hi, src, half):
                k = slice(HALF_K * half, HALF_K * (half + 1))
                nc.scalar.copy(hi[:, k], src[:, k]).then_inc(s.x_hi, 1)

            act.wait_ge(s.cmp_hid, 2)
            for half in range(2):
                x_rounded(hq_hi, hT, half)
                round_slot(ring_hi, half, 16 * (IT_Q + 1))
            round_slot(ring_hi, 2, 16 * (IT_Q + 1))
            round_slot(ring_hi, 3, 16 * (IT_Q + 1))

            def q_even(i):
                more = not (isinstance(i, int) and i == Q_IT - 1)
                if more:
                    round_slot(ring_hi, 0, i * 16 + 16 * (IT_Q + 2))
                    round_slot(ring_hi, 1, i * 16 + 16 * (IT_Q + 2))
                act.wait_ge(s.w_used, chunk_done(i + IT_Q, 0))
                nc.scalar.copy(qT[:, ds(i * 4, 2), :], ps[:, 0:2, 0:TOK]).then_inc(s.q_ev_act, 1)
                if more:
                    round_slot(ring_hi, 2, i * 16 + 16 * (IT_Q + 2))
                    round_slot(ring_hi, 3, i * 16 + 16 * (IT_Q + 2))

            loop(act, None, Q_IT, q_even, last=True)

            def exps(n, b):
                act.wait_ge(s.sc_ready, n + 1)
                after(act, s.pt_full, n - 1)
                for in_, out, c in score_parts(b):
                    ins = A(out, in_, ACT.Exp, scale=SCALE, bias=stt[:, b, 6 + c:7 + c], accum_out=stt[:, b, 12 + c:13 + c])
                ins.then_inc(s.p_exp, 1)

            def heads(kh, last):
                for g in range(GQ):
                    n = kh * GQ + g
                    if not (last and g == GQ - 1):
                        exps(n + 1, (g + 1) % 2)
                    act.wait_ge(s.pt_full, n + 1)
                    after(act, s.pv_done, n)
                    nc.scalar.copy(pT[:, 0:4 * P], ps[:, 4]).then_inc(s.pt_act, 1)

            exps(0, 0)
            kv_heads(act, None, heads)

            def keys_left(n, h):
                act.wait_ge(s.kxT_full, n * 4 + (h + 1))
                nc.scalar.copy(kxT[:, h], ps[:, 6 + h % 2]).then_inc(s.kx_ev, 1)

            for h in range(KVH):
                keys_left(0, h)

            def sample(i):
                for b in range(2):
                    n = i * 2 + b
                    more = not (isinstance(n, int) and n == DB - 1)
                    act.wait_ge(s.t_full, n + 1)
                    if more:
                        for h in range(3):
                            keys_left(n + 1, h)
                    act.wait_ge(s.tsc_ready, n + 1)
                    after(act, s.tpt_full, n)
                    st = stt[0:64, 0]
                    for c, (in_, out) in enumerate(((ps[0:64, 0, 0:288], tpr[:, 0:288]), (ps[0:64, 1, 0:288], tpr[:, 288:576]),
                                                    (ps[0:64, 0, 288:296], tpr[:, 576:584]))):
                        ins = A(out, in_, ACT.Exp, scale=SCALE, bias=st[:, 3 + c:4 + c], accum_out=st[:, 6 + c:7 + c])
                    ins.then_inc(s.tp_exp, 1)
                    if more:
                        keys_left(n + 1, 3)
                    act.wait_ge(s.tpt_full, n + 1)
                    after(act, s.tpv_done, n)
                    nc.scalar.copy(tpT, ps[:, 2, 0:256]).then_inc(s.tpt_act, 1)

            loop(act, None, DB // 2, sample, last=True)

            def round_ahead(it, b, r):
                act.wait_ge(s.w_used, it * 4 + (2 * b + 1 + r))
                round_slot(vu_hi, (2 * b + 2 + r) % 4, it * 16 + 16 * (b + 1))

            act.wait_ge(s.oT_full, DB)
            act.wait_ge(s.o_rows, DB)
            for half in range(2):
                x_rounded(h_hi, hT, half)
                round_slot(vu_hi, half, 16 * (IT_V + 1))

            def v_act(i):
                for b in range(2):
                    round_ahead(i + IT_V, b, 0)
                    act.wait_ge(s.w_used, chunk_done(i + IT_V, b))
                    A(v_tok[:, 0:2, ds(i * 512 + b * 256, 256)], ps[:, 3 * b:3 * b + 2, 0:256], ACT.Gelu_apprx_tanh)
                    A(v_tok[0:NS, 2, ds(i * 512 + b * 256, 256)], ps[0:NS, 3 * b + 2, 0:256], ACT.Gelu_apprx_tanh).then_inc(s.v_ev, 1)
                    round_ahead(i + IT_V, b, 1)

            loop(act, None, V_IT, v_act)
            act.wait_ge(s.rstd_sq, 2)
            A(rstd[:], mv[:, :, 1], ACT.Sqrt, bias=epsb[:, 0:1]).then_inc(s.rstd_sq, 1)

            def u_act(i):
                for b in range(2):
                    more = not (isinstance(i, int) and i == U_IT - 1 and b == 1)
                    if more:
                        round_ahead(i + IT_U, b, 0)
                    act.wait_ge(s.w_used, chunk_done(i + IT_U, b))
                    A(uT[:, ds(i * 4 + 2 * b, 2), :], ps[:, 3 * b:3 * b + 2, 0:TOK], ACT.Gelu_apprx_tanh).then_inc(s.u_ev, 1)
                    if more:
                        round_ahead(i + IT_U, b, 1)

            loop(act, None, U_IT, u_act, last=True)
            act.wait_ge(s.v_ready, 1)
            act.dma_start(o_vchunk[0].rearrange("b t c -> (b t) c"), v_tok[0:NS, 2, :]).then_inc(s.stores_a, 16)

            def w_rounded(n, u, out_turns=False):
                if isinstance(n, int) and n == N_SPLIT:
                    return
                round_slot(hi_slots(n, out_turns), u, n * 16 + (IT_M + 1) * 16)

            act.wait_ge(s.sp_done, KT)
            act.wait_ge(s.stores_a, 16 * N_STORES_A)
            w_rounded(0, 0)
            w_rounded(0, 1)
            for half in range(2):
                x_rounded(u_hi, uT, half)
                w_rounded(0, 2 + half)

            def gates(first):
                def body(j):
                    for b in range(2):
                        n = j * 2 + (first + b)
                        last = isinstance(n, int) and n == 2 * M_IT - 1
                        w_rounded(n + 1, 0)
                        w_rounded(n + 1, 1)
                        act.wait_ge(s.w_used, chunk_done(n + IT_M, 0))
                        after(act, s.m_ev_dve, n - 1)
                        A(sig[:, b], ps[:, 0:2, 0:TOK], ACT.Sigmoid).then_inc(s.m_ev_act, 1)
                        if last:
                            act.wait_ge(s.m_ev_dve, 2 * M_IT)
                            load_x(act)
                            for half in range(2):
                                x_rounded(m_hi, mT, half)
                        w_rounded(n + 1, 2)
                        w_rounded(n + 1, 3)
                return body

            loop(act, None, M_IT // 2, gates(0))
            act.wait_ge(s.w_used, chunk_done(IT_M + M_IT - 1, 1))
            for half in range(2):
                x_rounded(q_hi, qT, half)
            loop(act, None, M_IT // 2, gates(M_IT), last=True)

            def w_o_rounded(i):
                for u in range(4):
                    w_rounded(i + 2 * M_IT + 1, u, True)

            loop(act, None, O_IT, w_o_rounded, last=True)

            for t in range(3):
                sum_squares(1, t, s.wo_ev, 2 * O_IT)
            act.wait_ge(s.squares, 6)
            A(rstd[:], ss[:], ACT.Sqrt, bias=epsb[:, 0:1], scale=1.0 / D).then_inc(s.rstd_sq, 1)
            def round_weights(slot, q, arrived, n, done):
                act.wait_ge(arrived, n)
                nc.scalar.copy(split[slot][:, 0], staging[q]).then_inc(done, 1)

            act.wait_ge(s.w_used, 4 * IT_END)
            round_weights(0, 0, piece_sems[0], 32, s.hi_done)
            round_weights(1, 1, piece_sems[1], 32, s.hi_done)
            for t in range(3):
                act.wait_ge(s.normed, 3 + t + 1)
                act.dma_start(h2_d[t * P:t * P + ROWS[t], :], hn_at[1][t][0:ROWS[t]]).then_inc(s.h2_out, 16)
            act.wait_ge(s.zsq, 1)
            for t in range(3):
                A(g8[:, t, 0:NG], lg[:, t, 0:NG], ACT.Exp, bias=rs[:, 0, t:t + 1], accum_out=rs[:, 1, t:t + 1]).then_inc(s.lg_done, 1)
            act.wait_ge(s.zsq, 2)
            A(rs[:, 3], rs[:, 2], ACT.Exp).then_inc(s.lg_done, 1)

            def piece_hi(e, b, q):
                if q > 5:
                    e, b, q = e + 1, 1 - b, q - 6
                if isinstance(e, int) and (e == NE or (e == NE - 1 and q < 4)):
                    return
                n = before(e, q)
                act.wait_ge(s.piece_used, n - 3)
                round_weights((6 * b + q) % 4, q, piece_sems[q], (e + 2) * 32 if q < 4 else (e + 1) * 16, s.hi_done)

            def rows_hi(b, full, n, done):
                act.wait_ge(full, n)
                nc.scalar.copy(xgT[b][:, 0, 0:KT * CAP].rearrange("p (n c) -> p n c", n=2), ps[:, 0:2, 0:8 * CAP]).then_inc(done, 1)

            def hidT_hi(bank, full, n, done):
                act.wait_ge(full, n)
                nc.scalar.copy(hidT[:, 0, 0:2 * CAP], ps[:, bank, 0:2 * CAP]).then_inc(done, 1)

            def y_left(e):
                act.wait_ge(s.piece_used, before(e, 5) + 1)
                after(act, s.y_out, e * 16)
                nc.scalar.copy(y_sb[:, 0:1024].rearrange("p (n c) -> p n c", n=2), ps[0:CAP, 4:6]).then_inc(s.y_act, 1)

            act.wait_ge(s.h2_out, 48)
            act.wait_ge(s.lg_full, 3)
            round_weights(2, 2, piece_sems[2], 32, s.hi_done)
            round_weights(3, 3, piece_sems[3], 32, s.hi_done)
            rows_hi(0, s.xt_done, 1, s.xgh_done)
            piece_hi(0, 0, 0)
            piece_hi(0, 0, 1)
            rows_hi(1, s.xt_done, 2, s.xgh_done)

            def item(j):
                for b in range(2):
                    e = j * 2 + b
                    first = isinstance(e, int) and e == 0
                    act.wait_ge(s.piece_used, 4 if first else e * 6 + 2)
                    after(act, s.hid_done, e)
                    A(hgate, ps[0:CAP, 2 + b, 0:ED], ACT.Silu).then_inc(s.hg_done, 1)
                    piece_hi(e, b, 2)
                    piece_hi(e, b, 3)
                    if not first:
                        y_left(e - 1)
                    piece_hi(e, b, 4)
                    piece_hi(e, b, 5)
                    piece_hi(e, b, 6)
                    after(act, s.piece_used, e * 6)
                    hidT_hi(2 + b, s.ht_done, e + 1, s.hidTh_done)
                    if not (isinstance(e, int) and e >= NE - 2):
                        rows_hi(b, s.xt_done, e + 3, s.xgh_done)
                    piece_hi(e, b, 7)

            loop(act, None, NE // 2, item, last=True)
            y_left(NE - 1)
            n_ovf = act.value_load(ovf_e[0:1, NOVF:NOVF + 1], min_val=0, max_val=NOVF)
            with act.If(n_ovf > 0):
                with act.Fori(0, n_ovf) as o:
                    rows_hi(0, s.o_xt, o + 1, s.o_xgh)
                    for q in range(6):
                        if q >= 4:
                            act.wait_ge(s.o_used, o * 6 + (q - 3))
                        round_weights(q % 4, q, s.o_w, (o + 1) * 160, s.o_hi)
                    act.wait_ge(s.o_used, o * 6 + 4)
                    A(hgate, ps[0:CAP, 2, 0:ED], ACT.Silu).then_inc(s.o_hg, 1)
                    hidT_hi(2, s.o_ht, o + 1, s.o_hidTh)
                    act.wait_ge(s.o_used, o * 6 + 6)
                    nc.scalar.copy(y_sb.rearrange("p (n c) -> p n c", n=4), ps[0:CAP, 4:8]).then_inc(s.o_ya, 1)
            for t in range(3):
                act.wait_ge(s.x2_done, t + 1)
                sum_squares(2, t, None, 0)
                act.wait_ge(s.squares, 6 + t + 1)
                A(rstd[:, t:t + 1], ss[:, t:t + 1], ACT.Sqrt, bias=epsb[:, 0:1], scale=1.0 / D).then_inc(s.rstd_sq, 1)

        @block.vector
        def _(dve):
            ch = Chain(dve, s.dve_chain)
            V = nc.vector
            link = ch.link
            V.memset(epsb[:], EPS)
            V.memset(ss[:], 1.0).then_inc(s.dve_init, 1)
            V.memset(gbr[:], 0.0).then_inc(s.dve_init, 1)
            V.memset(lg[:], 0.0)
            V.memset(mv[:], 1.0)
            V.memset(posn[:], 0.0)
            link(V.memset(g8[:], NEG))
            tp = [0]

            def evac(out, in_, gain=None):
                dve.wait_ge(s.tp_full, tp[0] + 1)
                bank = 6 + tp[0] % 2
                src = in_(ps[:, bank])
                if gain is None:
                    V.tensor_copy(out, src).then_inc(s.tp_free, 1)
                else:
                    V.tensor_tensor(out, src, gain, ALU.mult).then_inc(s.tp_free, 1)
                tp[0] += 1

            evac(gT[:], lambda p: p[:, 0:KT])
            evac(peT[:, 0], lambda p: p[:, 0:CB])
            evac(peT[:, 1], lambda p: p[:, 0:CB])

            def norm(which, sq_value):
                hn = hn_at[which]
                if which == 1:
                    dve.wait_ge(s.gain_in, 16)
                dve.wait_ge(s.rstd_sq, sq_value)
                link(V.reciprocal(rstd[:], rstd[:]))
                for t in range(3):
                    r = ROWS[t]
                    if which == 0:
                        V.tensor_scalar(hn[t][0:r], xt[0:r, t, :], rstd[0:r, t:t + 1], None, ALU.mult).then_inc(s.normed, 1)
                    else:
                        V.scalar_tensor_tensor(out=hn[t][0:r], in0=xt[0:r, t, :], scalar=rstd[0:r, t:t + 1], in1=g_ffn[0:r],
                                               op0=ALU.mult, op1=ALU.mult).then_inc(s.normed, 1)
                for t in range(3):
                    r = ROWS[t]
                    for k4 in range(4):
                        if tp[0] == 3:
                            dve.wait_ge(s.tp_free, 3)
                        evac(hT[:, 4 * k4:4 * k4 + 4, t * P:t * P + r],
                             lambda p, r=r: p.rearrange("p (k t) -> p k t", k=4)[:, :, 0:r],
                             bcast(gT[:, 4 * k4:4 * k4 + 4].unsqueeze(2), [P, 4, r]) if which == 0 else None)
                    if which == 0 and t:
                        h_rest(t - 1)

            def h_rest(t):
                rows = slice(t * P, t * P + ROWS[t])
                dve.wait_ge(s.x_hi, t + 1)
                V.tensor_tensor(hkv_lo[:, :, rows], hT[:, :, rows], hkv_hi[:, :, rows].bitcast(F32), ALU.subtract).then_inc(s.x_lo, 1)

            def rest_slot(slots, u, count):
                dve.wait_ge(s.w_hi, count)
                for k0, hi in slots[u]:
                    k = slice(k0, k0 + hi.shape[1])
                    ins = V.tensor_tensor(ring_lo[:, u, k], ring[:, u, k], hi[:].bitcast(F32), ALU.subtract)
                ins.then_inc(s.w_lo, 1)

            norm(0, 1)
            h_rest(2)
            for u in range(4):
                rest_slot(ring_hi, u, u + 1)

            def kv_odd(i):
                more = not (isinstance(i, int) and i == KV_IT - 1)
                if more:
                    rest_slot(ring_hi, 0, i * 4 + 5)
                    rest_slot(ring_hi, 1, i * 4 + 6)
                dve.wait_ge(s.w_used, chunk_done(i, 1))
                V.tensor_copy(kv[:, 0:2, ds(i * 512 + 256, 256)], ps[:, 3:5, 0:256])
                V.tensor_copy(kv[0:NS, 2, ds(i * 512 + 256, 256)], ps[0:NS, 5, 0:256]).then_inc(s.kv_ev_dve, 1)
                if more:
                    rest_slot(ring_hi, 2, i * 4 + 7)
                    rest_slot(ring_hi, 3, i * 4 + 8)

            loop(dve, ch, KV_IT, kv_odd, last=True)
            dve.wait_ge(s.kv_ev_act, KV_IT)
            dve.wait_ge(s.kv_ev_dve, KV_IT)
            for t in range(3):
                r = ROWS[t]
                keys = kv[0:r, t].rearrange("p (b x h d) -> p b x h d", b=3, x=2, h=KVH)[:, :, 0]
                x1, x2 = keys[:, :, :, 0:HALF], keys[:, :, :, HALF:RD]
                co = bcast(c_("cos", r)[:, t * HALF:(t + 1) * HALF].unsqueeze(1).unsqueeze(1), [r, 3, KVH, HALF])
                si = bcast(c_("sin", r)[:, t * HALF:(t + 1) * HALF].unsqueeze(1).unsqueeze(1), [r, 3, KVH, HALF])
                tm = [rtmp[0:r, k].rearrange("p (b h d) -> p b h d", b=3, h=KVH) for k in range(4)]
                V.tensor_tensor(tm[0], x1, co, ALU.mult)
                V.tensor_tensor(tm[1], x2, si, ALU.mult)
                V.tensor_tensor(tm[2], x2, co, ALU.mult)
                link(V.tensor_tensor(tm[3], x1, si, ALU.mult))
                V.tensor_tensor(x1, tm[0], tm[1], ALU.subtract)
                ins = V.tensor_tensor(x2, tm[2], tm[3], ALU.add)
                link(ins)
            link(V.memset(stt[:], 0.0))
            dve.sem_inc(s.roped, 1)
            dve.wait_ge(s.br_done, 9)
            link(V.tensor_tensor(gbr[:, :, :, 2], gbr[:, :, :, 2], bcast(c_("anyvalid").unsqueeze(2), [P, 3, NH]), ALU.mult))
            dve.sem_inc(s.gates_done, 1)

            for br in range(2):
                for t in range(3):
                    r = ROWS[t]
                    evac(kT[:, br, :, t * P:t * P + r], lambda p, r=r: p.rearrange("p (k t) -> p k t", k=4)[:, :, 0:r])
            dve.wait_ge(s.tp_free, tp[0])
            dve.sem_inc(s.kT_ready, 1)

            for n in range(2):
                if n == 1:
                    dve.wait_ge(s.cmp_hid_full, 1)
                pe_b = bcast(peT[:, n].unsqueeze(1), [P, 16, CB])

                def pages(i, n=n, pe_b=pe_b):
                    for b in range(4):
                        dve.wait_ge(s.page_T, n * PAGES + (i * 4 + (b + 1)))
                        V.tensor_tensor(rowsT[:, ds(i * 2048 + b * 512, 512)].rearrange("p (a j) -> p a j", j=CB),
                                        ps[:, 6 + b % 2].rearrange("p (a j) -> p a j", j=CB), pe_b, ALU.add).then_inc(s.page_ev, 1)

                loop(dve, ch, PAGES // 4, pages)
                for t in range(2):
                    dve.wait_ge(s.tp_full, tp[0] + 1)
                    V.tensor_tensor(rowsT[:, (16 + t) * 512:(17 + t) * 512].rearrange("p (a j) -> p a j", j=CB),
                                    ps[:, 6 + tp[0] % 2].rearrange("p (a j) -> p a j", j=CB), pe_b, ALU.add).then_inc(s.tp_free, 1)
                    tp[0] += 1
                if n == 0:
                    dve.wait_ge(s.kc_full, 1)
                    V.tensor_copy(kcT[:], ps[:, 2, 0:288]).then_inc(s.kc_ready, 1)
                else:
                    dve.wait_ge(s.vc_full, 1)
                    V.tensor_copy(vc_st, ps[0:NCB, 3]).then_inc(s.vc_ready, 1)

            def x_rest(n, lo, src, hi, half):
                k = slice(HALF_K * half, HALF_K * (half + 1))
                dve.wait_ge(s.x_hi, n)
                V.tensor_tensor(lo[:, k], src[:, k], hi[:, k].bitcast(F32), ALU.subtract).then_inc(s.x_lo, 1)

            for half in range(2):
                x_rest(half + 4, hq_lo, hT, hq_hi, half)
                rest_slot(ring_hi, half, S_Q + half + 1)
            rest_slot(ring_hi, 2, S_Q + 3)
            rest_slot(ring_hi, 3, S_Q + 4)

            def q_odd(i):
                more = not (isinstance(i, int) and i == Q_IT - 1)
                if more:
                    rest_slot(ring_hi, 0, i * 4 + (S_Q + 5))
                    rest_slot(ring_hi, 1, i * 4 + (S_Q + 6))
                dve.wait_ge(s.w_used, chunk_done(i + IT_Q, 1))
                V.tensor_copy(qT[:, ds(i * 4 + 2, 2), :], ps[:, 3:5, 0:TOK]).then_inc(s.q_ev_dve, 1)
                if more:
                    rest_slot(ring_hi, 2, i * 4 + (S_Q + 7))
                    rest_slot(ring_hi, 3, i * 4 + (S_Q + 8))

            loop(dve, ch, Q_IT, q_odd, last=True)
            dve.wait_ge(s.q_ev_act, Q_IT)
            dve.wait_ge(s.q_ev_dve, Q_IT)
            cosb = bcast(c_("cosT", RD).unsqueeze(1), [RD, 4, TOK])
            sinb = bcast(c_("sinT", RD).unsqueeze(1), [RD, 4, TOK])

            def rope_q(i):
                dve.wait_ge(s.rot_full, i + 1)
                q4 = qT[0:RD, ds(i * 4, 4), :]
                part = scr2[0:RD].rearrange("p (h t) -> p h t", h=4)
                V.tensor_tensor(q4, q4, cosb, ALU.mult)
                link(V.tensor_tensor(part, ps[0:RD, 0:4, 0:TOK], sinb, ALU.mult))
                dve.sem_inc(s.rot_done, 1)
                link(V.tensor_tensor(q4, q4, part, ALU.add))

            loop(dve, ch, 4, rope_q)
            dve.sem_inc(s.q_ready, 1)
            dve.wait_ge(s.vc_ready, 1)
            dve.wait_ge(s.kc_ready, 1)

            def maxima(n, b):
                dve.wait_ge(s.s_full, n + 1)
                st = stt[:, b]
                lo, hi = ps[:, 2 * b], ps[:, 2 * b + 1]
                V.tensor_reduce(st[:, 2:4], hi.rearrange("p (w k) -> p w k", w=2), AX_X, ALU.max)
                V.tensor_reduce(st[:, 0:2], lo[:, 0:2 * P].rearrange("p (w k) -> p w k", w=2), AX_X, ALU.max)
                link(V.tensor_reduce(st[:, 4:6], lo[:, 2 * P:2 * P + 2 * NCB].rearrange("p (q k) -> p q k", q=2), AX_X, ALU.max))
                V.tensor_scalar(st[:, 6:12], st[:, 0:6], -SCALE, None, ALU.mult).then_inc(s.sc_ready, 1)

            def weigh(n, b):
                dve.wait_ge(s.p_exp, n + 1)
                st = stt[:, b]
                link(V.reciprocal(st[:, 18:24], st[:, 12:18]))
                gate = gbr[:, 0:2, ds(n, 1), :].rearrange("p q a c -> p q (a c)")
                V.tensor_tensor(st[:, 0:4].rearrange("p (q w) -> p q w", q=2), st[:, 18:22].rearrange("p (q w) -> p q w", q=2), gate[:, :, 0:2], ALU.mult)
                link(V.tensor_tensor(st[:, 4:6].unsqueeze(2), st[:, 22:24].unsqueeze(2), gate[:, :, 2:3], ALU.mult))
                for c, m, k in ((0, 2, P), (2, 2, 2 * P), (4, 2, NCB)):
                    part = pr[:, b, (0, 2 * P, 6 * P)[c // 2]:][:, 0:m * k].rearrange("p (w k) -> p w k", w=m)
                    ins = V.tensor_tensor(part, part, bcast(st[:, c:c + 2].unsqueeze(2), [P, m, k]), ALU.mult)
                ins.then_inc(s.p_ready, 1)

            def leave(n, b):
                apart(dve, s.pv_done, n + 1, s.dve_passed)
                V.tensor_copy(qT[:, ds(n, 1), 0:SEQ].rearrange("p a t -> p (a t)"), ps[:, 6 + b, 0:SEQ]).then_inc(s.o_ev, 1)

            def stage_q(kh):
                V.tensor_copy(q_st, qT[:, ds(kh * GQ, GQ), 0:SEQ]).then_inc(s.q_staged, 1)

            def stage_v(kh):
                V.tensor_copy(vch_st, vc_st[:, ds(kh * HD, HD)])
                for c, br in enumerate((3, 5)):
                    ins = V.tensor_copy(v_st[:, :, c], kv[:, 0:2, ds(kh * HD + br * KVC, HD)])
                ins.then_inc(s.v_staged, 1)

            def heads(kh, last):
                for g in range(GQ):
                    n = kh * GQ + g
                    b = g % 2
                    weigh(n, b)
                    if not (last and g == GQ - 1):
                        maxima(n + 1, 1 - b)
                    if g == GQ - 2 and not last:
                        stage_q(kh + 1)
                    if not (isinstance(n, int) and n == 0):
                        leave(n - 1, 1 - b)
                        if g == 0:
                            stage_v(kh)
                    dve.wait_ge(s.pt_full, n + 1)
                    after(dve, s.pv_done, n)
                    V.tensor_copy(pT[:, 4 * P:6 * P], ps[:, 5, 0:2 * P])
                    V.tensor_copy(pcT, ps[0:NCB, 5, 2 * P:4 * P]).then_inc(s.pt_dve, 1)

            stage_q(0)
            maxima(0, 0)
            stage_v(0)
            kv_heads(dve, ch, heads)
            leave(NH - 1, 1)

            dve.wait_ge(s.o_ev, NH)
            dve.wait_ge(s.gate_in, 16 * NH)
            link(V.memset(qpad, 0.0))
            qpv = qpad.rearrange("p (h r) -> p h r", h=KVH)[:, :, 0:16].rearrange("p h (g t) -> p h g t", g=GQ)

            def stage_sample(n):
                for h in range(KVH):
                    V.tensor_copy(qpv[:, h], qT[:, 4 * h:4 * h + 4, ds(n * DT + SEQ, DT)])
                V.tensor_copy(hidc_st, hidcT[:, 1, ds(n * (KVH * NCB), KVH * NCB)]).then_inc(s.qp_ready, 1)

            def cmp_values_left(n, b):
                dve.wait_ge(s.vcs_full, n + 1)
                V.tensor_copy(vcs_st[:, b], ps[0:NCB, 5]).then_inc(s.vcs_ev, 1)

            def rows_left(n):
                dve.wait_ge(s.tpv_done, n + 1)
                after(dve, s.oT_full, n)
                V.tensor_copy(o_st, ps[0:NH * DT, 4]).then_inc(s.o_rows, 1)

            def out_left(n):
                apart(dve, s.oT_full, n + 1, s.dve_passed)
                own = ps[:, 4, 0:KVH * 80].rearrange("p (h c) -> p h c", h=KVH)[:, :, 0:16].rearrange("p h (g t) -> p h g t", g=GQ)
                V.tensor_copy(qT[:, :, ds(n * DT + SEQ, DT)].rearrange("p (h g) t -> p h g t", h=KVH), own).then_inc(s.to_ev, 1)

            stage_sample(0)
            cmp_values_left(0, 0)

            def sample(i):
                for b in range(2):
                    n = i * 2 + b
                    more = not (isinstance(n, int) and n == DB - 1)
                    st = stt[0:64, 0]
                    dve.wait_ge(s.t_full, n + 1)
                    V.tensor_reduce(st[:, 0:2], ps[0:64, 0:2, 0:288], AX_X, ALU.max)
                    link(V.tensor_reduce(st[:, 2:3], ps[0:64, 0, 288:296], AX_X, ALU.max))
                    V.tensor_scalar(st[:, 3:6], st[:, 0:3], -SCALE, None, ALU.mult).then_inc(s.tsc_ready, 1)
                    if not (isinstance(n, int) and n == 0):
                        rows_left(n - 1)
                    if more:
                        stage_sample(n + 1)
                    dve.wait_ge(s.tp_exp, n + 1)
                    link(V.reciprocal(st[:, 9:12], st[:, 6:9]))
                    link(V.tensor_tensor(st[:, 0:3], st[:, 9:12], gsm[:, ds(n, 1), :].rearrange("p a c -> p (a c)"), ALU.mult))
                    sc = tpr[:, 0:576].rearrange("p (w k) -> p w k", w=2)
                    V.tensor_tensor(sc, sc, bcast(st[:, 0:2].unsqueeze(2), [64, 2, 288]), ALU.mult)
                    V.tensor_scalar(tpr[:, 576:584], tpr[:, 576:584], st[:, 2:3], None, ALU.mult).then_inc(s.tp_ready, 1)
                    dve.wait_ge(s.tpt_full, n + 1)
                    V.tensor_copy(tpcT[0:NS, 0:P], ps[0:NS, 3, 0:P])
                    V.tensor_copy(tpcT[0:NCB, P:P + 64], ps[0:NCB, 3, P:P + 64]).then_inc(s.tpt_dve, 1)
                    if not (isinstance(n, int) and n == 0):
                        out_left(n - 1)
                    if more:
                        cmp_values_left(n + 1, 1 - b)

            loop(dve, ch, DB // 2, sample, last=True)
            rows_left(DB - 1)
            out_left(DB - 1)

            for half in range(2):
                x_rest(half + 6, h_lo, hT, h_hi, half)
                rest_slot(vu_hi, half, S_V + half + 1)

            def v_rest(i):
                for u in range(4):
                    rest_slot(vu_hi, (u + 2) % 4, i * 4 + (S_V + u + 3))

            loop(dve, ch, V_IT, v_rest)
            for half in range(2):
                evac(wsT[:, 4 * half:4 * half + 4, :], lambda p: p.rearrange("p (g i) -> p g i", g=4))
            evac(wssT, lambda p: p[0:NS, 0:256].rearrange("p (g i) -> p g i", g=AG))
            dve.wait_ge(s.v_ev, 2 * V_IT)
            for t in range(3):
                for c in range(4):
                    ins = V.bn_stats(bn[0:ROWS[t], t, c, :], v_tok[0:ROWS[t], t, c * 512:(c + 1) * 512])
            link(ins)
            for t in range(3):
                ins = V.bn_aggr(mv[0:ROWS[t], t, :], bn[0:ROWS[t], t].rearrange("p c s -> p (c s)"))
            link(ins)
            dve.sem_inc(s.rstd_sq, 1)
            dve.wait_ge(s.rstd_sq, 3)
            link(V.reciprocal(rstd[:], rstd[:]))
            dve.wait_ge(s.ln_in, 16 * (4 + DB))
            for i in range(U_IT):
                for b in range(2):
                    if i < U_IT - 1 or b == 0:
                        for r in range(2):
                            rest_slot(vu_hi, (2 * b + 2 + r) % 4, S_U + 4 * i + 2 * b + 2 + r + 1)
                    if i < 3:
                        vt, r = v_tok[0:ROWS[i], i, :], ROWS[i]
                        if b == 0:
                            link(V.tensor_scalar(vt, vt, mv[0:r, i, 0:1], rstd[0:r, i:i + 1], ALU.subtract, ALU.mult))
                        else:
                            link(V.tensor_tensor(vt, vt, ln_g[0:r], ALU.mult))
                            link(V.tensor_tensor(vt, vt, ln_b[0:r], ALU.add))
            dve.sem_inc(s.v_ready, 1)
            dve.wait_ge(s.u_ev, 2 * U_IT)
            for k in range(KT):
                dve.wait_ge(s.sp_full, k + 1)
                t_ = sp_sum[:, (k % 2) * TOK:(k % 2) * TOK + TOK]
                link(V.tensor_tensor(t_, ps[:, k % 2, 0:TOK], sbias[:, k // 2, :], ALU.add))
                V.tensor_tensor(uT[:, k, :], uT[:, k, :], t_, ALU.mult).then_inc(s.sp_done, 1)

            def w_rest(n, u, out_turns=False):
                if isinstance(n, int) and n == N_SPLIT:
                    return
                rest_slot(hi_slots(n, out_turns), u, n * 4 + (S_M + u + 1))

            w_rest(0, 0)
            w_rest(0, 1)
            for half in range(2):
                x_rest(half + 8, u_lo, uT, u_hi, half)
                w_rest(0, 2 + half)

            def merge(first):
                def body(j):
                    for b in range(2):
                        n = j * 2 + (first + b)
                        w_rest(n + 1, 0)
                        w_rest(n + 1, 1)
                        dve.wait_ge(s.w_used, chunk_done(n + IT_M, 1))
                        dve.wait_ge(s.m_ev_act, n + 1)
                        m2 = mT[:, ds(j * 4 + 2 * b, 2), :]
                        if first == 0:
                            link(V.tensor_tensor(m2, ps[:, 3:5, 0:TOK], sig[:, b], ALU.mult))
                        else:
                            link(V.tensor_tensor(sig[:, b], ps[:, 3:5, 0:TOK], sig[:, b], ALU.mult))
                            link(V.tensor_tensor(m2, m2, sig[:, b], ALU.add))
                        dve.sem_inc(s.m_ev_dve, 1)
                        if isinstance(n, int) and n == 2 * M_IT - 1:
                            for half in range(2):
                                x_rest(half + 12, m_lo, mT, m_hi, half)
                        w_rest(n + 1, 2)
                        w_rest(n + 1, 3)
                return body

            loop(dve, ch, M_IT // 2, merge(0))
            for half in range(2):
                x_rest(half + 10, q_lo, qT, q_hi, half)
            loop(dve, ch, M_IT // 2, merge(M_IT), last=True)

            def w_o(i):
                for b in range(2):
                    dve.wait_ge(s.w_used, chunk_done(i + IT_O, b))
                    x2_ = xt[:, 0:2, ds(i * 512 + b * 256, 256)]
                    x1_ = xt[0:NS, 2, ds(i * 512 + b * 256, 256)]
                    V.tensor_tensor(x2_, x2_, ps[:, 3 * b:3 * b + 2, 0:256], ALU.add)
                    V.tensor_tensor(x1_, x1_, ps[0:NS, 3 * b + 2, 0:256], ALU.add).then_inc(s.wo_ev, 1)
                    w_rest(i + 2 * M_IT + 1, 2 * b, True)
                    w_rest(i + 2 * M_IT + 1, 2 * b + 1, True)

            dve.wait_ge(s.x_in, 96)
            loop(dve, ch, O_IT, w_o, last=True)
            norm(1, 4)

            def rest_of_weights(slot, q, hi, n, done):
                dve.wait_ge(hi, n)
                V.tensor_tensor(split[slot][:, 1], staging[q], split[slot][:, 0].bitcast(F32), ALU.subtract).then_inc(done, 1)

            for q in range(2):
                rest_of_weights(q, q, s.hi_done, q + 1, s.lo_done)

            dve.wait_ge(s.lg_full, 3)
            for t in range(3):
                r = ROWS[t]
                ins = V.tensor_tensor(lg[0:r, t, :], ps[0:r, 0, t * 36:(t + 1) * 36], rb[0:r], ALU.add)
            link(ins)
            link(V.tensor_copy(g8[:, :, 0:NG], lg[:, :, 0:NG]))
            for t in range(3):
                ins = V.max(mx8[:, t], g8[:, t])
            link(ins)
            for t in range(3):
                V.max_index(mi8[:, t], mx8[:, t], g8[:, t])
            link(V.tensor_scalar(rs[:, 0], mx8[:, :, 0], -1.0, None, ALU.mult))
            dve.sem_inc(s.zsq, 1)
            link(V.tensor_copy(mif[:], mi8[:]))
            link(V.tensor_copy(rs[:, 4], mif[:, :, 0]))
            link(V.tensor_tensor(goh[:], bcast(c_("iota8").unsqueeze(1), [P, 3, 8]), bcast(rs[:, 4].unsqueeze(2), [P, 3, 8]), ALU.is_equal))
            for t in range(3):
                ins = V.tensor_tensor(le4[:, t], lg[:, t, NG:].rearrange("p (g e) -> p e g", g=NG),
                                      bcast(goh[:, t, 0:NG].unsqueeze(1), [P, EPG, NG]), ALU.mult)
            link(ins)
            link(V.tensor_reduce(le[:], le4[:], AX_X, ALU.add))
            for t in range(3):
                ins = V.max(mx8[:, t], le[:, t])
            link(ins)
            for t in range(3):
                V.max_index(mi8[:, t], mx8[:, t], le[:, t])
            link(V.tensor_tensor(rs[:, 2], mx8[:, :, 1], mx8[:, :, 0], ALU.subtract))
            dve.sem_inc(s.zsq, 1)
            link(V.tensor_copy(mif[:], mi8[:]))
            for k in range(2):
                link(V.scalar_tensor_tensor(out=rs[:, 5 + k], in0=rs[:, 4], scalar=float(EPG), in1=mif[:, :, k], op0=ALU.mult, op1=ALU.add))
                link(V.tensor_tensor(oh[:, :, k], bcast(c_("iota32").unsqueeze(1), [P, 3, NE]), bcast(rs[:, 5 + k].unsqueeze(2), [P, 3, NE]), ALU.is_equal))
            V.tensor_tensor(selm[:], oh[:, :, 0], oh[:, :, 1], ALU.add).then_inc(s.rank_done, 1)
            dve.wait_ge(s.lg_done, 4)
            link(V.tensor_scalar(rs[:, 7], rs[:, 3], 1.0, None, ALU.add))
            link(V.tensor_tensor(rs[:, 7], rs[:, 7], rs[:, 1], ALU.mult))
            link(V.reciprocal(rs[:, 8], rs[:, 7]))
            link(V.tensor_tensor(rs[:, 9], rs[:, 8], rs[:, 3], ALU.mult))
            dve.wait_ge(s.rank_full, 1)
            link(V.tensor_copy(cnt[:], ps[:, 1, 96:128]))
            link(V.tensor_scalar(novf[:, 0], cnt[:], float(CAP), None, ALU.is_gt))
            for m in range(2, MAXCH):
                link(V.scalar_tensor_tensor(out=novf[:, 0], in0=cnt[:], scalar=float(CAP * m), in1=novf[:, 0], op0=ALU.is_gt, op1=ALU.add))
            link(V.tensor_copy(novf[:, 1], novf[:, 0]))
            cur = 1
            for sh in (1, 2, 4, 8, 16):
                nxt = 3 - cur
                V.tensor_copy(novf[:, nxt, 0:sh], novf[:, cur, 0:sh])
                link(V.tensor_tensor(novf[:, nxt, sh:], novf[:, cur, sh:], novf[:, cur, 0:NE - sh], ALU.add))
                cur = nxt
            incl = novf[:, cur]
            excl = novf[:, 3 - cur]
            link(V.tensor_tensor(excl, incl, novf[:, 0], ALU.subtract))
            link(V.tensor_tensor(ovf_cmp, bcast(incl.unsqueeze(1), [P, NOVF, NE]),
                                 c_("ovf_no").rearrange("p (o e) -> p o e", o=NOVF), ALU.is_le))
            link(V.tensor_reduce(ovf_ef[:, 0:NOVF], ovf_cmp, AX_X, ALU.add))
            link(V.tensor_scalar(ovf_ef[:, 0:NOVF], ovf_ef[:, 0:NOVF], float(NE - 1), None, ALU.min))
            link(V.tensor_copy(ovf_ef[:, NOVF:NOVF + 1], incl[:, NE - 1:NE]))
            link(V.tensor_copy(ovf_e[:], ovf_ef[:]))
            for t in range(3):
                ins = V.tensor_copy(posn[0:ROWS[t], t], ps[0:ROWS[t], 1, t * NE:(t + 1) * NE])
            link(ins)
            link(V.scalar_tensor_tensor(out=excl, in0=excl, scalar=float(CAP), in1=c_("base32"), op0=ALU.mult, op1=ALU.subtract))
            link(V.tensor_scalar(excl, excl, float((NE - 1) * CAP), None, ALU.add))
            link(V.tensor_scalar(posn2[:], posn[:], float(CAP), None, ALU.is_ge))
            link(V.tensor_tensor(posn2[:], posn2[:], bcast(excl.unsqueeze(1), [P, 3, NE]), ALU.mult))
            link(V.tensor_tensor(posn[:], posn[:], bcast(c_("base32").unsqueeze(1), [P, 3, NE]), ALU.add))
            link(V.tensor_tensor(posn[:], posn[:], posn2[:], ALU.add))
            for k in range(2):
                link(V.tensor_tensor(posn2[:], posn[:], oh[:, :, k], ALU.mult))
                link(V.tensor_reduce(slotf[:, :, k], posn2[:], AX_X, ALU.add))
            V.tensor_copy(sloti[:], slotf[:])
            V.tensor_copy(ids[:, :, :, 0], bcast(c_("token").unsqueeze(2), [P, 3, 2]))
            link(V.tensor_copy(ids[:, :, :, 1], c_("pair").rearrange("p (t k) -> p t k", t=3)))
            dve.sem_inc(s.slots_rdy, 1)
            dve.sem_inc(s.ids_ready, 1)

            def piece_lo(e, b, q):
                if q > 5:
                    e, b, q = e + 1, 1 - b, q - 6
                if isinstance(e, int) and (e == NE or (e == NE - 1 and q < 4)):
                    return
                rest_of_weights((6 * b + q) % 4, q, s.hi_done, before(e, q) + 1, s.lo_done)

            def rows_lo(b, hi, n, done):
                dve.wait_ge(hi, n)
                V.tensor_tensor(xgT[b][:, 1, 0:KT * CAP].rearrange("p (n c) -> p n c", n=2), ps[:, 0:2, 0:8 * CAP],
                                xgT[b][:, 0, 0:KT * CAP].bitcast(F32).rearrange("p (n c) -> p n c", n=2), ALU.subtract).then_inc(done, 1)

            def hidT_lo(bank, hi, n, done):
                dve.wait_ge(hi, n)
                V.tensor_tensor(hidT[:, 1, 0:2 * CAP], ps[:, bank, 0:2 * CAP], hidT[:, 0, 0:2 * CAP].bitcast(F32), ALU.subtract).then_inc(done, 1)

            def y_right(e):
                dve.wait_ge(s.piece_used, before(e, 5) + 1)
                after(dve, s.y_out, e * 16)
                V.tensor_copy(y_sb[:, 1024:2048].rearrange("p (n c) -> p n c", n=2), ps[0:CAP, 6:8]).then_inc(s.y_dve, 1)

            for b in range(2):
                V.memset(xgT[b][:, :, KT * CAP:].bitcast(F32), 0.0)
            link(V.memset(hidT[:, :, 2 * CAP:].bitcast(F32), 0.0))
            for q in range(2, 4):
                rest_of_weights(q, q, s.hi_done, q + 1, s.lo_done)
            rows_lo(0, s.xgh_done, 1, s.xgT_ready)
            piece_lo(0, 0, 0)
            piece_lo(0, 0, 1)
            rows_lo(1, s.xgh_done, 2, s.xgT_ready)

            def item(j):
                for b in range(2):
                    e = j * 2 + b
                    dve.wait_ge(s.hg_done, e + 1)
                    after(dve, s.ht_done, e)
                    V.tensor_tensor(hid, hgate, ps[0:CAP, 2 + b, ED:2 * ED], ALU.mult).then_inc(s.hid_done, 1)
                    piece_lo(e, b, 2)
                    piece_lo(e, b, 3)
                    if not (isinstance(e, int) and e == 0):
                        y_right(e - 1)
                    piece_lo(e, b, 4)
                    piece_lo(e, b, 5)
                    piece_lo(e, b, 6)
                    hidT_lo(2 + b, s.hidTh_done, e + 1, s.hidT_ready)
                    if not (isinstance(e, int) and e >= NE - 2):
                        rows_lo(b, s.xgh_done, e + 3, s.xgT_ready)
                    piece_lo(e, b, 7)

            loop(dve, ch, NE // 2, item, last=True)
            y_right(NE - 1)
            n_ovf = dve.value_load(ovf_e[0:1, NOVF:NOVF + 1], min_val=0, max_val=NOVF)
            with dve.If(n_ovf > 0):
                with dve.Fori(0, n_ovf) as o:
                    rows_lo(0, s.o_xgh, o + 1, s.o_xgT)
                    for q in range(6):
                        rest_of_weights(q % 4, q, s.o_hi, o * 6 + (q + 1), s.o_lo)
                    dve.wait_ge(s.o_hg, o + 1)
                    V.tensor_tensor(hid, hgate, ps[0:CAP, 2, ED:2 * ED], ALU.mult).then_inc(s.o_hid, 1)
                    hidT_lo(2, s.o_hidTh, o + 1, s.o_hidT)

            yp_sems = [s.yp_in0, s.yp_in1, s.yp_in2]

            def combine(t):
                r = ROWS[t]
                xr = xt[0:r, t, :]
                dve.wait_ge(yp_sems[t], 32)
                for k in range(2):
                    ins = V.scalar_tensor_tensor(out=xr, in0=yp[2 * t + k][0:r], scalar=rs[0:r, 8 + k, t:t + 1], in1=xr, op0=ALU.mult, op1=ALU.add)
                    if k == 0:
                        link(ins)
                ins.then_inc(s.x2_done, 1)

            def finish(t):
                r = ROWS[t]
                dve.wait_ge(s.rstd_sq, 4 + t + 1)
                link(V.reciprocal(rstd[:, t:t + 1], rstd[:, t:t + 1]))
                V.scalar_tensor_tensor(out=fin[t][0:r], in0=xt[0:r, t, :], scalar=rstd[0:r, t:t + 1], in1=gfin[0:r], op0=ALU.mult, op1=ALU.mult).then_inc(s.fin_ready, 1)

            combine(0)
            combine(1)
            dve.wait_ge(s.gain_in, 32)
            finish(0)
            combine(2)
            finish(1)
            finish(2)

        @block.tensor
        def _(pe):
            M = nc.tensor.matmul
            T = nc.tensor.transpose
            tp = [0]

            def group(parts):
                n = tp[0]
                if n >= 2:
                    pe.wait_ge(s.tp_free, n - 1)
                for col, src in parts:
                    rows, cols = src.shape
                    ins = T(ps[0:cols, 6 + n % 2, col:col + rows], src, ident[0:rows, 0:rows])
                ins.then_inc(s.tp_full, 1)
                tp[0] += 1

            pe.wait_ge(s.consts_in, 16)
            pe.wait_ge(s.small_in_in, 48)
            group([(0, small_in[0:KT, 0])])
            group([(0, small_in[:, 1])])
            group([(0, small_in[:, 2])])

            def norm_T(which, then=None):
                hn, base = hn_at[which], 3 * which
                for t in range(3):
                    pe.wait_ge(s.normed, base + t + 1)
                    for k4 in range(4):
                        group([(q * P, hn[t][0:ROWS[t], (4 * k4 + q) * P:(4 * k4 + q + 1) * P]) for q in range(4)])
                    if then and t:
                        then(t - 1)
                pe.wait_ge(s.tp_free, tp[0])
                if then:
                    then(2)

            norm_T(0)

            def used(ins):
                ins.then_inc(s.w_used, 1)

            def split_rows_chunk(b, hi, lo, slots, n, x_split):
                for half in range(2):
                    u = 2 * b + half
                    pe.wait_ge(s.w_lo, n + (u + 1))
                    if x_split:
                        pe.wait_ge(s.x_lo, x_split[half])
                    for k0, w in slots[u]:
                        for k in range(k0, k0 + w.shape[1]):
                            x = HALF_K * half + k
                            for t in range(3):
                                r = ROWS[t]
                                out, rows = ps[0:r, 3 * b + t, 0:256], slice(t * P, t * P + r)
                                M(out, hi[:, x, rows], w[:, k - k0], start=(x == 0), stop=False)
                                M(out, hi[:, x, rows], ring_lo[:, u, k], start=False, stop=False)
                                ins = M(out, lo[:, x, rows], w[:, k - k0], start=False, stop=(x == KT - 1))
                    used(ins)

            def split_cols_chunk(b, hi, lo, slots, n, x_split):
                for half in range(2):
                    u = 2 * b + half
                    pe.wait_ge(s.w_lo, n + (u + 1))
                    if x_split:
                        pe.wait_ge(s.x_lo, x_split + half)
                    for k0, w in slots[u]:
                        for k in range(k0, k0 + w.shape[1]):
                            x = HALF_K * half + k
                            for c in range(2):
                                out, cols = ps[:, 3 * b + c, 0:TOK], slice(c * P, (c + 1) * P)
                                M(out, w[:, k - k0, cols], hi[:, x, :], start=(x == 0), stop=False)
                                M(out, w[:, k - k0, cols], lo[:, x, :], start=False, stop=False)
                                ins = M(out, ring_lo[:, u, k, cols], hi[:, x, :], start=False, stop=(x == KT - 1))
                    used(ins)

            def kv_(i):
                new = isinstance(i, int) and i == 0
                after(pe, s.kv_ev_act, i)
                split_rows_chunk(0, hkv_hi, hkv_lo, ring_hi, i * 4, (3, 3) if new else None)
                after(pe, s.kv_ev_dve, i)
                split_rows_chunk(1, hkv_hi, hkv_lo, ring_hi, i * 4, None)

            loop(pe, None, KV_IT, kv_)
            pe.wait_ge(s.wbr_in, 16)
            for t in range(3):
                for k in range(KT):
                    ins = M(ps[0:ROWS[t], 6, t * 48:(t + 1) * 48], hT[:, k, t * P:t * P + ROWS[t]], wbr[:, k, :],
                            start=(k == 0), stop=(k == KT - 1))
            ins.then_inc(s.br_full, 1)
            pe.wait_ge(s.roped, 1)
            pe.wait_ge(s.br_done, 9)
            for br in range(2):
                for t in range(3):
                    group([(h * P, kv[0:ROWS[t], t, (2 + 2 * br) * KVC + h * HD:(2 + 2 * br) * KVC + (h + 1) * HD]) for h in range(KVH)])

            rv = rowsT.rearrange("p (n j) -> p n j", j=CB)
            for n in range(2):
                def pages(i, n=n):
                    for b in range(4):
                        k = n * PAGES + i * 4 + b
                        pe.wait_ge(page_sems[b], n * (16 * PAGES // 4) + (i * 16 + 16))
                        after(pe, s.page_ev, k - 1)
                        for h in range(KVH):
                            ins = T(ps[:, 6 + b % 2, h * P:(h + 1) * P], page_rows[:, b, h * P:(h + 1) * P], ident)
                        ins.then_inc(s.page_T, 1)

                pe.wait_ge(s.tp_free, tp[0])
                loop(pe, None, PAGES // 4, pages)
                pe.wait_ge(s.page_ev, (n + 1) * PAGES)
                for t in range(2):
                    group([(h * P, kv[:, t, n * KVC + h * HD:n * KVC + (h + 1) * HD]) for h in range(KVH)])
                pe.wait_ge(s.tp_free, tp[0])
                pe.wait_ge(s.w1_in, 16 * (n + 1))
                for j in range(CB):
                    ins = M(ps[:, n, 0:288], w1[:, j, :], rv[:, :, j], start=(j == 0), stop=(j == CB - 1))
                ins.then_inc(s.cmp_hid_full, 1)
                pe.wait_ge(s.cmp_hid, n + 1)
                pe.wait_ge(s.w_aux_in, 96)
                if n == 0:
                    M(ps[:, 2, 0:288], w2[:, 0], hidcT[:, 0], start=True, stop=True).then_inc(s.kc_full, 1)
                else:
                    for h in range(KVH):
                        c = (DB * KVH + h) * NCB
                        ins = M(ps[0:NCB, 3, h * HD:(h + 1) * HD], hidcT[:, 1, c:c + NCB], w2[:, 1], start=True, stop=True)
                    ins.then_inc(s.vc_full, 1)
            pe.wait_ge(s.vc_ready, 1)
            pe.wait_ge(s.kc_ready, 1)

            def q_(i):
                for b in range(2):
                    after(pe, (s.q_ev_act, s.q_ev_dve)[b], i)
                    split_cols_chunk(b, hq_hi, hq_lo, ring_hi, i * 4 + S_Q, 4 if isinstance(i, int) and i == 0 and b == 0 else 0)

            loop(pe, None, Q_IT, q_)
            pe.wait_ge(s.q_ev_act, Q_IT)
            pe.wait_ge(s.q_ev_dve, Q_IT)

            def rot(i):
                after(pe, s.rot_done, i)
                for h in range(4):
                    ins = M(ps[0:RD, h, 0:TOK], c_("swap"), qT[:, ds(i * 4 + h, 1), :].rearrange("p a t -> p (a t)"), start=True, stop=True)
                ins.then_inc(s.rot_full, 1)

            loop(pe, None, 4, rot)
            pe.wait_ge(s.q_ready, 1)

            def scores(n, kh, g):
                b = g % 2
                if g == 0:
                    pe.wait_ge(s.q_staged, kh + 1)
                after(pe, s.p_exp, n - 1)
                for qt, (in_tile, tri) in enumerate(((P, 0), (2 * P, P))):
                    q_ = q_st[:, g, qt * P:(qt + 1) * P]
                    for w in range(2):
                        out = ps[:, 2 * b + qt, w * in_tile:(w + 1) * in_tile]
                        M(out, q_, kT[:, w, ds(kh, 1), 0:in_tile].rearrange("p a t -> p (a t)"), start=True, stop=False)
                        M(out[:, tri:tri + P], ident, c_("pmask")[:, P:2 * P], start=False, stop=True)
                    out = ps[:, 2 * b, 2 * P + qt * NCB:2 * P + (qt + 1) * NCB]
                    M(out, q_, kcT[:, ds(kh * NCB + DB * KVH * NCB, NCB)], start=True, stop=False)
                    ins = M(out, ident, c_("cmask")[:, qt * NCB:(qt + 1) * NCB], start=False, stop=True)
                ins.then_inc(s.s_full, 1)

            def values(n, b):
                pe.wait_ge(s.pt_act, n + 1)
                pe.wait_ge(s.pt_dve, n + 1)
                after(pe, s.o_ev, n - 1)
                out = ps[:, 6 + b, 0:2 * P]
                for w in range(2):
                    M(out, v_st[:, 0, w, :], pT[:, w * 2 * P:(w + 1) * 2 * P], start=(w == 0), stop=False)
                M(out, vch_st, pcT, start=False, stop=False)
                for w in range(2):
                    ins = M(out[:, P:2 * P], v_st[:, 1, w, :], pT[:, (4 + w) * P:(5 + w) * P], start=False, stop=(w == 1))
                ins.then_inc(s.pv_done, 1)

            def transposes(n, b):
                pe.wait_ge(s.p_ready, n + 1)
                after(pe, s.pt_act, n)
                after(pe, s.pt_dve, n)
                for w in range(2):
                    T(ps[:, 4, 2 * w * P:(2 * w + 1) * P], pr[:, b, w * P:(w + 1) * P], ident)
                    for k in range(2):
                        c = (2 + 2 * w + k) * P
                        out = ps[:, 4, (2 * w + 1) * P:(2 * w + 2) * P] if k == 0 else ps[:, 5, w * P:(w + 1) * P]
                        T(out, pr[:, b, c:c + P], ident)
                for qt in range(2):
                    ins = T(ps[0:NCB, 5, (2 + qt) * P:(3 + qt) * P], pr[:, b, 6 * P + qt * NCB:6 * P + (qt + 1) * NCB], ident)
                ins.then_inc(s.pt_full, 1)

            def heads(kh, last):
                for g in range(GQ):
                    n = kh * GQ + g
                    b = g % 2
                    if g < GQ - 1:
                        scores(n + 1, kh, g + 1)
                    elif not last:
                        scores(n + 1, kh + 1, 0)
                    if not (isinstance(n, int) and n == 0):
                        if g == 1:
                            pe.wait_ge(s.v_staged, kh + 1)
                        values(n - 1, 1 - b)
                    transposes(n, b)

            scores(0, 0, 0)
            kv_heads(pe, None, heads)
            values(NH - 1, 1)
            pe.wait_ge(s.o_ev, NH)

            def keys_T(n, b, loads):
                pe.wait_ge(kx_sems[b], loads)
                for h in range(KVH):
                    after(pe, s.kx_ev, n * 4 + (h - 1))
                    for t in range(4):
                        ins = T(ps[:, 6 + h % 2, t * P:(t + 1) * P], kx[:, b, t, h * HD:(h + 1) * HD], ident)
                    ins.then_inc(s.kxT_full, 1)

            def cmp_values(n):
                pe.wait_ge(s.qp_ready, n + 1)
                after(pe, s.vcs_ev, n)
                for h in range(KVH):
                    ins = M(ps[0:NCB, 5, h * HD:(h + 1) * HD], hidc_st[:, h * NCB:(h + 1) * NCB], w2[:, 1], start=True, stop=True)
                ins.then_inc(s.vcs_full, 1)

            def out_T(n):
                apart(pe, s.o_rows, n + 1, s.pe_passed)
                for h in range(KVH):
                    ins = T(ps[:, 4, h * 64:(h + 1) * 64], o_st[:, h * HD:(h + 1) * HD], ident[0:64, 0:64])
                ins.then_inc(s.oT_full, 1)

            keys_T(0, 0, 48)
            cmp_values(0)

            def sample(i):
                for b in range(2):
                    n = i * 2 + b
                    more = not (isinstance(n, int) and n == DB - 1)
                    pe.wait_ge(s.qp_ready, n + 1)
                    pe.wait_ge(s.kx_ev, n * 4 + 4)
                    after(pe, s.tp_exp, n)
                    for w in range(2):
                        for h in range(KVH):
                            M(ps[0:64, w, 0:256], qpad[:, h * 64:(h + 1) * 64], kxT[:, h, w * 256:(w + 1) * 256], start=(h == 0), stop=(h == KVH - 1))
                        for h in range(KVH):
                            M(ps[0:64, w, 256:288], qpad[:, h * 64:(h + 1) * 64], kT[:, w, h, SEQ:TOK], start=(h == 0), stop=False)
                        M(ps[0:64, w, 256:288], ident[:, 0:64], c_("smask")[:, ds(n * NS, NS)], start=False, stop=True)
                    for h in range(KVH):
                        ins = M(ps[0:64, 0, 288:296], qpad[:, h * 64:(h + 1) * 64], kcT[:, ds(n * (KVH * NCB) + h * NCB, NCB)], start=(h == 0), stop=(h == KVH - 1))
                    ins.then_inc(s.t_full, 1)
                    if more:
                        keys_T(n + 1, 1 - b, (i + b) * 48 + 48)
                    if not (isinstance(n, int) and n == 0):
                        out_T(n - 1)
                    apart(pe, s.tp_ready, n + 1, s.pe_passed)
                    for w in range(2):
                        for k in range(2):
                            T(ps[:, 2, (2 * w + k) * 64:(2 * w + k + 1) * 64], tpr[:, w * 288 + k * P:w * 288 + (k + 1) * P], ident[0:64, 0:64])
                        T(ps[0:NS, 3, w * 64:(w + 1) * 64], tpr[:, w * 288 + 256:w * 288 + 288], ident[0:64, 0:64])
                    T(ps[0:NCB, 3, 128:192], tpr[:, 576:584], ident[0:64, 0:64]).then_inc(s.tpt_full, 1)
                    if more:
                        cmp_values(n + 1)
                    pe.wait_ge(vx_sems[b], i * 48 + 48)
                    pe.wait_ge(s.tpt_act, n + 1)
                    pe.wait_ge(s.tpt_dve, n + 1)
                    pe.wait_ge(s.vcs_ev, n + 1)
                    after(pe, s.to_ev, n)
                    out = ps[0:NH * DT, 4]
                    for w in range(2):
                        for k in range(2):
                            c = (2 * w + k) * 64
                            M(out, tpT[:, c:c + 64], vx[:, b, 2 * w + k, :], start=(w == 0 and k == 0), stop=False)
                        M(out, tpcT[0:NS, w * 64:(w + 1) * 64], kv[0:NS, 2, (3 + 2 * w) * KVC:(4 + 2 * w) * KVC], start=False, stop=False)
                    ins = M(out, tpcT[0:NCB, 128:192], vcs_st[:, b], start=False, stop=True)
                    ins.then_inc(s.tpv_done, 1)

            loop(pe, None, DB // 2, sample, last=True)
            out_T(DB - 1)
            pe.wait_ge(s.to_ev, DB)

            def v_(i):
                for b in range(2):
                    if not (isinstance(i, int)):
                        pe.wait_ge(s.v_ev, i * 2 + (b - 1))
                    split_rows_chunk(b, h_hi, h_lo, vu_hi, i * 4 + S_V, (6, 7) if isinstance(i, int) and b == 0 else None)

            loop(pe, None, V_IT, v_)
            pe.wait_ge(s.ws_masked, 2)
            for half in range(2):
                group([(q * P, ws_raw[:, 4 * half + q, :]) for q in range(4)])
            group([(g * NS, wss_raw[:, g, :]) for g in range(AG)])
            pe.wait_ge(s.v_ev, 2 * V_IT)

            def u_(i):
                for b in range(2):
                    if not (isinstance(i, int)):
                        pe.wait_ge(s.u_ev, i * 2 + (b - 1))
                    split_cols_chunk(b, h_hi, h_lo, vu_hi, i * 4 + S_U, 0)

            loop(pe, None, U_IT, u_)
            pe.wait_ge(s.u_ev, 2 * U_IT)
            pe.wait_ge(s.v_ready, 1)
            pe.wait_ge(s.tp_free, tp[0])
            for k in range(KT):
                after(pe, s.sp_done, k - 1)
                g = k // 2
                for t in range(2):
                    M(ps[:, k % 2, t * P:(t + 1) * P], v_tok[:, t, k * P:(k + 1) * P], wsT[:, g, :], start=True, stop=True)
                M(ps[:, k % 2, SEQ:TOK], v_tok[0:NS, 2, k * P:(k + 1) * P], wssT[:, g, :], start=True, stop=True).then_inc(s.sp_full, 1)
            pe.wait_ge(s.sp_done, KT)

            def merge(first, hi, lo):
                def body(j):
                    for b in range(2):
                        n = j * 2 + (first + b)
                        new = isinstance(j, int) and j == 0 and b == 0
                        after(pe, s.m_ev_act, n)
                        split_cols_chunk(0, h_hi, h_lo, ring_hi, n * 4 + S_M, 0)
                        after(pe, s.m_ev_dve, n)
                        split_cols_chunk(1, hi, lo, ring_hi, n * 4 + S_M, (8 if first == 0 else 10) if new else 0)
                return body

            loop(pe, None, M_IT // 2, merge(0, u_hi, u_lo))
            loop(pe, None, M_IT // 2, merge(M_IT, q_hi, q_lo), last=True)
            pe.wait_ge(s.m_ev_act, 2 * M_IT)
            pe.wait_ge(s.m_ev_dve, 2 * M_IT)

            def w_o(i):
                for b in range(2):
                    if not isinstance(i, int):
                        pe.wait_ge(s.wo_ev, i * 2 + (b - 1))
                    new = isinstance(i, int) and i == 0 and b == 0
                    split_rows_chunk(b, m_hi, m_lo, out_hi, i * 4 + (S_M + 8 * M_IT), (12, 13) if new else None)

            loop(pe, None, O_IT, w_o)
            pe.wait_ge(s.wo_ev, 2 * O_IT)

            def router(t):
                pe.wait_ge(s.tp_free, tp[0] - (4 if t < 2 else 0))
                for k in range(KT):
                    ins = M(ps[0:ROWS[t], 0, t * 36:(t + 1) * 36], hT[:, k, t * P:t * P + ROWS[t]], wr[:, k, :],
                            start=(k == 0), stop=(k == KT - 1))
                ins.then_inc(s.lg_full, 1)

            norm_T(1, router)
            pe.wait_ge(s.rank_done, 1)
            for t in range(3):
                r = ROWS[t]
                for j in range(t):
                    M(ps[0:r, 1, t * NE:(t + 1) * NE], c_("ones")[:, 0:r], selm[:, j], start=(j == 0), stop=False)
                M(ps[0:r, 1, t * NE:(t + 1) * NE], c_("before", r)[:, 0:r], selm[0:r, t], start=(t == 0), stop=True)
            for t in range(3):
                r = ROWS[t]
                ins = M(ps[:, 1, 96:128], c_("ones", r), selm[0:r, t], start=(t == 0), stop=(t == 2))
            ins.then_inc(s.rank_full, 1)
            pe.wait_ge(s.ids_ready, 1)

            def rows_T(done):
                for k in range(KT):
                    ins = T(ps[:, k // 8, (k % 8) * CAP:(k % 8 + 1) * CAP], xg[:, k * P:(k + 1) * P], ident[0:CAP, 0:CAP])
                ins.then_inc(done, 1)

            def three(out, x, col, w, start, stop):
                M(out, x[:, 0, col:col + P], w[0], start=start, stop=False)
                M(out, x[:, 0, col:col + P], w[1], start=False, stop=False)
                return M(out, x[:, 1, col:col + P], w[0], start=False, stop=stop)

            def gate_up(x, bank, slot0, lo, n, done):
                for q in range(4):
                    pe.wait_ge(lo, n + (q + 1))
                    sl = split[(slot0 + q) % 4]
                    for k in range(4):
                        c = slice(2 * ED * k, 2 * ED * (k + 1))
                        ins = three(ps[:, bank], x, (4 * q + k) * CAP, (sl[:, 0, c], sl[:, 1, c]),
                                    start=(q == 0 and k == 0), stop=(q == 3 and k == 3))
                    ins.then_inc(done, 1)

            def hid_T(bank, done):
                for f in range(2):
                    ins = T(ps[:, bank, f * CAP:(f + 1) * CAP], hid[:, f * P:(f + 1) * P], ident[0:CAP, 0:CAP])
                ins.then_inc(done, 1)

            def down(slot0, lo, n, done):
                for f in range(2):
                    pe.wait_ge(lo, n + (f + 1))
                    sl = split[(slot0 + f) % 4]
                    for c4 in range(4):
                        c = slice(512 * c4, 512 * (c4 + 1))
                        ins = three(ps[:, 4 + c4], hidT, f * CAP, (sl[:, 0, c], sl[:, 1, c]), start=(f == 0), stop=(f == 1))
                    ins.then_inc(done, 1)

            pe.wait_ge(s.xg_in, 16)
            rows_T(s.xt_done)
            pe.wait_ge(s.xgT_ready, 1)
            gate_up(xgT[0], 2, 0, s.lo_done, 0, s.piece_used)
            pe.wait_ge(s.xg_in, 32)
            rows_T(s.xt_done)

            def item(j):
                for b in range(2):
                    e = j * 2 + b
                    last = isinstance(e, int) and e == NE - 1
                    after(pe, s.hidT_ready, e)
                    if not last:
                        pe.wait_ge(s.xgT_ready, e + 2)
                        gate_up(xgT[1 - b], 3 - b, 6 * b, s.lo_done, before(e, 0), s.piece_used)
                    apart(pe, s.hid_done, e + 1, s.pe_passed)
                    hid_T(2 + b, s.ht_done)
                    if not (isinstance(e, int) and e >= NE - 2):
                        apart(pe, s.xg_in, (e + 3) * 16, s.pe_passed)
                        rows_T(s.xt_done)
                    pe.wait_ge(s.hidT_ready, e + 1)
                    after(pe, s.y_act, e)
                    after(pe, s.y_dve, e)
                    down(6 * b + 4, s.lo_done, before(e, 4), s.piece_used)

            loop(pe, None, NE // 2, item, last=True)
            n_ovf = pe.value_load(ovf_e[0:1, NOVF:NOVF + 1], min_val=0, max_val=NOVF)
            with pe.If(n_ovf > 0):
                pe.wait_ge(s.y_act, NE)
                pe.wait_ge(s.y_dve, NE)
                pe.wait_ge(s.lo_done, 6 * NE)
                pe.sem_inc(s.o_free, 1)
                with pe.Fori(0, n_ovf) as o:
                    apart(pe, s.o_xg, o * 16 + 16, s.pe_passed)
                    rows_T(s.o_xt)
                    pe.wait_ge(s.o_xgT, o + 1)
                    gate_up(xgT[0], 2, 0, s.o_lo, o * 6, s.o_used)
                    apart(pe, s.o_hid, o + 1, s.pe_passed)
                    hid_T(2, s.o_ht)
                    pe.wait_ge(s.o_hidT, o + 1)
                    down(4, s.o_lo, o * 6 + 4, s.o_used)
                    pe.wait_ge(s.o_ya, o + 1)
                    pe.sem_inc(s.o_free, 1)


_INS = ['x_prompt', 'x_sample', 'cache_k_cmp', 'cache_v_cmp', 'cache_k_slc', 'cache_v_slc', 'state_k_win', 'state_v_win',
        'page_table', 'g_mix', 'w_in', 'a_ln_g', 'a_ln_b', 'a_w_s', 'a_b_s', 'cmp_pe_k', 'cmp_w1_k', 'cmp_w2_k',
        'cmp_pe_v', 'cmp_w1_v', 'cmp_w2_v', 'w_pa', 'w_pb', 'w_o', 'g_ffn', 'w_rg', 'b_rg', 'w_re', 'b_re',
        'w_gate', 'w_up', 'w_down', 'g_final']
_ROW = (KVH, HD)
_OUTS = ([(1, SEQ, D), (DB, DT, D)] + [(1, 1, SEQ) + _ROW] * 6 + [(1, DB, DT) + _ROW] * 4
         + [(1, DB, PAST) + _ROW] * 2 + [(1, DB, DT, D)])


def kernel(**inputs):
    import concourse.bacc as _bacc
    from concourse.bass_utils import run_bass_kernel_spmd as _run

    nc = _bacc.Bacc("TRN2", target_bir_lowering=False, num_devices=1)
    arrays, aps = {}, {}
    named = [(n, np.ascontiguousarray(inputs[n])) for n in _INS] + [("consts", constants())]
    for name, x in named:
        arrays[f"in_{name}"] = x
        aps[name] = nc.dram_tensor(f"in_{name}", x.shape, mybir.dt.from_np(x.dtype), kind="ExternalInput").ap()
    outs = [nc.dram_tensor(f"out_{i}", shape, F32, kind="ExternalOutput").ap() for i, shape in enumerate(_OUTS)]
    build(nc, aps, outs)
    r = _run(nc, [arrays], core_ids=[0])
    return tuple(r.results[0][f"out_{i}"] for i in range(len(_OUTS)))
```
